# Optimizing a Trainium2 kernel written in Bass

```python
import jax, jax.numpy as jnp
from jax import lax
import numpy as np
import math

D_MODEL = 1024
BATCH = 1
SEQ = 512
DEPTH = 1

N_META = 16
D_MIX = D_MODEL
GLA_HEADS = 4
GLA_DK = D_MIX // 4 // GLA_HEADS
GLA_DV = D_MIX // 2 // GLA_HEADS
GLA_RANK = 16
GLA_TAU = 16.0
GLA_CHUNK = 64
GLA_PAD = GLA_CHUNK - N_META
SWA_HEADS = 8
SWA_KV_HEADS = 2
SWA_GROUP = SWA_HEADS // SWA_KV_HEADS
SWA_HD = D_MIX // 2 // SWA_HEADS
SWA_WINDOW = 128
SWA_BLOCK = 128
ROPE_DIM = SWA_HD // 4
ROPE_THETA = 500000.0
D_FF = 4 * D_MODEL
EPS = 1e-5

IN_SIZES = (GLA_HEADS * GLA_DK,
            GLA_HEADS * GLA_DK,
            GLA_HEADS * GLA_DV,
            GLA_HEADS * GLA_DV,
            GLA_RANK,
            SWA_HEADS * SWA_HD,
            SWA_KV_HEADS * SWA_HD,
            SWA_KV_HEADS * SWA_HD)
D_IN = sum(IN_SIZES)


def rmsnorm(x, w):
    xf = x.astype(jnp.float32)
    y = xf * lax.rsqrt(jnp.mean(jnp.square(xf), axis=-1, keepdims=True) + EPS)
    return (y * w.astype(jnp.float32)).astype(x.dtype)

def partial_rope(x, pos):
    inv_freq = 1.0 / (ROPE_THETA ** (jnp.arange(0, ROPE_DIM, 2, dtype=jnp.float32) / ROPE_DIM))
    ang = pos.astype(jnp.float32)[:, None] * inv_freq[None, :]
    ang = jnp.concatenate([ang, ang], axis=-1)[:, None, :]
    cos, sin = jnp.cos(ang), jnp.sin(ang)
    xr = x[..., :ROPE_DIM].astype(jnp.float32)
    half = ROPE_DIM // 2
    rot = jnp.concatenate([-xr[..., half:], xr[..., :half]], axis=-1)
    xr = (xr * cos + rot * sin).astype(x.dtype)
    return jnp.concatenate([xr, x[..., ROPE_DIM:]], axis=-1)

def gla_chunk_step(S, inp):
    q, k, v, g = inp
    b = jnp.cumsum(g, axis=2)
    causal = jnp.tril(jnp.ones((GLA_CHUNK, GLA_CHUNK), dtype=bool))
    diff = b[:, :, :, None, :] - b[:, :, None, :, :]
    decay = jnp.exp(jnp.where(causal[None, None, :, :, None], diff, -jnp.inf))
    A = jnp.einsum('bhid,bhjd,bhijd->bhij', q, k, decay)
    o = (jnp.einsum('bhij,bhjv->bhiv', A, v)
         + jnp.einsum('bhid,bhdv->bhiv', q * jnp.exp(b), S))
    b_last = b[:, :, -1:, :]
    S = (jnp.exp(b_last[:, :, 0, :])[..., None] * S
         + jnp.einsum('bhjd,bhjv->bhdv', k * jnp.exp(b_last - b), v))
    return S, o

def gla_mixer(q, k, v, r, lr, w_gate_up, b_gate, gla_norm_w):
    B, L, _ = q.shape
    dtype = q.dtype
    g = jax.nn.log_sigmoid((lr @ w_gate_up + b_gate).astype(jnp.float32)) / GLA_TAU
    q = q.astype(jnp.float32).reshape(B, L, GLA_HEADS, GLA_DK) * (GLA_DK ** -0.5)
    k = k.astype(jnp.float32).reshape(B, L, GLA_HEADS, GLA_DK)
    v = v.astype(jnp.float32).reshape(B, L, GLA_HEADS, GLA_DV)
    g = g.reshape(B, L, GLA_HEADS, GLA_DK)
    pad = ((0, 0), (GLA_PAD, 0), (0, 0), (0, 0))
    Lp = L + GLA_PAD
    n_chunks = Lp // GLA_CHUNK

    def to_chunks(t):
        t = jnp.pad(t, pad).reshape(B, n_chunks, GLA_CHUNK, GLA_HEADS, t.shape[-1])
        return t.transpose(1, 0, 3, 2, 4)

    S0 = jnp.zeros((B, GLA_HEADS, GLA_DK, GLA_DV), jnp.float32)
    _, o = lax.scan(gla_chunk_step, S0, (to_chunks(q), to_chunks(k), to_chunks(v), to_chunks(g)))
    o = o.transpose(1, 0, 3, 2, 4).reshape(B, Lp, GLA_HEADS, GLA_DV)[:, GLA_PAD:]
    o = rmsnorm(o.astype(dtype), gla_norm_w)
    o = o * jax.nn.silu(r.reshape(B, L, GLA_HEADS, GLA_DV))
    return o.reshape(B, L, GLA_HEADS * GLA_DV)

def sink_softmax(scores, sink):
    sink_b = jnp.broadcast_to(sink, scores.shape[:-1] + (1,))
    p = jax.nn.softmax(jnp.concatenate([scores, sink_b], axis=-1), axis=-1)
    return p[..., :-1]

def swa_mixer(q, k, v, sinks, pos):
    B, L, _ = q.shape
    dtype = q.dtype
    q = partial_rope(q.reshape(B, L, SWA_HEADS, SWA_HD), pos) * (SWA_HD ** -0.5)
    k = partial_rope(k.reshape(B, L, SWA_KV_HEADS, SWA_HD), pos)
    v = v.reshape(B, L, SWA_KV_HEADS, SWA_HD)
    q = q.reshape(B, L, SWA_KV_HEADS, SWA_GROUP, SWA_HD)
    qm, qr = q[:, :N_META], q[:, N_META:]
    km, kr = k[:, :N_META], k[:, N_META:]
    vm, vr = v[:, :N_META], v[:, N_META:]
    sink = sinks.astype(jnp.float32).reshape(SWA_KV_HEADS, SWA_GROUP)

    sm = jnp.einsum('bqkgd,bjkd->bkgqj', qm, km).astype(jnp.float32)
    mmask = jnp.tril(jnp.ones((N_META, N_META), dtype=bool))
    pm = sink_softmax(jnp.where(mmask, sm, -jnp.inf), sink[None, :, :, None, None])
    om = jnp.einsum('bkgqj,bjkd->bqkgd', pm.astype(dtype), vm).reshape(B, N_META, SWA_HEADS * SWA_HD)

    S = L - N_META
    nb = S // SWA_BLOCK
    qb = qr.reshape(B, nb, SWA_BLOCK, SWA_KV_HEADS, SWA_GROUP, SWA_HD)

    def band(t):
        cur = t.reshape(B, nb, SWA_BLOCK, SWA_KV_HEADS, SWA_HD)
        prev = jnp.pad(t, ((0, 0), (SWA_BLOCK, 0), (0, 0), (0, 0)))[:, :S]
        prev = prev.reshape(B, nb, SWA_BLOCK, SWA_KV_HEADS, SWA_HD)
        return jnp.concatenate([prev, cur], axis=2)

    kw, vw = band(kr), band(vr)
    s_meta = jnp.einsum('bnqkgd,bjkd->bnkgqj', qb, km).astype(jnp.float32)
    s_win = jnp.einsum('bnqkgd,bnjkd->bnkgqj', qb, kw).astype(jnp.float32)
    rr = jnp.arange(SWA_BLOCK)[:, None]
    jj = jnp.arange(2 * SWA_BLOCK)[None, :]
    dist = SWA_BLOCK + rr - jj
    in_band = (dist >= 0) & (dist < SWA_WINDOW)
    blk = jnp.arange(nb)[:, None, None]
    wmask = in_band[None] & ((blk > 0) | (jj[None] >= SWA_BLOCK))
    s_win = jnp.where(wmask[None, :, None, None], s_win, -jnp.inf)
    p = sink_softmax(jnp.concatenate([s_meta, s_win], axis=-1),
                     sink[None, None, :, :, None, None]).astype(dtype)
    orr = (jnp.einsum('bnkgqj,bjkd->bnqkgd', p[..., :N_META], vm)
           + jnp.einsum('bnkgqj,bnjkd->bnqkgd', p[..., N_META:], vw))
    orr = orr.reshape(B, S, SWA_HEADS * SWA_HD)
    return jnp.concatenate([om, orr], axis=1)

def hybrid_layer(h, pos, norm_mix_w, w_in, w_gate_up, b_gate, gla_norm_w, sinks,
                 w_out, norm_ff_w, w_ff1, w_ff2):
    u = rmsnorm(h, norm_mix_w)
    proj = u @ w_in
    split_points = np.cumsum(IN_SIZES)[:-1].tolist()
    gq, gk, gv, gr, glr, sq, sk, sv = jnp.split(proj, split_points, axis=-1)
    o_gla = gla_mixer(gq, gk, gv, gr, glr, w_gate_up, b_gate, gla_norm_w)
    o_swa = swa_mixer(sq, sk, sv, sinks, pos)
    h = h + jnp.concatenate([o_gla, o_swa], axis=-1) @ w_out
    f = rmsnorm(h, norm_ff_w)
    return h + jnp.square(jax.nn.relu(f @ w_ff1)) @ w_ff2

def first_inputs(seed: int = 0) -> dict:
    key = jax.random.key(seed)
    ks = jax.random.split(key, 14)
    f32 = jnp.float32
    nrm = lambda k, shape, s: jax.random.normal(k, shape, f32) * s
    return {
        "x": nrm(ks[0], (BATCH, SEQ, D_MODEL), 1.0),
        "meta_tokens": nrm(ks[1], (N_META, D_MODEL), 1.0),
        "norm_mix_w": 1.0 + nrm(ks[2], (DEPTH, D_MODEL), 0.02),
        "w_in": nrm(ks[3], (DEPTH, D_MODEL, D_IN), D_MODEL ** -0.5),
        "w_gate_up": nrm(ks[4], (DEPTH, GLA_RANK, GLA_HEADS * GLA_DK), GLA_RANK ** -0.5),
        "b_gate": nrm(ks[5], (DEPTH, GLA_HEADS * GLA_DK), 0.1),
        "gla_norm_w": 1.0 + nrm(ks[6], (DEPTH, GLA_DV), 0.02),
        "sinks": nrm(ks[7], (DEPTH, SWA_HEADS), 1.0),
        "w_out": nrm(ks[8], (DEPTH, D_MIX, D_MODEL), D_MIX ** -0.5),
        "norm_ff_w": 1.0 + nrm(ks[9], (DEPTH, D_MODEL), 0.02),
        "w_ff1": nrm(ks[10], (DEPTH, D_MODEL, D_FF), D_MODEL ** -0.5),
        "w_ff2": nrm(ks[11], (DEPTH, D_FF, D_MODEL), D_FF ** -0.5),
        "final_norm_w": 1.0 + nrm(ks[12], (D_MODEL,), 0.02),
    }

def first_block(x, meta_tokens, norm_mix_w, w_in, w_gate_up, b_gate, gla_norm_w, sinks,
              w_out, norm_ff_w, w_ff1, w_ff2, final_norm_w):
    B = x.shape[0]
    meta = jnp.broadcast_to(meta_tokens[None].astype(x.dtype), (B, N_META, D_MODEL))
    h = jnp.concatenate([meta, x], axis=1)
    pos = jnp.arange(h.shape[1], dtype=jnp.int32)
    for layer in range(DEPTH):
        h = hybrid_layer(h, pos, norm_mix_w[layer], w_in[layer], w_gate_up[layer], b_gate[layer],
                         gla_norm_w[layer], sinks[layer], w_out[layer], norm_ff_w[layer],
                         w_ff1[layer], w_ff2[layer])
    return rmsnorm(h, final_norm_w)[:, N_META:]


MIX_WIDTH = D_MODEL
M_HEADS = 4
M_HEAD_DIM = (MIX_WIDTH // 2) // M_HEADS
M_WIDTH = M_HEADS * M_HEAD_DIM
CONV_WIDTH = 4
CHUNK = 64
D_HEADS = 4
D_HEAD_DIM = (MIX_WIDTH // 2) // (2 * D_HEADS)
D_WIDTH = D_HEADS * 2 * D_HEAD_DIM
Q_BLOCK = 128
P_HEADS = 8
N_KEYS = 128
N_EXPERTS = N_KEYS * N_KEYS
P_TOPK = 16
P_QUERY_DIM = 256
P_HALF = P_QUERY_DIM // 2
TOKEN_BLOCK = 128

EPS_2 = 1e-6
NEG = -1e30


def rmsnorm_2(x, g):
    xf = x.astype(jnp.float32)
    y = xf * lax.rsqrt(jnp.mean(xf * xf, axis=-1, keepdims=True) + EPS_2)
    return (y * g.astype(jnp.float32)).astype(x.dtype)

def causal_dwconv(u, w, b):
    C = u.shape[-1]
    y = lax.conv_general_dilated(
        u, w[:, None, :].astype(u.dtype), window_strides=(1,),
        padding=[(CONV_WIDTH - 1, 0)],
        dimension_numbers=("NWC", "WIO", "NWC"),
        feature_group_count=C)
    return y + b.astype(u.dtype)

def mlstm_chunkwise(q, k, v, ig, lf):
    Bb, H, S, d = q.shape
    nc = S // CHUNK

    def to_chunks(a):
        a = a.reshape(a.shape[:2] + (nc, CHUNK) + a.shape[3:])
        return jnp.moveaxis(a, 2, 0)

    qc, kc, vc, ic, fc = (to_chunks(a) for a in (q, k, v, ig, lf))
    causal = jnp.tril(jnp.ones((CHUNK, CHUNK), dtype=bool))

    def step(carry, inp):
        C, n, m = carry
        qb, kb, vb, ib, fb = inp
        b = jnp.cumsum(fb, axis=-1)
        logD = jnp.where(causal, b[..., :, None] - b[..., None, :] + ib[..., None, :], -jnp.inf)
        m_t = jnp.maximum(b + m[..., None], jnp.max(logD, axis=-1))
        Dw = jnp.exp(logD - m_t[..., None])
        inter = jnp.exp(b + m[..., None] - m_t)
        sqk = jnp.einsum('bhtd,bhsd->bhts', qb, kb) * Dw
        num = (jnp.einsum('bhts,bhsv->bhtv', sqk, vb)
               + inter[..., None] * jnp.einsum('bhtd,bhdv->bhtv', qb, C))
        den = jnp.sum(sqk, axis=-1) + inter * jnp.einsum('bhtd,bhd->bht', qb, n)
        h = num / jnp.maximum(jnp.abs(den), jnp.exp(-m_t))[..., None]
        bL = b[..., -1]
        logw = bL[..., None] - b + ib
        m_new = jnp.maximum(bL + m, jnp.max(logw, axis=-1))
        w = jnp.exp(logw - m_new[..., None])
        decay = jnp.exp(bL + m - m_new)
        C_new = decay[..., None, None] * C + jnp.einsum('bhs,bhsd,bhsv->bhdv', w, kb, vb)
        n_new = decay[..., None] * n + jnp.einsum('bhs,bhsd->bhd', w, kb)
        return (C_new, n_new, m_new), h

    init = (jnp.zeros((Bb, H, d, d), jnp.float32),
            jnp.zeros((Bb, H, d), jnp.float32),
            jnp.zeros((Bb, H), jnp.float32))
    _, hs = lax.scan(step, init, (qc, kc, vc, ic, fc))
    return jnp.moveaxis(hs, 0, 2).reshape(Bb, H, S, d)

def diff_attention(q, k, v, lam):
    Bb, H, _, S, dh = q.shape
    nb = S // Q_BLOCK
    kpos = jnp.arange(S)
    scale = D_HEAD_DIM ** -0.5

    def block(i):
        qb = lax.dynamic_slice_in_dim(q, i * Q_BLOCK, Q_BLOCK, axis=3)
        s = jnp.einsum('bhptd,bhpsd->bhpts', qb, k) * scale
        qpos = i * Q_BLOCK + jnp.arange(Q_BLOCK)
        mask = kpos[None, :] <= qpos[:, None]
        a = jax.nn.softmax(jnp.where(mask, s, NEG), axis=-1)
        att = a[:, :, 0] - lam * a[:, :, 1]
        return jnp.einsum('bhts,bhsv->bhtv', att, v)

    o = lax.map(block, jnp.arange(nb))
    return jnp.moveaxis(o, 0, 2).reshape(Bb, H, S, v.shape[-1])

def peer(h, w_query, sub_keys, u_tab, v_tab):
    Bb, S, D = h.shape
    xt = h.reshape(-1, TOKEN_BLOCK, D)

    def block(xb):
        q = (xb @ w_query).reshape(TOKEN_BLOCK, P_HEADS, 2, P_HALF)
        s = jnp.einsum('thpk,hpnk->thpn', q, sub_keys).astype(jnp.float32)
        sv, si = lax.top_k(s, P_TOPK)
        cand = (sv[:, :, 0, :, None] + sv[:, :, 1, None, :]).reshape(TOKEN_BLOCK, P_HEADS, P_TOPK * P_TOPK)
        cidx = (si[:, :, 0, :, None] * N_KEYS + si[:, :, 1, None, :]).reshape(TOKEN_BLOCK, P_HEADS, P_TOPK * P_TOPK)
        fv, fpos = lax.top_k(cand, P_TOPK)
        eidx = jnp.take_along_axis(cidx, fpos, axis=-1)
        g = jax.nn.softmax(fv, axis=-1)
        u = u_tab[eidx]
        act = jax.nn.gelu(jnp.einsum('td,thkd->thk', xb, u).astype(jnp.float32), approximate=False)
        return jnp.einsum('thk,thkd->td', (g * act).astype(xb.dtype), v_tab[eidx])

    return lax.map(block, xt).reshape(Bb, S, D)

def second_inputs(seed: int = 0) -> dict:
    key = jax.random.key(seed)
    ks = jax.random.split(key, 24)
    L, D = DEPTH, D_MODEL
    n_in = 4 * M_WIDTH + 2 * M_HEADS + 3 * D_WIDTH
    nrm = lambda k, shape, s: jax.random.normal(k, shape, jnp.float32) * s
    f_bias = jnp.linspace(3.0, 6.0, M_HEADS, dtype=jnp.float32)
    gate_b = jnp.concatenate([
        nrm(ks[7], (L, M_HEADS), 0.1),
        f_bias[None, :] + nrm(ks[8], (L, M_HEADS), 0.1)], axis=-1)
    return {
        "x": nrm(ks[0], (BATCH, SEQ, D), 1.0),
        "c": nrm(ks[1], (BATCH, D), 1.0),
        "ada_w": nrm(ks[2], (L, D, 6 * D), 0.5 * D ** -0.5),
        "ada_b": nrm(ks[3], (L, 6 * D), 0.02),
        "norm1_g": 1.0 + nrm(ks[4], (L, D), 0.02),
        "w_in": nrm(ks[5], (L, D, n_in), D ** -0.5),
        "conv_w": nrm(ks[6], (L, CONV_WIDTH, 2 * M_WIDTH), CONV_WIDTH ** -0.5),
        "conv_b": nrm(ks[9], (L, 2 * M_WIDTH), 0.02),
        "mlstm_gate_b": gate_b,
        "mlstm_norm_g": 1.0 + nrm(ks[10], (L, M_WIDTH), 0.02),
        "lambda_q1": nrm(ks[11], (L, D_HEAD_DIM), 0.1),
        "lambda_k1": nrm(ks[12], (L, D_HEAD_DIM), 0.1),
        "lambda_q2": nrm(ks[13], (L, D_HEAD_DIM), 0.1),
        "lambda_k2": nrm(ks[14], (L, D_HEAD_DIM), 0.1),
        "diff_norm_g": 1.0 + nrm(ks[15], (L, 2 * D_HEAD_DIM), 0.02),
        "w_out": nrm(ks[16], (L, MIX_WIDTH, D), MIX_WIDTH ** -0.5),
        "norm2_g": 1.0 + nrm(ks[17], (L, D), 0.02),
        "peer_w_query": nrm(ks[18], (L, D, P_HEADS * P_QUERY_DIM), D ** -0.5),
        "peer_sub_keys": nrm(ks[19], (L, P_HEADS, 2, N_KEYS, P_HALF), P_HALF ** -0.5),
        "peer_u": nrm(ks[20], (L, N_EXPERTS, D), D ** -0.5),
        "peer_v": nrm(ks[21], (L, N_EXPERTS, D), 0.1),
        "final_g": 1.0 + nrm(ks[22], (D,), 0.02),
    }

def second_block(x, c, ada_w, ada_b, norm1_g, w_in, conv_w, conv_b, mlstm_gate_b,
              mlstm_norm_g, lambda_q1, lambda_k1, lambda_q2, lambda_k2, diff_norm_g,
              w_out, norm2_g, peer_w_query, peer_sub_keys, peer_u, peer_v, final_g):
    Bb, S, D = x.shape
    split_pts = [M_WIDTH, 2 * M_WIDTH, 3 * M_WIDTH, 4 * M_WIDTH,
                 4 * M_WIDTH + M_HEADS, 4 * M_WIDTH + 2 * M_HEADS,
                 4 * M_WIDTH + 2 * M_HEADS + D_WIDTH,
                 4 * M_WIDTH + 2 * M_HEADS + 2 * D_WIDTH]
    for l in range(DEPTH):
        mod = jax.nn.silu(c) @ ada_w[l] + ada_b[l]
        sh1, sc1, g1, sh2, sc2, g2 = jnp.split(mod[:, None, :], 6, axis=-1)

        h = rmsnorm_2(x, norm1_g[l]) * (1.0 + sc1) + sh1
        p = h @ w_in[l]
        mq, mk, mv, mo, mi, mf, dq, dk, dv = jnp.split(p, split_pts, axis=-1)

        qk = jax.nn.silu(causal_dwconv(jnp.concatenate([mq, mk], axis=-1), conv_w[l], conv_b[l]))
        mq, mk = jnp.split(qk, 2, axis=-1)
        heads = lambda a: a.reshape(Bb, S, M_HEADS, M_HEAD_DIM).transpose(0, 2, 1, 3).astype(jnp.float32)
        q_m = heads(mq)
        k_m = heads(mk) * (M_HEAD_DIM ** -0.5)
        v_m = heads(mv)
        gb = mlstm_gate_b[l].astype(jnp.float32)
        ig = (mi.astype(jnp.float32) + gb[:M_HEADS]).transpose(0, 2, 1)
        lf = jax.nn.log_sigmoid(mf.astype(jnp.float32) + gb[M_HEADS:]).transpose(0, 2, 1)
        hm = mlstm_chunkwise(q_m, k_m, v_m, ig, lf).transpose(0, 2, 1, 3)
        hm = rmsnorm_2(hm, mlstm_norm_g[l].reshape(M_HEADS, M_HEAD_DIM)).reshape(Bb, S, M_WIDTH)
        hm = (hm * jax.nn.sigmoid(mo.astype(jnp.float32))).astype(x.dtype)

        lam_init = 0.8 - 0.6 * math.exp(-0.3 * l)
        lam = (jnp.exp(jnp.sum(lambda_q1[l].astype(jnp.float32) * lambda_k1[l].astype(jnp.float32)))
               - jnp.exp(jnp.sum(lambda_q2[l].astype(jnp.float32) * lambda_k2[l].astype(jnp.float32)))
               + lam_init)
        qk_heads = lambda a: a.reshape(Bb, S, D_HEADS, 2, D_HEAD_DIM).transpose(0, 2, 3, 1, 4).astype(jnp.float32)
        q_d, k_d = qk_heads(dq), qk_heads(dk)
        v_d = dv.reshape(Bb, S, D_HEADS, 2 * D_HEAD_DIM).transpose(0, 2, 1, 3).astype(jnp.float32)
        od = diff_attention(q_d, k_d, v_d, lam)
        od = rmsnorm_2(od, diff_norm_g[l]) * (1.0 - lam_init)
        od = od.transpose(0, 2, 1, 3).reshape(Bb, S, D_WIDTH).astype(x.dtype)

        y = jnp.concatenate([hm, od], axis=-1) @ w_out[l]
        x = x + g1 * y

        h2 = rmsnorm_2(x, norm2_g[l]) * (1.0 + sc2) + sh2
        x = x + g2 * peer(h2, peer_w_query[l], peer_sub_keys[l], peer_u[l], peer_v[l])

    return rmsnorm_2(x, final_g)


def setup_inputs(seed=0):
    out = dict(first_inputs(seed))
    for name, value in second_inputs(seed + 1).items():
        if name != "x":
            out[name + "_2"] = value
    return out


def reference(
    x, meta_tokens, norm_mix_w, w_in, w_gate_up, b_gate, gla_norm_w, sinks, w_out, norm_ff_w,
    w_ff1, w_ff2, final_norm_w, c_2, ada_w_2, ada_b_2, norm1_g_2, w_in_2, conv_w_2, conv_b_2,
    mlstm_gate_b_2, mlstm_norm_g_2, lambda_q1_2, lambda_k1_2, lambda_q2_2, lambda_k2_2,
    diff_norm_g_2, w_out_2, norm2_g_2, peer_w_query_2, peer_sub_keys_2, peer_u_2, peer_v_2,
    final_g_2,
):
    x = first_block(
        x, meta_tokens, norm_mix_w, w_in, w_gate_up, b_gate, gla_norm_w, sinks, w_out,
        norm_ff_w, w_ff1, w_ff2, final_norm_w,
    )
    return second_block(
        x, c_2, ada_w_2, ada_b_2, norm1_g_2, w_in_2, conv_w_2, conv_b_2, mlstm_gate_b_2,
        mlstm_norm_g_2, lambda_q1_2, lambda_k1_2, lambda_q2_2, lambda_k2_2, diff_norm_g_2,
        w_out_2, norm2_g_2, peer_w_query_2, peer_sub_keys_2, peer_u_2, peer_v_2, final_g_2,
    )


_drawn_inputs = setup_inputs


def setup_inputs(seed=0):
    import zlib

    import numpy as np

    out = dict(_drawn_inputs(seed))
    spreads = {}
    factors = {'norm_mix_w': 3.104,
     'b_gate': 2.841,
     'gla_norm_w': 6.266,
     'sinks': 64.0,
     'norm_ff_w': 3.295,
     'final_norm_w': 2.853,
     'ada_b_2': 3.47,
     'norm1_g_2': 8.0,
     'conv_b_2': 48.141,
     'mlstm_norm_g_2': 8.0,
     'lambda_q1_2': 3.534,
     'lambda_k1_2': 3.298,
     'lambda_q2_2': 4.383,
     'lambda_k2_2': 3.769,
     'diff_norm_g_2': 8.0,
     'norm2_g_2': 8.0,
     'peer_w_query_2': 3.416,
     'peer_sub_keys_2': 3.419,
     'peer_u_2': 3.818,
     'peer_v_2': 3.409,
     'final_g_2': 8.394}
    for name, (base, spread) in spreads.items():
        noise = np.random.default_rng([zlib.crc32(name.encode()), seed]).standard_normal(out[name].shape)
        drawn = base * np.exp(spread * noise) if base else spread * noise
        out[name] = __import__('jax').numpy.asarray(drawn.astype(out[name].dtype))
    for name, factor in factors.items():
        out[name] = (out[name] * factor).astype(out[name].dtype)
    return out
```

```python
from contextlib import ExitStack

import numpy as np

import concourse.bass as bass
from concourse import mybir

F32 = mybir.dt.float32
U32 = mybir.dt.uint32
ALU = mybir.AluOpType
ACT = mybir.ActivationFunctionType
AX = mybir.AxisListType.X

NT = 4
NM = 16
TX = 512
TA = TX + NM
LEVELS = (64, 32, 16, 8, 4, 2, 1)
BIGNEG = -1e30

COLS = [("ident", 128), ("mixw", 8), ("ffw", 8), ("n1g", 8), ("n2g", 8), ("bgate", 2), ("adab", 48), ("ccol", 8),
        ("convw", 32), ("convb", 8), ("gbi", 1), ("gbf", 1), ("wgu", 256), ("wig", 64), ("cos", TA), ("sin", TA),
        ("rot", 128), ("masks", 8 * 128), ("wmask", 272), ("negm", 128), ("caus", 128), ("reset", TA),
        ("iota", 16), ("sel", 512), ("mhalf", 4)]
COFF = {}
_o = 0
for _n, _w in COLS:
    COFF[_n] = (_o, _w)
    _o += _w
NCOL = _o
ROWS = [("fw", 1024), ("fg", 1024), ("gnw", 128), ("mng", 512), ("dng", 128), ("sink", 8),
        ("lq1", 64), ("lk1", 64), ("lq2", 64), ("lk2", 64)]
ROFF = {}
_o = 0
for _n, _w in ROWS:
    ROFF[_n] = (_o, _w)
    _o += _w
NROW = _o

PANELS = {"w1": 5, "wo1": 2, "ff1": 8, "ff2": 8, "ada": 12, "w2": 7, "wo2": 2, "wq": 4}
NP_RING = 3
NG = 8


class Queue:

    def __init__(self, sem):
        self.sem, self.n, self.items, self.seen = sem, 0, [], {}

    def need(self, toks):
        waits = []
        for sem, val in toks:
            if self.seen.get(sem.name, 0) < val:
                self.seen[sem.name] = val
                waits.append((sem, val))
        return waits

    def tok(self):
        return (self.sem, self.n)

    def add(self, fn, after, mark=True, sem=None, inc=1):
        waits = self.need(after)
        if sem is None and mark:
            self.n += 1
            sem = self.sem
        self.items.append((waits, fn, sem, inc))
        return (sem, self.n) if inc == 1 else None

    def run(self, eng):
        for waits, fn, sem, inc in self.items:
            for s, v in waits:
                eng.wait_ge(s, v)
            if fn is None:
                continue
            ins = fn(eng)
            if sem is not None:
                ins.then_inc(sem, inc)


def build(nc, packs, rows, x, meta, W, skT, utab, vtab, out):
    ctx = ExitStack()
    with ctx:
        def sb(name, n, dt=F32, p=128):
            return ctx.enter_context(nc.sbuf_tensor(name, [p, n], dt))

        ring = sb("ring", NP_RING * 4096)
        hres = sb("hres", 4096)
        xT = sb("xT", 8 * TA)
        cols = sb("cols", NCOL)
        rowb = sb("rowb", NROW)
        mod = sb("mod", 48)
        small = sb("small", 640)
        big = sb("big", 23460)
        g2b, B2b = big[:, 21412:22436], big[:, 22436:23460]
        g1b = cols[:, COFF["cos"][0]:COFF["cos"][0] + 1024]
        A2b = cols[:, COFF["masks"][0]:COFF["masks"][0] + 1024]
        PS = [ctx.enter_context(nc.psum_tensor(f"ps{i}", [128, 512], F32)) for i in range(8)]

        def sem(name):
            return ctx.enter_context(nc.semaphore(name))

        qv, qs, qg, qp, qd = (Queue(sem("s_" + n)) for n in ("vec", "act", "pool", "pe", "sp"))

        def V(f, *after):
            return qv.add(f, [*after, qv.tok()])

        def S(f, *after):
            return qs.add(f, [*after, qs.tok()])

        def G(f, *after):
            return qg.add(f, [*after, qg.tok()])

        def MM(o, l, r, *after, start=True, stop=True, mark=None, share=False):
            return qp.add(lambda e: e.matmul(o, lhsT=l, rhs=r, start=start, stop=stop, skip_group_check=share),
                          after, mark=stop if mark is None else mark)

        def TR(o, i, *after, mark=True):
            k = i.shape[0]
            return qp.add(lambda e: e.transpose(o, i, ident[0:k, 0:k]), after, mark=mark)

        def fence():
            toks = [q.tok() for q in (qv, qs, qg, qp) if q.n]
            for q in (qv, qs, qg, qp):
                q.items.append((q.need([t for t in toks if t[0] is not q.sem]), None, None, 0))
            return toks

        def col(name, a=0, b=None):
            o, w = COFF[name]
            return cols[:, o + a:o + (w if b is None else b)]

        def row(name, a=0, b=None):
            o, w = ROFF[name]
            return rowb[:, o + a:o + (w if b is None else b)]

        ident = col("ident")
        dma_n = {}

        def LOAD(q, dst, src, s, *after, n=16):
            q.add(lambda e: e.dma_start(dst, src), after, sem=s, inc=16)
            dma_n[s.name] = dma_n.get(s.name, 0) + 16
            return (s, dma_n[s.name])

        s_x, s_c, s_r, s_sk, s_out = sem("s_x"), sem("s_c"), sem("s_r"), sem("s_sk"), sem("s_out")
        s_pan = [sem(f"s_pan{i}") for i in range(NP_RING)]
        h3 = hres[:, :].rearrange("p (t d) -> p t d", t=NT)
        mrow = big[0:NM, 16384:16384 + 1024]
        t_c = LOAD(qs, cols[:, :], packs, s_c)
        LOAD(qd, h3, x.rearrange("(t p) d -> p t d", p=128), s_x)
        t_x = LOAD(qd, mrow, meta, s_x)
        t_r = LOAD(qs, rowb[:, :], rows.to_broadcast([128, NROW]), s_r)

        order = [("w1", i) for i in range(5)] + [("wo1", 0), ("wo1", 1)]
        for i in range(8):
            order += [("ff1", i), ("ada", i)]
        for i in range(8):
            order += [("ff2", i)] + ([("ada", 8 + i)] if i < 4 else [])
        order += [("w2", i) for i in range(7)] + [("wo2", 0), ("wo2", 1)] + [("wq", i) for i in range(4)]
        freed = {}
        state = {"i": 0}

        def issue(n):
            name, i = order[n]
            slot = n % NP_RING
            w = W[name][i].shape[1]
            after = [freed[n - NP_RING]] if n >= NP_RING else []
            freed[("load", n)] = LOAD(qd, ring[:, slot * 4096:slot * 4096 + w], W[name][i], s_pan[slot], *after)

        for n in range(NP_RING):
            issue(n)

        def panel(name, i):
            n = state["i"]
            assert order[n] == (name, i), (order[n], name, i)
            state["i"] += 1
            w = W[name][i].shape[1]
            slot = n % NP_RING
            return ring[:, slot * 4096:slot * 4096 + w].rearrange("p (k c) -> p k c", k=8), freed[("load", n)], n

        def release(n, tok):
            freed[n] = tok
            if n + NP_RING < len(order):
                issue(n + NP_RING)

        sm = small
        mh = col("mhalf")

        def rstd(dst, ss, d, eps, *after):
            p, n = ss.shape[0], ss.shape[1]
            t = V(lambda e: e.tensor_scalar(ss, ss, 1.0 / d, eps, ALU.mult, ALU.add), *after)
            return G(lambda e: e.tensor_tensor(dst, ss, mh[0:p, 0:n], ALU.pow), t, t_c)

        def sumsq(dst, src, junk, *after):
            return S(lambda e: e.activation(junk, src, ACT.Square, accum_out=dst), *after)

        bankfree = [[] for _ in range(8)]

        def norm_T(src, scale, bias, banks, t_src, dst3, toks):
            for k in range(8):
                b = banks[k % len(banks)]
                for t in range(NT):
                    tk = TR(PS[b][:, t * 128:(t + 1) * 128], src[:, t, k * 128:(k + 1) * 128], t_src[t], t_c,
                            *bankfree[b], mark=(t == NT - 1))
                o = dst3[:, k, 0:TX]
                if bias is None:
                    v = V(lambda e, o=o, b=b, k=k: e.tensor_scalar(o, PS[b][:, :], scale[:, k:k + 1], None, ALU.mult), tk)
                elif k % 2:
                    v = S(lambda e, o=o, b=b, k=k: e.activation(o, PS[b][:, :], ACT.Identity, bias=bias[:, k:k + 1],
                                                                scale=scale[:, k:k + 1]), tk)
                else:
                    v = V(lambda e, o=o, b=b, k=k: e.tensor_scalar(o, PS[b][:, :], scale[:, k:k + 1],
                                                                   bias[:, k:k + 1], ALU.mult, ALU.add), tk)
                bankfree[b] = [v]
                toks.append(v)

        x3 = xT[:, :].rearrange("p (k c) -> p k c", k=8)

        xs3 = big[:, 8192:12288].rearrange("p (t d) -> p t d", t=NT)
        junk = big[:, 12288:13312]
        ssa = sm[:, 0:4]
        ssm = sm[0:NM, 4:5]
        for t in range(NT):
            a = sumsq(sm[:, t:t + 1], h3[:, t, :], junk, t_x)
        am = sumsq(ssm, mrow, junk[0:NM, :])
        r = rstd(sm[:, 8:12], ssa, 1024.0, 1e-5, am)
        rm = rstd(sm[0:NM, 12:13], ssm, 1024.0, 1e-5, am)
        t_src = [V(lambda e, t=t: e.tensor_scalar(xs3[:, t, :], h3[:, t, :], sm[:, 8 + t:9 + t], None, ALU.mult), r)
                 for t in range(NT)]
        tm = V(lambda e: e.tensor_scalar(mrow, mrow, sm[0:NM, 12:13], None, ALU.mult), rm)
        toks = []
        norm_T(xs3, col("mixw"), None, [0, 1, 2], t_src, x3, toks)
        for k in range(8):
            tk = TR(PS[3][:, k * NM:(k + 1) * NM], mrow[:, k * 128:(k + 1) * 128], tm, t_c)
        mw = col("mixw").rearrange("p (k o) -> p k o", o=1).to_broadcast([128, 8, NM])
        toks.append(V(lambda e: e.tensor_tensor(x3[:, :, TX:TA], PS[3][:, 0:128].rearrange("p (k c) -> p k c", k=8),
                                                mw, ALU.mult), tk))
        t_xT = fence()

        off, lim = [0], [23460]

        def carve(n, p=128):
            o = off[0]
            off[0] += n
            assert off[0] <= lim[0], off[0]
            return big[0:p, o:o + n]

        mixT = carve(4096).rearrange("p (k c) -> p k c", k=8)
        gqT = carve(1024).rearrange("p (a c) -> p a c", a=2)
        gkT = carve(1024).rearrange("p (a c) -> p a c", a=2)
        gkm = carve(32).rearrange("p (a c) -> p a c", a=2)
        lrT = carve(TA, 16)
        sqT = carve(2048).rearrange("p (a c) -> p a c", a=4)
        skT1 = carve(TA)
        gv = carve(2048).rearrange("p (t c) -> p t c", t=NT)
        gvm = carve(512, NM)
        gr = carve(2048).rearrange("p (t c) -> p t c", t=NT)
        sv = carve(512).rearrange("p (t c) -> p t c", t=NT)
        svm = carve(128, NM)
        mark1 = off[0]
        rr = {"i": 0}

        def bank(banks=tuple(range(8))):
            b = banks[rr["i"] % len(banks)]
            rr["i"] += 1
            return b

        def projT(pv, c, m, tp, outs, scale=None):
            for (a, z, dst) in outs:
                b = bank()
                for k in range(8):
                    tk = MM(PS[b][0:m, 0:z - a], pv[:, k, c:c + m], x3[:, k, a:z], tp, *(bankfree[b] if k == 0 else []),
                            start=(k == 0), stop=(k == 7))
                src = PS[b][0:m, 0:z - a]
                if scale is None:
                    v = V(lambda e, dst=dst, src=src: e.tensor_copy(dst, src), tk)
                else:
                    v = V(lambda e, dst=dst, src=src: e.tensor_scalar(dst, src, scale, None, ALU.mult), tk)
                bankfree[b] = [v]
            return tk, v

        def projR(pv, c, m, tp, outs, fn=None):
            for (a, z, dst) in outs:
                b = bank()
                for k in range(8):
                    tk = MM(PS[b][0:z - a, 0:m], x3[:, k, a:z], pv[:, k, c:c + m], tp, *(bankfree[b] if k == 0 else []),
                            start=(k == 0), stop=(k == 7))
                v = S(lambda e, dst=dst, src=PS[b][0:z - a, 0:m]: e.activation(dst, src, fn or ACT.Copy), tk)
                bankfree[b] = [v]
            return tk, v

        for b in range(8):
            bankfree[b] = []
        pv, tp, n = panel("w1", 0)
        for a in range(2):
            projT(pv, 128 * a, 128, tp, [(0, TX, gqT[:, a, :])], scale=0.125)
        for a in range(2):
            tk, v = projT(pv, 256 + 128 * a, 128, tp, [(0, TX, gkT[:, a, :]), (TX, TA, gkm[:, a, :])])
        release(n, tk)
        pv, tp, n = panel("w1", 1)
        for a in range(4):
            tk, v = projT(pv, 128 * a, 128, tp, [(0, TX, sqT[:, a, :])])
        release(n, tk)
        pv, tp, n = panel("w1", 2)
        tk, v = projR(pv, 0, 512, tp, [(t * 128, t * 128 + 128, gv[:, t, :]) for t in range(NT)] + [(TX, TA, gvm)])
        release(n, tk)
        pv, tp, n = panel("w1", 3)
        tk, v = projR(pv, 0, 512, tp, [(t * 128, t * 128 + 128, gr[:, t, :]) for t in range(NT)], fn=ACT.Silu)
        release(n, tk)
        pv, tp, n = panel("w1", 4)
        projT(pv, 0, 128, tp, [(0, TX, skT1[:, 0:TX]), (TX, TA, skT1[:, TX:TA])])
        projT(pv, 256, 16, tp, [(0, TX, lrT[:, 0:TX]), (TX, TA, lrT[:, TX:TA])])
        tk, v = projR(pv, 128, 128, tp, [(t * 128, t * 128 + 128, sv[:, t, :]) for t in range(NT)] + [(TX, TA, svm)])
        release(n, tk)
        gnw = row("gnw").rearrange("p (o c) -> p o c", o=1).to_broadcast([128, 16, 128])
        grv = gr.rearrange("p t (h c) -> p (t h) c", h=4)
        V(lambda e: e.tensor_tensor(grv, grv, gnw, ALU.mult), v, t_r)
        fence()

        for b in range(8):
            bankfree[b] = []
        zb = xT[:, 0:2 * TA].rearrange("p (a c) -> p a c", a=2)
        za = xT[:, 2 * TA:4 * TA].rearrange("p (a c) -> p a c", a=2)
        bx = carve(1024).rearrange("p (a c) -> p a c", a=2)
        bm = carve(32).rearrange("p (a c) -> p a c", a=2)
        rc = xT[:, 4 * TA:5 * TA]

        def rope(xap, a, z):
            b = bank((6, 7))
            tk = MM(PS[b][:, 0:z - a], col("rot"), xap, *bankfree[b])
            w = rc[:, 0:z - a]
            v = V(lambda e: e.tensor_tensor(w, PS[b][:, 0:z - a], col("sin", a, z), ALU.mult), tk)
            bankfree[b] = [v]
            v = V(lambda e: e.tensor_tensor(xap, xap, col("cos", a, z), ALU.mult))
            return V(lambda e: e.tensor_tensor(xap, xap, w, ALU.add))

        for a in range(2):
            for (c0, c1) in ((0, TX), (TX, TA)):
                b = bank((0, 1, 2, 3))
                tk = MM(PS[b][:, 0:c1 - c0], cols[0:16, COFF["wgu"][0] + 128 * a:COFF["wgu"][0] + 128 * a + 128],
                        lrT[:, c0:c1])
                V(lambda e, a=a, b=b, c0=c0, c1=c1: e.tensor_scalar(zb[:, a, c0:c1], PS[b][:, 0:c1 - c0],
                                                                    col("bgate", a, a + 1), None, ALU.add), tk)
        t = qv.tok()
        t = S(lambda e: e.activation(za, zb, ACT.Abs), t)
        t = S(lambda e: e.activation(za, za, ACT.Exp, scale=-1.0))
        t = S(lambda e: e.activation(za, za, ACT.Ln, bias=1.0))
        for a in range(4):
            rope(sqT[:, a, :], 0, TX)
        rope(skT1[:, 0:TX], 0, TX)
        t_rope = rope(skT1[:, TX:TA], TX, TA)
        V(lambda e: e.scalar_tensor_tensor(out=zb, in0=zb, scalar=0.0, in1=za, op0=ALU.min, op1=ALU.subtract), t)
        for a in range(2):
            V(lambda e, a=a: e.tensor_tensor_scan(bx[:, a, :], col("reset", 0, TX), zb[:, a, 0:TX], 0.0, ALU.mult, ALU.add))
            V(lambda e, a=a: e.tensor_tensor_scan(bm[:, a, :], col("reset", TX, TA), zb[:, a, TX:TA], 0.0, ALU.mult, ALU.add))
        E = za[:, :, 0:TX]
        D = zb[:, :, 0:TX]
        Qs = carve(1024).rearrange("p (a c) -> p a c", a=2)
        Ks = carve(1024).rearrange("p (a c) -> p a c", a=2)
        Qs2 = carve(1024).rearrange("p (a c) -> p a c", a=2)
        A = carve(2048)
        fl = "p a (n s) -> p (a n) s"
        last = V(lambda e: e.memset(A[:, :], 0.0))
        prev_mm = None
        for li, s in enumerate((0,) + LEVELS):
            if s == 0:
                q_in, k_in, t_q = gqT, gkT, last
            else:
                Ef = xT[:, 2 * TA:2 * TA + 1024]
                Df = xT[:, 0:1024]
                bxf = bx.rearrange("p a c -> p (a c)").rearrange("p (n s) -> p n s", s=2 * s)
                nb = 1024 // (2 * s)
                ref = bxf[:, :, s - 1:s].to_broadcast([128, nb, 2 * s])
                d = V(lambda e, bxf=bxf, ref=ref, s=s: e.tensor_tensor(Df.rearrange("p (n s) -> p n s", s=2 * s), bxf, ref,
                                                                       ALU.subtract), qs.tok())
                ab = S(lambda e: e.activation(Ef, Df, ACT.Abs), d)
                ex = S(lambda e: e.activation(Ef, Ef, ACT.Exp, scale=-1.0 / 16.0))
                Efv = Ef.rearrange("p (a c) -> p a c", a=2)
                V(lambda e: e.tensor_tensor(Qs, gqT, Efv, ALU.mult), ex, prev_mm)
                t_q = V(lambda e: e.tensor_tensor(Ks, gkT, Efv, ALU.mult))
                q_in, k_in = Qs, Ks
            for c in range(NT):
                cc, par = c // 2, c % 2
                for i in range(4):
                    ci, h = 2 * cc + i // 2, 2 * (i % 2) + par
                    p0 = 64 * par
                    prev_mm = MM(PS[c][:, i * 128:(i + 1) * 128], k_in[p0:p0 + 64, h // 2, ci * 128:(ci + 1) * 128],
                                 q_in[p0:p0 + 64, h // 2, ci * 128:(ci + 1) * 128], t_q, *bankfree[c])
                mk = cols[:, COFF["masks"][0] + 128 * li:COFF["masks"][0] + 128 * (li + 1)].bitcast(U32)\
                    .rearrange("p (o c) -> p o c", o=1).to_broadcast([128, 4, 128])
                v = V(lambda e, c=c, mk=mk: e.copy_predicated(
                    A[:, c * 512:(c + 1) * 512].rearrange("p (h i) -> p h i", h=4), mk,
                    PS[c][:, :].rearrange("p (h i) -> p h i", h=4)), prev_mm)
                bankfree[c] = [v]
        dec = sm[:, 16:26]
        dec3 = dec[:, 0:8].rearrange("p (a c) -> p a c", a=2)
        Df = xT[:, 0:1024]
        Ef = xT[:, 2 * TA:2 * TA + 1024]
        bc = bx.rearrange("p a c -> p (a c)").rearrange("p (n s) -> p n s", s=128)
        d = V(lambda e: e.tensor_tensor(Df.rearrange("p (n s) -> p n s", s=128), bc[:, :, 127:128].to_broadcast([128, 8, 128]),
                                        bc, ALU.subtract), qs.tok())
        ex = S(lambda e: e.activation(Ef, Df, ACT.Exp, scale=1.0 / 16.0), d)
        V(lambda e: e.tensor_tensor(Ks.rearrange("p a c -> p (a c)"), gkT.rearrange("p a c -> p (a c)"), Ef, ALU.mult), ex, prev_mm)
        d = V(lambda e: e.tensor_tensor(Qs2[:, :, 0:NM], bm[:, :, NM - 1:NM].to_broadcast([128, 2, NM]), bm, ALU.subtract))
        ex = S(lambda e: e.activation(Qs2[:, :, 0:NM], Qs2[:, :, 0:NM], ACT.Exp, scale=1.0 / 16.0), d)
        t_km = V(lambda e: e.tensor_tensor(gkm, gkm, Qs2[:, :, 0:NM], ALU.mult), ex)
        bl = bc[:, :, 127]
        t_dec = S(lambda e: e.activation(dec[:, 0:8], bl, ACT.Exp, scale=1.0 / 16.0))
        ex = S(lambda e: e.activation(Qs2.rearrange("p a c -> p (a c)"), bx.rearrange("p a c -> p (a c)"), ACT.Exp, scale=1.0 / 16.0),
               t_km)
        t_qb = V(lambda e: e.tensor_tensor(Qs2, Qs2, gqT, ALU.mult), ex)
        kh = Qs
        khv = kh.rearrange("p a c -> p (a c)").rearrange("p (c d) -> p c d", c=4)
        khm = big[0:NM, off[0]:off[0] + 256]
        off[0] += 256
        for a in range(2):
            tk = TR(PS[4][0:NM, a * 128:(a + 1) * 128], gkm[:, a, :], t_km)
        t_kh = [V(lambda e: e.tensor_copy(khm, PS[4][0:NM, 0:256]), tk)]
        for c in range(3):
            b = (5, 6, 7)[c]
            for a in range(2):
                tk = TR(PS[b][:, a * 128:(a + 1) * 128], Ks[:, a, c * 128:(c + 1) * 128], t_km, *bankfree[b])
            v = V(lambda e, b=b, c=c: e.tensor_copy(khv[:, c, :], PS[b][:, 0:256]), tk)
            bankfree[b] = [v]
            t_kh.append(v)
        bankfree[4] = [t_kh[0]]
        St = carve(2048).rearrange("p (c a v) -> p c a v", c=4, a=2)
        t_z = V(lambda e: e.memset(St, 0.0))
        t_S = None
        for c in range(NT):
            b = (5, 6, 7, 4)[c]
            kk = khm if c == 0 else khv[:, c - 1, :]
            vv = gvm if c == 0 else gv[:, c - 1, :]
            for a in range(2):
                tk = MM(PS[b][:, a * 256:(a + 1) * 256], kk[:, a * 128:(a + 1) * 128], vv[:, a * 256:(a + 1) * 256],
                        t_kh[c], *bankfree[b])
            for a in range(2):
                for u in range(2):
                    p0 = 64 * u
                    blk = PS[b][p0:p0 + 64, a * 256 + u * 128:a * 256 + (u + 1) * 128]
                    dst = St[p0:p0 + 64, c, a, u * 128:(u + 1) * 128]
                    if c == 0:
                        t_S = V(lambda e, dst=dst, blk=blk: e.tensor_copy(dst, blk), tk)
                    else:
                        t_S = V(lambda e, dst=dst, blk=blk, a=a, u=u, p0=p0, c=c: e.scalar_tensor_tensor(
                            out=dst, in0=St[p0:p0 + 64, c - 1, a, u * 128:(u + 1) * 128], scalar=dec3[p0:p0 + 64, a, c - 1:c],
                            in1=blk, op0=ALU.mult, op1=ALU.add), tk, t_dec)
            bankfree[b] = [t_S]
        o3 = xT[:, 0:2048].rearrange("p (t c) -> p t c", t=NT)
        sq = xT[:, 3600:4112]
        ss4 = sm[:, 32:48]
        ev = []
        for c in range(NT):
            for a in range(2):
                MM(PS[c][:, a * 256:(a + 1) * 256], Qs2[:, a, c * 128:(c + 1) * 128], St[:, c, a, :], t_qb, t_S,
                   *bankfree[c], stop=False)
                for u in range(2):
                    h = 2 * a + u
                    blk = ((c // 2) * 2 + u) * 4 + (c % 2) * 2 + a
                    tk = MM(PS[c][:, h * 128:(h + 1) * 128], A[:, blk * 128:(blk + 1) * 128],
                            gv[:, c, h * 128:(h + 1) * 128], start=False, stop=(u == 1), mark=True)
            a = S(lambda e, c=c: e.activation(sq, PS[c][:, :], ACT.Square), tk, qv.tok())
            V(lambda e, c=c: e.tensor_reduce(ss4[:, 4 * c:4 * c + 4], sq.rearrange("p (h v) -> p h v", h=4), AX, ALU.add), a)
            v = V(lambda e, c=c: e.tensor_tensor(o3[:, c, :], PS[c][:, :], gr[:, c, :], ALU.mult))
            r = rstd(sm[:, 48 + 4 * c:52 + 4 * c], ss4[:, 4 * c:4 * c + 4], 128.0, 1e-5)
            v = V(lambda e, c=c: e.tensor_tensor(
                o3[:, c, :].rearrange("p (h v) -> p h v", h=4), o3[:, c, :].rearrange("p (h v) -> p h v", h=4),
                sm[:, 48 + 4 * c:52 + 4 * c].rearrange("p (h o) -> p h o", o=1).to_broadcast([128, 4, 128]), ALU.mult), r)
            b = 4 + c
            for h in range(4):
                tk = TR(PS[b][:, h * 128:(h + 1) * 128], o3[:, c, h * 128:(h + 1) * 128], v, *bankfree[b], mark=(h == 3))
            S(lambda e, b=b, c=c: e.activation(mixT[:, 0:4, c * 128:(c + 1) * 128],
                                               PS[b][:, :].rearrange("p (h v) -> p h v", h=4), ACT.Copy), tk)
        fence()

        for b in range(8):
            bankfree[b] = []
        off[0] = mark1
        Sa = carve(8 * 272).rearrange("p (h k) -> p h k", h=8)
        PT = xT[:, 0:3072].rearrange("p (b c) -> p b c", b=3)
        snk = row("sink")
        for n in range(NT):
            w0 = 0 if n else 128
            for h in range(8):
                p0, j = 64 * (h // 4), h % 4
                b = bank((0, 1) if h < 4 else (2, 3))
                q = sqT[p0:p0 + 64, j, n * 128:(n + 1) * 128]
                MM(PS[b][:, 256:272], q, skT1[p0:p0 + 64, TX:TA], *bankfree[b], mark=False)
                tk = MM(PS[b][:, w0:256], q, skT1[p0:p0 + 64, (n - 1) * 128 + w0:(n + 1) * 128])
                v = V(lambda e, b=b, h=h, w0=w0: e.scalar_tensor_tensor(
                    out=Sa[:, h, w0:272], in0=PS[b][:, w0:272], scalar=0.125, in1=col("wmask", w0, 272),
                    op0=ALU.mult, op1=ALU.add), tk)
                bankfree[b] = [v]
            mx, ng, Z, es = sm[:, 64:72], sm[:, 72:80], sm[:, 80:88], sm[:, 88:96]
            V(lambda e, w0=w0: e.tensor_reduce(mx, Sa[:, :, w0:272], AX, ALU.max))
            V(lambda e: e.tensor_tensor(mx, mx, snk, ALU.max))
            V(lambda e: e.tensor_scalar(ng, mx, -1.0, None, ALU.mult))
            v = V(lambda e: e.tensor_tensor(es, snk, mx, ALU.subtract))
            for h in range(8):
                a = S(lambda e, h=h, w0=w0: e.activation(Sa[:, h, w0:272], Sa[:, h, w0:272], ACT.Exp, bias=ng[:, h:h + 1],
                                                        accum_out=Z[:, h:h + 1]), v)
            a = S(lambda e: e.activation(es, es, ACT.Exp))
            V(lambda e: e.tensor_tensor(Z, Z, es, ALU.add), a)
            V(lambda e: e.reciprocal(Z, Z))
            v = V(lambda e, w0=w0: e.tensor_tensor(
                Sa[:, :, w0:272], Sa[:, :, w0:272],
                Z.rearrange("p (h o) -> p h o", o=1).to_broadcast([128, 8, 272 - w0]), ALU.mult))
            blocks = [(0, 0, 128)] * (n > 0) + [(1, 128, 128), (2, 256, NM)]
            tv = {}
            for (bi, c0, w) in blocks:
                for g in range(2):
                    b = bank((4, 5, 6))
                    for j in range(4):
                        tk = TR(PS[b][0:w, j * 128:(j + 1) * 128], Sa[:, 4 * g + j, c0:c0 + w], v, *bankfree[b], mark=(j == 3))
                    dst = PT[0:w, bi, g * 512:(g + 1) * 512]
                    cp = S(lambda e, dst=dst, b=b, w=w: e.activation(dst, PS[b][0:w, :], ACT.Copy), tk)
                    bankfree[b] = [cp]
                    tv[(bi, g)] = cp
            for g in range(2):
                for i, (bi, c0, w) in enumerate(blocks):
                    vs = svm if bi == 2 else sv[:, n - 1 + bi, :]
                    tk = MM(PS[7][64 * g:64 * g + 64, :], vs[:, 64 * g:64 * g + 64], PT[0:w, bi, g * 512:(g + 1) * 512],
                            tv[(bi, g)], *bankfree[7], start=(i == 0), stop=(i == len(blocks) - 1))
            cp = S(lambda e, n=n: e.activation(mixT[:, 4:8, n * 128:(n + 1) * 128],
                                               PS[7][:, :].rearrange("p (j c) -> p j c", j=4), ACT.Copy), tk)
            bankfree[7] = [cp]
        fence()

        for b in range(8):
            bankfree[b] = []

        def out_proj(name, gate):
            for half in range(2):
                pv, tp, n = panel(name, half)
                for t in range(NT):
                    b = bank()
                    for k in range(8):
                        tk = MM(PS[b][:, :], mixT[:, k, t * 128:(t + 1) * 128], pv[:, k, :], tp,
                                *(bankfree[b] if k == 0 else []), start=(k == 0), stop=(k == 7))
                    hs = h3[:, t, half * 512:(half + 1) * 512]
                    if gate is None:
                        v = V(lambda e, hs=hs, b=b: e.tensor_tensor(hs, hs, PS[b][:, :], ALU.add), tk)
                    else:
                        w = xT[:, (b % 4) * 512:(b % 4) * 512 + 512]
                        v = V(lambda e, w=w, b=b, half=half: e.tensor_tensor(w, PS[b][:, :], gate[:, half * 512:(half + 1) * 512],
                                                                          ALU.mult), tk)
                        v2 = V(lambda e, w=w, hs=hs: e.tensor_tensor(hs, hs, w, ALU.add))
                    bankfree[b] = [v]
                release(n, tk)
            return qv.tok()

        v = out_proj("wo1", None)
        fence()

        def row_norm(eps, junk):
            for t in range(NT):
                a = sumsq(sm[:, t:t + 1], h3[:, t, :], junk)
            return rstd(sm[:, 8:12], sm[:, 0:4], 1024.0, eps, a)

        xs3b = big[:, 0:4096].rearrange("p (t d) -> p t d", t=NT)
        r = row_norm(1e-5, big[:, 8192:9216])
        t_src = [V(lambda e, t=t: e.tensor_scalar(xs3b[:, t, :], h3[:, t, :], sm[:, 8 + t:9 + t], None, ALU.mult), r)
                 for t in range(NT)]
        for b in range(8):
            bankfree[b] = []
        norm_T(xs3b, col("ffw"), None, [0, 1, 2, 3], t_src, x3, [])
        fence()

        csil = sm[:, 96:104]
        t_cs = S(lambda e: e.activation(csil, col("ccol"), ACT.Silu), t_c)
        aT = big[:, 0:16384].rearrange("p (f c) -> p f c", f=32)

        def ada(i):
            pv, tp, n = panel("ada", i)
            for j in range(4):
                for k in range(8):
                    tk = MM(PS[7][:, 4 * i + j:4 * i + j + 1], pv[:, k, j * 128:(j + 1) * 128], csil[:, k:k + 1], tp, t_cs,
                            start=(k == 0), stop=(k == 7))
            release(n, tk)
            return tk

        for b in range(8):
            bankfree[b] = []
        t_a = {}
        for i in range(8):
            pv, tp, n = panel("ff1", i)
            for j in range(4):
                f = 4 * i + j
                b = bank((4, 5, 6))
                for k in range(8):
                    tk = MM(PS[b][:, :], pv[:, k, j * 128:(j + 1) * 128], x3[:, k, 0:TX], tp,
                            *(bankfree[b] if k == 0 else []), start=(k == 0), stop=(k == 7))
                a = S(lambda e, f=f, b=b: e.activation(aT[:, f, :], PS[b][:, :], ACT.Relu), tk)
                bankfree[b] = [a]
                t_a[f] = S(lambda e, f=f: e.activation(aT[:, f, :], aT[:, f, :], ACT.Square))
            release(n, tk)
            ada(i)
        for half in range(2):
            bs = (0, 1, 2, 3) if half == 0 else (4, 5, 6, 7)
            for q in range(4):
                pv, tp, n = panel("ff2", 4 * half + q)
                for t in range(NT):
                    for k in range(8):
                        f = 8 * q + k
                        tk = MM(PS[bs[t]][:, :], aT[:, f, t * 128:(t + 1) * 128], pv[:, k, :], tp, t_a[f],
                                *(bankfree[bs[t]] if f == 0 else []), start=(f == 0), stop=(f == 31), mark=(f == 31 or k == 7))
                    if q == 3:
                        hs = h3[:, t, half * 512:(half + 1) * 512]
                        V(lambda e, hs=hs, b=bs[t]: e.tensor_tensor(hs, hs, PS[b][:, :], ALU.add), tk)
                release(n, tk)
                if half == 0:
                    tk = ada(8 + q)
                    if q == 3:
                        v = V(lambda e: e.tensor_tensor(mod[:, :], PS[7][:, 0:48], col("adab"), ALU.add), tk)
                        bankfree[7] = [v]
        fence()

        jk = big[:, 8192:9216]
        for t in range(NT):
            a = sumsq(sm[:, t:t + 1], h3[:, t, :], jk)
        r = rstd(sm[:, 8:12], sm[:, 0:4], 1024.0, 1e-5, a)
        for t in range(NT):
            v = V(lambda e, t=t: e.scalar_tensor_tensor(out=h3[:, t, :], in0=h3[:, t, :], scalar=sm[:, 8 + t:9 + t],
                                                        in1=row("fw"), op0=ALU.mult, op1=ALU.mult), r)
            a = sumsq(sm[:, t:t + 1], h3[:, t, :], jk, v)
        r = rstd(sm[:, 12:16], sm[:, 0:4], 1024.0, 1e-6, a)
        t_src = [V(lambda e, t=t: e.tensor_scalar(xs3b[:, t, :], h3[:, t, :], sm[:, 12 + t:13 + t], None, ALU.mult), r)
                 for t in range(NT)]
        sc1 = sm[:, 104:112]
        sc2 = sm[:, 112:120]
        V(lambda e: e.scalar_tensor_tensor(out=sc1, in0=mod[:, 8:16], scalar=1.0, in1=col("n1g"), op0=ALU.add, op1=ALU.mult))
        v = V(lambda e: e.scalar_tensor_tensor(out=sc2, in0=mod[:, 32:40], scalar=1.0, in1=col("n2g"), op0=ALU.add,
                                               op1=ALU.mult))
        for b in range(8):
            bankfree[b] = []
        t_src = [v if i == 3 else t_ for i, t_ in enumerate(t_src)]
        norm_T(xs3b, sc1, mod[:, 0:8], [0, 1, 2, 3], t_src, x3, [])


        def spread(dst, colap, i, *after):
            dg = big[:, 9216 + 1024 * i:9216 + 1024 * (i + 1)].rearrange("p (k c) -> p k c", k=8)
            v = V(lambda e: e.tensor_tensor(dg, ident.rearrange("p (o c) -> p o c", o=1).to_broadcast([128, 8, 128]),
                                            colap.rearrange("p (k o) -> p k o", o=1).to_broadcast([128, 8, 128]), ALU.mult), *after)
            for hf in range(2):
                b = (4, 5, 6, 7)[(2 * i + hf) % 4]
                for k in range(4):
                    tk = MM(PS[b][:, k * 128:(k + 1) * 128], ones, dg[:, 4 * hf + k, :], v, *bankfree[b])
                cp = V(lambda e, b=b, hf=hf: e.tensor_copy(dst[:, hf * 512:(hf + 1) * 512], PS[b][:, :]), tk)
                bankfree[b] = [cp]

        ones = big[:, 9216 + 4096:9216 + 4096 + 128]
        v1 = V(lambda e: e.memset(ones, 1.0))
        spread(g1b, mod[:, 16:24], 0, v1)
        spread(g2b, mod[:, 40:48], 1)
        spread(A2b, sc2, 2)
        spread(B2b, mod[:, 24:32], 3)
        fence()

        for b in range(8):
            bankfree[b] = []
        off[0], lim[0] = 0, 21412
        mixT = carve(4096).rearrange("p (k c) -> p k c", k=8)
        qk = carve(4096).rearrange("p (a c) -> p a c", a=8)
        mv = carve(4 * 4 * 129).rearrange("p (t h c) -> p t h c", t=4, h=4)
        mo = carve(2048).rearrange("p (t c) -> p t c", t=NT)
        dq = carve(2048).rearrange("p (a c) -> p a c", a=4)
        dk = carve(2048).rearrange("p (a c) -> p a c", a=4)
        dv = carve(2048).rearrange("p (t c) -> p t c", t=NT)
        ho3 = carve(2048).rearrange("p (t c) -> p t c", t=NT)
        ub = big[:, 0:1030].rearrange("p (a c) -> p a c", a=2)
        cy = big[:, 1030:1542]
        V(lambda e: e.memset(ub[:, :, 0:3], 0.0))
        V(lambda e: e.memset(mv[:, :, :, 128:129], 1.0))
        cyfree = None
        for i in range(2):
            pv, tp, n = panel("w2", i)
            for j in range(4):
                ch = 4 * i + j
                b = bank()
                for k in range(8):
                    tk = MM(PS[b][:, :], pv[:, k, j * 128:(j + 1) * 128], x3[:, k, 0:TX], tp,
                            *(bankfree[b] if k == 0 else []), start=(k == 0), stop=(k == 7))
                u = ub[:, ch % 2, :]
                cw = [col("convw", 4 * ch + w, 4 * ch + w + 1) for w in range(4)]
                cp = S(lambda e, u=u, b=b: e.activation(u[:, 3:515], PS[b][:, :], ACT.Copy), tk, qv.tok())
                bankfree[b] = [cp]
                V(lambda e, u=u, cw=cw: e.tensor_scalar(cy, u[:, 0:512], cw[0], None, ALU.mult), cp, cyfree or cp)
                for w in (1, 2, 3):
                    v = V(lambda e, u=u, cw=cw, w=w: e.scalar_tensor_tensor(out=cy, in0=u[:, w:w + 512], scalar=cw[w], in1=cy,
                                                                        op0=ALU.mult, op1=ALU.add))
                a = S(lambda e, ch=ch: e.activation(qk[:, ch, :], cy, ACT.Silu, bias=col("convb", ch, ch + 1)), v)
                cyfree = a
            release(n, tk)
        for i, dst in ((2, dq), (3, dk)):
            pv, tp, n = panel("w2", i)
            for a in range(4):
                tk, v = projT(pv, 128 * a, 128, tp, [(0, TX, dst[:, a, :])])
            release(n, tk)
        pv, tp, n = panel("w2", 4)
        for t in range(NT):
            b = bank()
            for k in range(8):
                tk = MM(PS[b][:, :], x3[:, k, t * 128:(t + 1) * 128], pv[:, k, :], tp, *(bankfree[b] if k == 0 else []),
                        start=(k == 0), stop=(k == 7))
            v = V(lambda e, t=t, b=b: e.tensor_copy(mv[:, t, :, 0:128], PS[b][:, :].rearrange("p (h c) -> p h c", h=4)), tk)
            bankfree[b] = [v]
        release(n, tk)
        pv, tp, n = panel("w2", 5)
        tk, v = projR(pv, 0, 512, tp, [(t * 128, t * 128 + 128, dv[:, t, :]) for t in range(NT)])
        release(n, tk)
        pv, tp, n = panel("w2", 6)
        tk, v = projR(pv, 0, 512, tp, [(t * 128, t * 128 + 128, mo[:, t, :]) for t in range(NT)], fn=ACT.Sigmoid)
        release(n, tk)
        mng = row("mng").rearrange("p (o c) -> p o c", o=1).to_broadcast([128, 4, 512])
        V(lambda e: e.tensor_tensor(mo, mo, mng, ALU.mult), v)
        wig = col("wig").rearrange("p (k c) -> p k c", k=8)
        gb = []
        for i in range(2):
            b = bank()
            for k in range(8):
                tk = MM(PS[b][0:4, :], wig[:, k, 4 * i:4 * i + 4], x3[:, k, 0:TX], *(bankfree[b] if k == 0 else []),
                        start=(k == 0), stop=(k == 7))
            gb.append(b)
        fence()

        ig, lf, bb, MM_, tmp = (xT[0:4, i * 512:(i + 1) * 512] for i in range(5))
        V(lambda e: e.tensor_scalar(ig, PS[gb[0]][0:4, :], cols[0:4, COFF["gbi"][0]:COFF["gbi"][0] + 1], None, ALU.add), tk)
        v = V(lambda e: e.tensor_scalar(lf, PS[gb[1]][0:4, :], cols[0:4, COFF["gbf"][0]:COFF["gbf"][0] + 1], None, ALU.add))
        S(lambda e: e.activation(tmp, lf, ACT.Abs), v)
        S(lambda e: e.activation(tmp, tmp, ACT.Exp, scale=-1.0))
        a = S(lambda e: e.activation(tmp, tmp, ACT.Ln, bias=1.0))
        V(lambda e: e.scalar_tensor_tensor(out=lf, in0=lf, scalar=0.0, in1=tmp, op0=ALU.min, op1=ALU.subtract), a)
        onesrow = xT[0:4, 5 * 512:6 * 512]
        V(lambda e: e.memset(onesrow, 1.0))
        V(lambda e: e.tensor_tensor_scan(bb, onesrow, lf, 0.0, ALU.mult, ALU.add))
        V(lambda e: e.tensor_tensor(ig, ig, bb, ALU.subtract))
        V(lambda e: e.tensor_tensor_scan(MM_, ig, ig, 0.0, ALU.max, ALU.max))
        V(lambda e: e.tensor_tensor(bb, bb, MM_, ALU.add))
        V(lambda e: e.tensor_scalar(bb, bb, -1.0, None, ALU.mult))
        v = V(lambda e: e.tensor_scalar(MM_, MM_, -1.0, None, ALU.mult))
        ac, emc = sm[:, 128:144], sm[:, 144:160]
        for t in range(NT):
            TR(PS[0][:, 4 * t:4 * t + 4], ig[:, t * 128:(t + 1) * 128], v, mark=False)
            tk = TR(PS[0][:, 16 + 4 * t:20 + 4 * t], bb[:, t * 128:(t + 1) * 128])
        v = V(lambda e: e.tensor_copy(ac, PS[0][:, 0:16]), tk)
        a = S(lambda e: e.activation(emc, PS[0][:, 16:32], ACT.Exp), v)
        Wt = big[:, 0:2048].rearrange("p (j c) -> p j c", j=4)
        Dt = big[:, 2048:2560]
        dn = sm[:, 160:164]
        sel = cols[0:4, COFF["sel"][0]:COFF["sel"][0] + 512]
        for b in range(8):
            bankfree[b] = [v, a]
        num_t = None
        for h in range(4):
            tmb = MM(PS[1][:, :], sel[:, h * 128:(h + 1) * 128], MM_, *bankfree[1])
            for j in range(NT):
                w = TX - j * 128
                b = 2 + j % 2
                tk = MM(PS[b][:, 0:w], qk[:, 4 + h, j * 128:(j + 1) * 128], qk[:, h, j * 128:TX], *bankfree[b])
                V(lambda e, j=j, w=w, h=h: e.tensor_scalar(Dt[:, 0:w], PS[1][:, j * 128:TX], ac[:, 4 * j + h:4 * j + h + 1], 0.0,
                                                           ALU.add, ALU.min), tmb, qs.tok())
                a = S(lambda e, w=w: e.activation(Dt[:, 0:w], Dt[:, 0:w], ACT.Exp), qv.tok())
                V(lambda e: e.tensor_tensor(Dt[:, 0:128], Dt[:, 0:128], col("caus"), ALU.mult), a)
                v = V(lambda e, j=j, w=w, b=b: e.scalar_tensor_tensor(
                    out=Wt[:, j, j * 128:TX], in0=PS[b][:, 0:w], scalar=128.0 ** -0.5, in1=Dt[:, 0:w], op0=ALU.mult,
                    op1=ALU.mult), tk, num_t or tk)
                bankfree[b] = [v]
            bankfree[1] = [v]
            for t in range(NT):
                b = 4 + t
                for j in range(t + 1):
                    tk = MM(PS[b][:, 0:129], Wt[:, j, t * 128:(t + 1) * 128], mv[:, j, h, :], v, *bankfree[b],
                            start=(j == 0), stop=(j == t))
                V(lambda e, b=b, t=t, h=h: e.tensor_tensor(dn[:, t:t + 1], PS[b][:, 128:129], emc[:, 4 * t + h:4 * t + h + 1],
                                                           ALU.max), tk)
                V(lambda e, b=b, t=t: e.scalar_tensor_tensor(out=dn[:, t:t + 1], in0=PS[b][:, 128:129], scalar=-1.0,
                                                             in1=dn[:, t:t + 1], op0=ALU.mult, op1=ALU.max))
                V(lambda e, t=t: e.reciprocal(dn[:, t:t + 1], dn[:, t:t + 1]))
                vv = V(lambda e, b=b, t=t, h=h: e.tensor_scalar(ho3[:, t, h * 128:(h + 1) * 128], PS[b][:, 0:128],
                                                                dn[:, t:t + 1], None, ALU.mult))
                bankfree[b] = [vv]
            num_t = tk
        fence()

        def head_norm(o3, gate, eps, base, banks):
            s4, r4 = sm[:, 176:192], sm[:, 192:208]
            sqb = qk[:, 0:4, :].rearrange("p a c -> p (a c)")
            a = S(lambda e: e.activation(sqb, o3.rearrange("p t c -> p (t c)"), ACT.Square), qv.tok())
            V(lambda e: e.tensor_reduce(s4, sqb.rearrange("p (n c) -> p n c", c=128), AX, ALU.add), a)
            for i in range(4):
                r = rstd(r4[:, 4 * i:4 * i + 4], s4[:, 4 * i:4 * i + 4], 128.0, eps)
            ov = o3.rearrange("p t (h c) -> p (t h) c", h=4)
            V(lambda e: e.tensor_tensor(ov, ov, r4.rearrange("p (n o) -> p n o", o=1).to_broadcast([128, 16, 128]), ALU.mult), r)
            v = V(lambda e: e.tensor_tensor(ov, ov, gate, ALU.mult))
            for t in range(NT):
                b = banks[t]
                for h in range(4):
                    tk = TR(PS[b][:, h * 128:(h + 1) * 128], o3[:, t, h * 128:(h + 1) * 128], v, mark=(h == 3))
                S(lambda e, b=b, t=t: e.activation(mixT[:, base:base + 4, t * 128:(t + 1) * 128],
                                                   PS[b][:, :].rearrange("p (h c) -> p h c", h=4), ACT.Copy), tk)

        head_norm(ho3, mo.rearrange("p t (h c) -> p (t h) c", h=4), 1e-6, 0, (0, 1, 2, 3))
        fence()

        lt = sm[:, 208:272]
        ls = sm[:, 272:276]
        V(lambda e: e.tensor_tensor_reduce(out=lt, in0=row("lq1"), in1=row("lk1"), scale=1.0, scalar=0.0, op0=ALU.mult,
                                           op1=ALU.add, accum_out=ls[:, 0:1]))
        v = V(lambda e: e.tensor_tensor_reduce(out=lt, in0=row("lq2"), in1=row("lk2"), scale=1.0, scalar=0.0, op0=ALU.mult,
                                               op1=ALU.add, accum_out=ls[:, 1:2]))
        a = S(lambda e: e.activation(ls[:, 0:2], ls[:, 0:2], ACT.Exp), v)
        V(lambda e: e.tensor_tensor(ls[:, 2:3], ls[:, 1:2], ls[:, 0:1], ALU.subtract), a)
        V(lambda e: e.tensor_scalar(ls[:, 2:3], ls[:, 2:3], -0.2, None, ALU.add))
        for b in range(8):
            bankfree[b] = []
        P = [xT[:, i * 512:(i + 1) * 512] for i in range(4)]
        aTt = [xT[:, 2048 + i * 512:2560 + i * 512].rearrange("p (j c) -> p j c", j=4) for i in range(2)]
        sc = sm[:, 276:300]
        cnt = 0
        pf = [[], []]
        atf = [[], []]
        for t in range(NT):
            n = (t + 1) * 128
            for h in range(4):
                i2 = cnt % 2
                cnt += 1
                so = sc[:, 12 * i2:12 * i2 + 12]
                P0, P1 = P[2 * i2], P[2 * i2 + 1]
                for p in range(2):
                    b = 2 * i2 + p
                    tk = MM(PS[b][:, 0:n], dq[64 * p:64 * p + 64, h, t * 128:(t + 1) * 128], dk[64 * p:64 * p + 64, h, 0:n],
                            *bankfree[b])
                    V(lambda e, b=b, n=n: e.tensor_tensor(PS[b][:, n - 128:n], PS[b][:, n - 128:n], col("negm"), ALU.add), tk)
                    V(lambda e, b=b, n=n, p=p, so=so: e.tensor_reduce(so[:, p:p + 1], PS[b][:, 0:n], AX, ALU.max))
                    v = V(lambda e, p=p, so=so: e.tensor_scalar(so[:, 2 + p:3 + p], so[:, p:p + 1], -0.125, None, ALU.mult))
                    a = S(lambda e, b=b, n=n, p=p, so=so, Pp=P[2 * i2 + p]: e.activation(
                        Pp[:, 0:n], PS[b][:, 0:n], ACT.Exp, bias=so[:, 2 + p:3 + p], scale=0.125,
                        accum_out=so[:, 4 + p:5 + p]), v, *pf[i2])
                    bankfree[b] = [a]
                V(lambda e, so=so: e.reciprocal(so[:, 6:8], so[:, 4:6]), a)
                V(lambda e, so=so: e.tensor_tensor(so[:, 7:8], so[:, 7:8], ls[:, 2:3], ALU.mult))
                V(lambda e, so=so, P1=P1, n=n: e.tensor_scalar(P1[:, 0:n], P1[:, 0:n], so[:, 7:8], None, ALU.mult))
                v = V(lambda e, so=so, P0=P0, P1=P1, n=n: e.scalar_tensor_tensor(
                    out=P0[:, 0:n], in0=P0[:, 0:n], scalar=so[:, 6:7], in1=P1[:, 0:n], op0=ALU.mult, op1=ALU.add))
                b = 4 + i2
                for j in range(t + 1):
                    tk = TR(PS[b][:, j * 128:(j + 1) * 128], P0[:, j * 128:(j + 1) * 128], v, *bankfree[b], mark=(j == t))
                pf[i2] = [tk]
                at = aTt[i2]
                cp = S(lambda e, b=b, at=at, n=n: e.activation(at.rearrange("p j c -> p (j c)")[:, 0:n], PS[b][:, 0:n], ACT.Copy),
                       tk, *atf[i2])
                bankfree[b] = [cp]
                ob = 6 + t % 2
                for j in range(t + 1):
                    tk = MM(PS[ob][:, h * 128:(h + 1) * 128], at[:, j, :], dv[:, j, h * 128:(h + 1) * 128], cp, *bankfree[ob],
                            start=(j == 0), stop=(j == t))
                atf[i2] = [tk]
            v = V(lambda e, ob=ob, t=t: e.tensor_copy(ho3[:, t, :], PS[ob][:, :]), tk)
            bankfree[ob] = [v]
        fence()
        dg8 = sm[:, 300:428]
        V(lambda e: e.tensor_scalar(dg8, row("dng"), 0.8, None, ALU.mult))
        head_norm(ho3, dg8.rearrange("p (o c) -> p o c", o=1).to_broadcast([128, 16, 128]), 1e-6, 4, (0, 1, 2, 3))
        fence()

        for b in range(8):
            bankfree[b] = []
        out_proj("wo2", g1b)
        fence()
        h2 = big[:, 0:4096].rearrange("p (t d) -> p t d", t=NT)
        r = row_norm(1e-6, big[:, 8192:9216])
        t_src = []
        for t in range(NT):
            V(lambda e, t=t: e.scalar_tensor_tensor(out=h2[:, t, :], in0=h3[:, t, :], scalar=sm[:, 8 + t:9 + t], in1=A2b,
                                                    op0=ALU.mult, op1=ALU.mult), r)
            t_src.append(V(lambda e, t=t: e.tensor_tensor(h2[:, t, :], h2[:, t, :], B2b, ALU.add)))
        for b in range(8):
            bankfree[b] = []
        for k in range(8):
            b = k % 4
            for t in range(NT):
                tk = TR(PS[b][:, t * 128:(t + 1) * 128], h2[:, t, k * 128:(k + 1) * 128], t_src[t], *bankfree[b],
                        mark=(t == NT - 1))
            v = S(lambda e, b=b, k=k: e.activation(x3[:, k, 0:TX], PS[b][:, :], ACT.Copy), tk)
            bankfree[b] = [v]
        fence()
        off[0] = 4096
        qT = carve(8192).rearrange("p (a c) -> p a c", a=16)
        for b in range(8):
            bankfree[b] = []
        for i in range(4):
            pv, tp, n = panel("wq", i)
            for a in range(4):
                tk, v = projT(pv, 128 * a, 128, tp, [(0, TX, qT[:, 4 * i + a, :])])
            release(n, tk)
        sk = carve(2048).rearrange("p (a c) -> p a c", a=16)
        t_sk = LOAD(qd, sk, skT, s_sk)
        tf = fence()
        for b in range(8):
            bankfree[b] = []
        sS = carve(2048).rearrange("p (a c) -> p a c", a=16)
        cand = ring[:, 8192:10240]
        oh = ring[:, 10240:12288]
        svv = carve(256).rearrange("p (a k) -> p a k", a=16)
        siv = carve(256).bitcast(U32).rearrange("p (a k) -> p a k", a=16)
        sif = carve(256).rearrange("p (a k) -> p a k", a=16)
        fv = carve(128).rearrange("p (h k) -> p h k", h=8)
        fpo = carve(128).bitcast(U32).rearrange("p (h k) -> p h k", h=8)
        fhi = carve(128).bitcast(U32)
        fhf = carve(128)
        es0 = carve(128)
        es1 = carve(128)
        gw = carve(256).rearrange("p (i k) -> p i k", i=2)
        eid = carve(256).bitcast(U32).rearrange("p (i k) -> p i k", i=2)
        act = carve(256).rearrange("p (i k) -> p i k", i=2)
        w_ = carve(256).rearrange("p (i k) -> p i k", i=2)
        eidf = carve(128)
        w32 = xT[:, 0:4128]
        eidT = carve(128).bitcast(U32)
        yT = cand[:, 0:1024]
        jk2 = carve(1024)
        gs = ring[:, 0:NG * 1024].rearrange("p (i d) -> p i d", i=NG)
        s_g = [sem(f"s_g{i}") for i in range(NG)]
        iota = col("iota")
        gi = {"n": 0}
        gfree = [list(tf) for _ in range(NG)]

        def gather(tab, idx, tok):
            i = gi["n"] % NG
            gi["n"] += 1
            qg.add(lambda e, i=i, idx=idx: e.indirect_dma_start(
                gs[:, i, :], None, tab, bass.IndirectOffsetOnAxis(ap=idx, axis=0)), [tok, *gfree[i]], sem=s_g[i], inc=16)
            dma_n[s_g[i].name] = dma_n.get(s_g[i].name, 0) + 16
            return i, (s_g[i], dma_n[s_g[i].name])

        def topk(t):
            e2 = t % 2
            for q in range(4):
                b = q % 2 + 4
                for a in range(4):
                    tk = MM(PS[b][:, a * 128:(a + 1) * 128], qT[:, 4 * q + a, t * 128:(t + 1) * 128], sk[:, 4 * q + a, :], t_sk,
                            *bankfree[b])
                v = S(lambda e, q=q, b=b: e.activation(sS[:, 4 * q:4 * q + 4, :], PS[b][:, :].rearrange("p (a c) -> p a c", a=4),
                                                       ACT.Copy), tk, qv.tok())
                bankfree[b] = [v]

            def top16(vals, src, idx, *after):
                V(lambda e: e.max(vals[:, 0:8], src), *after)
                V(lambda e: e.max_index(idx[:, 0:8], vals[:, 0:8], src))
                V(lambda e: e.match_replace(src, vals[:, 0:8], src, -3.0e38))
                V(lambda e: e.max(vals[:, 8:16], src))
                V(lambda e: e.max_index(idx[:, 8:16], vals[:, 8:16], src))

            for a in range(16):
                top16(svv[:, a, :], sS[:, a, :], siv[:, a, :], v)
            V(lambda e: e.tensor_copy(sif, siv))
            s4 = svv.rearrange("p (h t) k -> p h t k", t=2)
            c4 = cand.rearrange("p (h i j) -> p h i j", h=8, i=16)
            V(lambda e: e.tensor_tensor(
                c4, s4[:, :, 0, :].rearrange("p h (k o) -> p h k o", o=1).to_broadcast([128, 8, 16, 16]),
                s4[:, :, 1, :].rearrange("p h (o k) -> p h o k", o=1).to_broadcast([128, 8, 16, 16]), ALU.add))
            for h in range(8):
                top16(fv[:, h, :], cand[:, h * 256:(h + 1) * 256], fpo[:, h, :])
            fpf = fpo.rearrange("p h k -> p (h k)")
            i4 = sif.rearrange("p (h t) k -> p h t k", t=2)
            for part, es in ((0, es0), (1, es1)):
                V(lambda e, part=part: e.tensor_scalar(fhi, fpf, 4 if part == 0 else 15, None,
                                                       ALU.logical_shift_right if part == 0 else ALU.bitwise_and))
                V(lambda e: e.tensor_copy(fhf, fhi))
                o3_ = oh.rearrange("p (n i) -> p n i", i=16)
                V(lambda e, o3_=o3_: e.tensor_tensor(
                    o3_, fhf.rearrange("p (n o) -> p n o", o=1).to_broadcast([128, 128, 16]),
                    iota.rearrange("p (o i) -> p o i", o=1).to_broadcast([128, 128, 16]), ALU.is_equal))
                o4_ = oh.rearrange("p (h k i) -> p h k i", h=8, k=16)
                V(lambda e, o4_=o4_, part=part: e.tensor_tensor(
                    o4_, o4_, i4[:, :, part, :].rearrange("p h (o k) -> p h o k", o=1).to_broadcast([128, 8, 16, 16]), ALU.mult))
                V(lambda e, o3_=o3_, es=es: e.tensor_reduce(es, o3_, AX, ALU.add))
            V(lambda e: e.scalar_tensor_tensor(out=eidf, in0=es0, scalar=128.0, in1=es1, op0=ALU.mult, op1=ALU.add))
            ve = V(lambda e, e2=e2: e.tensor_copy(eid[:, e2, :], eidf), ufree[e2])
            V(lambda e: e.tensor_copy(sm[:, 128:136], fv[:, :, 0]))
            gv_ = gw[:, e2, :].rearrange("p (h k) -> p h k", h=8)
            v = V(lambda e, gv_=gv_: e.tensor_tensor(
                gv_, fv, sm[:, 128:136].rearrange("p (h o) -> p h o", o=1).to_broadcast([128, 8, 16]), ALU.subtract))
            a = S(lambda e, e2=e2: e.activation(gw[:, e2, :], gw[:, e2, :], ACT.Exp), v)
            V(lambda e, gv_=gv_: e.tensor_reduce(sm[:, 136:144], gv_, AX, ALU.add), a)
            V(lambda e: e.reciprocal(sm[:, 136:144], sm[:, 136:144]))
            V(lambda e, gv_=gv_: e.tensor_tensor(
                gv_, gv_, sm[:, 136:144].rearrange("p (h o) -> p h o", o=1).to_broadcast([128, 8, 16]), ALU.mult))
            return ve

        def turn_ids(ve, *after):
            tk = TR(PS[6][:, 0:128], eidf, ve, *bankfree[6])
            v = V(lambda e: e.tensor_copy(eidT, PS[6][:, 0:128]), tk, *after)
            bankfree[6] = [v]
            return v

        V(lambda e: e.memset(w32[:, :], 0.0))
        ufree = [tf[0], tf[0]]
        ve = topk(0)
        vt = turn_ids(ve)
        yfree, vgl = [], None
        for t in range(NT):
            e2 = t % 2
            for k in range(128):
                i, tok = gather(utab, eid[:, e2, k:k + 1], ve)
                v = V(lambda e, i=i, k=k, t=t, e2=e2: e.tensor_tensor_reduce(
                    out=jk2, in0=gs[:, i, :], in1=h2[:, t, :], scale=1.0, scalar=0.0, op0=ALU.mult, op1=ALU.add,
                    accum_out=act[:, e2, k:k + 1]), tok)
                gfree[i] = [v]
            ufree[e2] = v
            a = S(lambda e, e2=e2: e.activation(w_[:, e2, :], act[:, e2, :], ACT.Gelu), v)
            v = V(lambda e, e2=e2: e.tensor_tensor(w_[:, e2, :], w_[:, e2, :], gw[:, e2, :], ALU.mult), a)
            tk = TR(PS[7][:, 0:128], w_[:, e2, :], v, *bankfree[7])
            vw = V(lambda e: e.tensor_copy(w32[:, 32:].rearrange("p (t c) -> p t c", c=32)[:, :, 0], PS[7][:, 0:128]), tk)
            bankfree[7] = [vw]
            if t + 1 < NT:
                ve = topk(t + 1)
            for m in range(32):
                gg = [gather(vtab, eidT[:, 32 * j + m:32 * j + m + 1], vt) for j in range(4)]
                for hf in range(2):
                    for j in range(4):
                        i, tok = gg[j]
                        c0 = 32 + 32 * (32 * j + m) - m
                        tk = MM(PS[hf][32 * j:32 * j + 32, :], w32[:, c0:c0 + 32], gs[:, i, hf * 512:(hf + 1) * 512],
                                vw, tok, *yfree, start=(m == 0), stop=(m == 31), mark=True)
                        gfree[i] = [tk]
            if t + 1 < NT:
                vt = turn_ids(ve)
            for hf in range(2):
                v = V(lambda e, hf=hf: e.tensor_tensor(yT[:, hf * 512:(hf + 1) * 512], PS[hf][:, :],
                                                       g2b[:, hf * 512:(hf + 1) * 512], ALU.mult), tk)
            yfree = [v]
            V(lambda e, t=t: e.tensor_tensor(h3[:, t, :], h3[:, t, :], yT, ALU.add))
            a = sumsq(sm[:, 0:1], h3[:, t, :], oh[:, 0:1024], qv.tok())
            r = rstd(sm[:, 8:9], sm[:, 0:1], 1024.0, 1e-6, a)
            v = V(lambda e, t=t: e.scalar_tensor_tensor(out=h3[:, t, :], in0=h3[:, t, :], scalar=sm[:, 8:9], in1=row("fg"),
                                                        op0=ALU.mult, op1=ALU.mult), r)
            t_o = LOAD(qd, out[t * 128:(t + 1) * 128, :], h3[:, t, :], s_out, v)
        qd.items.append((qd.need([t_o]), None, None, 0))

        block = ctx.enter_context(nc.Block())

        @block.sync
        def _(e):
            qd.run(e)

        @block.scalar
        def _(e):
            qs.run(e)

        @block.gpsimd
        def _(e):
            qg.run(e)

        @block.vector
        def _(e):
            qv.run(e)

        @block.tensor
        def _(e):
            qp.run(e)


def shape_constants():
    c = {}
    c["ident"] = np.eye(128)
    inv = np.float32(1.0) / np.float32(500000.0) ** (np.arange(0, 16, 2, dtype=np.float32) / np.float32(16))
    pos = np.concatenate([np.arange(NM, NM + TX), np.arange(NM)]).astype(np.float32)
    ang = (pos[None, :] * inv.astype(np.float32)[:, None]).astype(np.float32)
    cos = np.ones((64, TA), np.float32)
    sin = np.zeros((64, TA), np.float32)
    cos[0:8] = cos[8:16] = np.cos(ang)
    sin[0:8] = sin[8:16] = np.sin(ang)
    c["cos"], c["sin"] = np.tile(cos, (2, 1)), np.tile(sin, (2, 1))
    rot = np.zeros((128, 128), np.float32)
    for b in (0, 64):
        for m in range(8):
            rot[b + m + 8, b + m] = -1.0
            rot[b + m, b + m + 8] = 1.0
    c["rot"] = rot
    j, i = np.arange(128)[:, None], np.arange(128)[None, :]
    ms = [(j == i)]
    for s in LEVELS:
        ms.append((j // (2 * s) == i // (2 * s)) & (j % (2 * s) < s) & (i % (2 * s) >= s))
    c["masks"] = np.concatenate(ms, axis=1).astype(np.float32)
    r, k = np.arange(128)[:, None], np.arange(256)[None, :]
    dist = 128 + r - k
    w = np.zeros((128, 272), np.float32)
    w[:, 0:256] = np.where((dist >= 0) & (dist < 128), 0.0, BIGNEG)
    c["wmask"] = w
    c["negm"] = np.where(i <= j, 0.0, BIGNEG)
    c["caus"] = (j <= i).astype(np.float32)
    rs = np.ones((128, TA), np.float32)
    rs[:, [0, 128, 256, 384, 512]] = 0.0
    c["reset"] = rs
    c["iota"] = np.tile(np.arange(16, dtype=np.float32), (128, 1))
    sel = np.zeros((128, 4, 128), np.float32)
    for h in range(4):
        sel[h, h, :] = 1.0
    c["sel"] = sel.reshape(128, 512)
    c["mhalf"] = np.full((128, 4), -0.5)
    return c


def colv(v):
    return np.asarray(v).reshape(-1, 128).T


def panelize(w):
    k, n = w.shape
    return np.ascontiguousarray(w.reshape(8, 128, n).transpose(1, 0, 2).reshape(128, 8 * n))


def kernel(x, meta_tokens, norm_mix_w, w_in, w_gate_up, b_gate, gla_norm_w, sinks, w_out, norm_ff_w, w_ff1, w_ff2,
           final_norm_w, c_2, ada_w_2, ada_b_2, norm1_g_2, w_in_2, conv_w_2, conv_b_2, mlstm_gate_b_2, mlstm_norm_g_2,
           lambda_q1_2, lambda_k1_2, lambda_q2_2, lambda_k2_2, diff_norm_g_2, w_out_2, norm2_g_2, peer_w_query_2,
           peer_sub_keys_2, peer_u_2, peer_v_2, final_g_2):
    import concourse.bacc as bacc
    from concourse.bass_utils import run_bass_kernel_spmd

    A = np.asarray
    f = np.float32
    c = shape_constants()
    c.update(mixw=colv(A(norm_mix_w)[0]), ffw=colv(A(norm_ff_w)[0]), n1g=colv(A(norm1_g_2)[0]), n2g=colv(A(norm2_g_2)[0]),
             bgate=colv(A(b_gate)[0]), adab=colv(A(ada_b_2)[0]), ccol=colv(A(c_2)[0]))
    cw = A(conv_w_2)[0]
    c["convw"] = cw.reshape(4, 8, 128).transpose(2, 1, 0).reshape(128, 32)
    c["convb"] = colv(A(conv_b_2)[0])
    w2 = A(w_in_2)[0]
    c["wig"] = w2[:, 2048:2056].reshape(8, 128, 8).transpose(1, 0, 2).reshape(128, 64)
    pack = np.zeros((128, NCOL), f)
    for name, w in COLS:
        o = COFF[name][0]
        if name in c:
            pack[:, o:o + w] = c[name]
    gbv = A(mlstm_gate_b_2)[0]
    pack[0:4, COFF["gbi"][0]] = gbv[0:4]
    pack[0:4, COFF["gbf"][0]] = gbv[4:8]
    pack[0:16, COFF["wgu"][0]:COFF["wgu"][0] + 256] = A(w_gate_up)[0]
    rows = np.concatenate([A(final_norm_w), A(final_g_2), A(gla_norm_w)[0], A(mlstm_norm_g_2)[0], A(diff_norm_g_2)[0],
                           A(sinks)[0], A(lambda_q1_2)[0], A(lambda_k1_2)[0], A(lambda_q2_2)[0],
                           A(lambda_k2_2)[0]]).reshape(1, NROW)
    w1 = A(w_in)[0]
    gq, gk, gv_, gr_, glr, sq, sk_, sv_ = np.split(w1, np.cumsum([256, 256, 512, 512, 16, 512, 128]), axis=1)
    sqh = sq.reshape(1024, 8, 64)
    sqp = np.concatenate([sqh[:, [j, j + 4]].reshape(1024, 128) for j in range(4)], axis=1)
    wo = A(w_out)[0]
    woh = wo[512:].reshape(8, 64, 1024)
    wop = np.concatenate([wo[0:512]] + [woh[[j, j + 4]].reshape(128, 1024) for j in range(4)], axis=0)
    ff1, ff2, ada, wo2, wq = A(w_ff1)[0], A(w_ff2)[0], A(ada_w_2)[0], A(w_out_2)[0], A(peer_w_query_2)[0]
    cut = lambda w: [w[:, i:i + 512] for i in range(0, w.shape[1], 512)]
    P = {
        "w1": [np.concatenate([gq, gk], 1), sqp, gv_, gr_, np.concatenate([sk_, sv_, glr], 1)],
        "wo1": cut(wop),
        "ff1": cut(ff1),
        "ff2": [ff2[q * 1024:(q + 1) * 1024, h * 512:(h + 1) * 512] for h in range(2) for q in range(4)],
        "ada": cut(ada),
        "w2": [w2[:, 0:512], w2[:, 512:1024], w2[:, 2056:2568], w2[:, 2568:3080], w2[:, 1024:1536], w2[:, 3080:3592],
               w2[:, 1536:2048]],
        "wo2": cut(wo2),
        "wq": cut(wq),
    }
    skt = A(peer_sub_keys_2)[0].reshape(16, 128, 128).transpose(2, 0, 1).reshape(128, 2048)
    arrays = {"packs": pack, "rows": rows, "x": A(x)[0], "meta": A(meta_tokens), "skt": skt, "utab": A(peer_u_2)[0],
              "vtab": A(peer_v_2)[0]}
    for name, ws in P.items():
        for i, w in enumerate(ws):
            arrays[f"{name}_{i}"] = panelize(w)
    arrays = {k: np.ascontiguousarray(v) for k, v in arrays.items()}

    nc = bacc.Bacc("TRN2", target_bir_lowering=False, num_devices=1)
    ap = {k: nc.dram_tensor(k, v.shape, F32, kind="ExternalInput").ap() for k, v in arrays.items()}
    o = nc.dram_tensor("out0", (TX, 1024), F32, kind="ExternalOutput").ap()
    W = {name: [ap[f"{name}_{i}"] for i in range(len(ws))] for name, ws in P.items()}
    build(nc, ap["packs"], ap["rows"], ap["x"], ap["meta"], W, ap["skt"], ap["utab"], ap["vtab"], o)
    r = run_bass_kernel_spmd(nc, [arrays], core_ids=[0])
    return r.results[0]["out0"].reshape(1, TX, 1024)
```

```python
from contextlib import ExitStack

import numpy as np

import concourse.bass as bass
from concourse import mybir

F32 = mybir.dt.float32
U32 = mybir.dt.uint32
R32 = mybir.dt.float32r
ALU = mybir.AluOpType
ACT = mybir.ActivationFunctionType
AX = mybir.AxisListType.X

NT = 4
NM = 16
TX = 512
TA = TX + NM
LEVELS = (64, 32, 16, 8, 4, 2, 1)
BIGNEG = -1e30

COLS = [("ident", 128), ("mixw", 8), ("ffw", 8), ("n1g", 8), ("bgate", 2), ("adab", 48), ("ccol", 8),
        ("convw", 32), ("convb", 8), ("gbi", 1), ("gbf", 1), ("wgu", 256), ("cos", TA), ("sin", TA),
        ("rot", 128), ("masks", 8 * 128), ("wmask", 272), ("negm", 128), ("caus", 128), ("reset", TA),
        ("iota", 16), ("sel", 512), ("mhalf", 4)]
COFF = {}
_o = 0
for _n, _w in COLS:
    COFF[_n] = (_o, _w)
    _o += _w
NCOL = _o
ROWS = [("fw", 1024), ("fg", 1024), ("gnw", 128), ("mng", 512), ("dng", 128), ("sink", 8),
        ("lq1", 64), ("lk1", 64), ("lq2", 64), ("lk2", 64)]
ROFF = {}
_o = 0
for _n, _w in ROWS:
    ROFF[_n] = (_o, _w)
    _o += _w
NROW = _o

BIG1 = 19016
BIG4 = 20320
OVER = 2 * 4096 + 2 * (8 * TA + 112)
BIG2 = 16968
NP_RING = 2
CW = 256
NG = 8


class Queue:

    def __init__(self, sem):
        self.sem, self.n, self.items, self.seen = sem, 0, [], {}

    def need(self, toks):
        waits = []
        for sem, val in toks:
            if self.seen.get(sem.name, 0) < val:
                self.seen[sem.name] = val
                waits.append((sem, val))
        return waits

    def tok(self):
        return (self.sem, self.n)

    def add(self, fn, after, mark=True, sem=None, inc=1):
        waits = self.need(after)
        if sem is None and mark:
            self.n += 1
            sem = self.sem
        self.items.append((waits, fn, sem, inc))
        return (sem, self.n) if inc == 1 else None

    def run(self, eng):
        for waits, fn, sem, inc in self.items:
            for s, v in waits:
                eng.wait_ge(s, v)
            if fn is None:
                continue
            ins = fn(eng)
            if sem is not None:
                ins.then_inc(sem, inc)


def build(nc, packs, rows, brows, x, meta, W, skT, utab, vtab, out):
    ctx = ExitStack()
    with ctx:
        def sb(name, n, dt=F32, p=128):
            return ctx.enter_context(nc.sbuf_tensor(name, [p, n], dt))

        def scope():
            return ctx.enter_context(ExitStack())

        def sbs(sc, name, n, dt=F32, side="left"):
            return sc.enter_context(nc.sbuf_tensor(name, [128, n], dt, side=side))

        raw = sb("raw", NP_RING * 8 * CW)
        hres = sb("hres", 4096)
        cols = sb("cols", NCOL)
        rowb = sb("rowb", NROW)
        mod = sb("mod", 16)
        small = sb("small", 640)
        NX = 8 * TA + 112

        def open_split(tag):
            sc = scope()
            wh, wl = sbs(sc, "wh" + tag, 4096, R32, "right"), sbs(sc, "wl" + tag, 4096, R32, "right")
            xh, xl = sbs(sc, "xh" + tag, NX, R32, "right"), sbs(sc, "xl" + tag, NX, R32, "right")
            state.update(wh=wh, wl=wl, wfree=[[], []])
            return sc, xh, xl

        state = {"wi": 0, "prep": 0, "ready": None}
        g1b = cols[:, COFF["cos"][0]:COFF["cos"][0] + 1024]
        A2b = cols[:, COFF["masks"][0]:COFF["masks"][0] + 1024]
        PS = [ctx.enter_context(nc.psum_tensor(f"ps{i}", [128, 512], F32)) for i in range(8)]

        def sem(name):
            return ctx.enter_context(nc.semaphore(name))

        qv, qs, qg, qp, qd = (Queue(sem("s_" + n)) for n in ("vec", "act", "pool", "pe", "sp"))

        def V(f, *after):
            return qv.add(f, [*after, qv.tok()])

        def S(f, *after):
            return qs.add(f, [*after, qs.tok()])

        def G(f, *after):
            return qg.add(f, [*after, qg.tok()])

        def MM(o, l, r, *after, start=True, stop=True, mark=None, share=False):
            return qp.add(lambda e: e.matmul(o, lhsT=l, rhs=r, start=start, stop=stop, skip_group_check=share),
                          after, mark=stop if mark is None else mark)

        def TR(o, i, *after, mark=True):
            k = i.shape[0]
            return qp.add(lambda e: e.transpose(o, i, ident[0:k, 0:k]), after, mark=mark)

        def fence():
            toks = [q.tok() for q in (qv, qs, qg, qp) if q.n]
            for q in (qv, qs, qg, qp):
                q.items.append((q.need([t for t in toks if t[0] is not q.sem]), None, None, 0))
            return toks

        def col(name, a=0, b=None):
            o, w = COFF[name]
            return cols[:, o + a:o + (w if b is None else b)]

        def row(name, a=0, b=None):
            o, w = ROFF[name]
            return rowb[:, o + a:o + (w if b is None else b)]

        ident = col("ident")
        dma_n = {}

        def LOAD(q, dst, src, s, *after, n=16):
            q.add(lambda e: e.dma_start(dst, src), after, sem=s, inc=16)
            dma_n[s.name] = dma_n.get(s.name, 0) + 16
            return (s, dma_n[s.name])

        s_x, s_c, s_r, s_sk, s_out = sem("s_x"), sem("s_c"), sem("s_r"), sem("s_sk"), sem("s_out")
        s_pan = [sem(f"s_pan{i}") for i in range(NP_RING)]
        h3 = hres[:, :].rearrange("p (t d) -> p t d", t=NT)
        splits, xh_, xl_ = open_split("a")
        sb1 = scope()
        big = sbs(sb1, "big1", BIG1)
        mrow = big[0:NM, 16384:16384 + 1024]
        t_c = LOAD(qs, cols[:, :], packs, s_c)
        LOAD(qd, h3, x.rearrange("(t p) d -> p t d", p=128), s_x)
        t_x = LOAD(qd, mrow, meta, s_x)
        t_r = LOAD(qs, rowb[:, :], rows.to_broadcast([128, NROW]), s_r)

        order = [("w1", i) for i in range(10)] + [("wo1", i) for i in range(4)]
        ffs = []
        for q in range(4):
            ffs += [("ff1", 4 * q + i) for i in range(4)] + [("ff2", 4 * q + i) for i in range(4)]
        for i, f in enumerate(ffs):
            order += ([("ada", i)] if i < 24 else []) + [f]
        order += [("w2", i) for i in range(15)] + [("wo2", i) for i in range(4)] + [("wq", i) for i in range(8)]
        loaded = {}

        def issue(n, *after):
            name, i = order[n]
            slot = n % NP_RING
            w = W[name][i].shape[1]
            loaded[n] = LOAD(qd, raw[:, slot * 2048:slot * 2048 + w], W[name][i], s_pan[slot], *after)

        for n in range(NP_RING):
            issue(n)

        def prep():
            while state["ready"] is None and state["prep"] < len(order):
                n = state["prep"]
                state["prep"] += 1
                name, i = order[n]
                w = W[name][i].shape[1]
                r = raw[:, (n % NP_RING) * 2048:(n % NP_RING) * 2048 + w]
                if name == "ada":
                    toks = [ada_acc(i, r.rearrange("p (k c) -> p k c", k=8), loaded[n])]
                else:
                    u = state["wi"] % 2
                    state["wi"] += 1
                    hi, lo = (state[x][:, u * 2048:u * 2048 + w] for x in ("wh", "wl"))
                    a = S(lambda e, hi=hi, r=r: e.activation(hi, r, ACT.Copy), loaded[n], *state["wfree"][u])
                    v = V(lambda e, hi=hi, lo=lo, r=r: e.tensor_tensor(lo, r, hi.bitcast(F32), ALU.subtract), a,
                          *state["wfree"][u])
                    toks = [a, v]
                    state["ready"] = (name, i, u, toks, hi.rearrange("p (k c) -> p k c", k=8),
                                      lo.rearrange("p (k c) -> p k c", k=8))
                if n + NP_RING < len(order):
                    issue(n + NP_RING, *toks)

        def panel(name, i, last=False):
            prep()
            nm, j, u, toks, hi, lo = state["ready"]
            assert (nm, j) == (name, i), (nm, j, name, i)
            state["ready"] = None
            if not last:
                prep()
            return (hi, lo), toks, u

        def release(u, tok):
            state["wfree"][u] = [tok]

        def MM3(o, parts, tp, *after):
            for k, ((lh, ll), (rh, rl)) in enumerate(parts):
                f = [*after] if k == 0 else []
                MM(o, lh, rh, *tp, *f, start=(k == 0), stop=False)
                MM(o, ll, rh, start=False, stop=False)
                tk = MM(o, lh, rl, start=False, stop=(k == len(parts) - 1))
            return tk

        sm = small
        mh = col("mhalf")

        def rstd(dst, ss, d, eps, *after):
            p, n = ss.shape[0], ss.shape[1]
            t = V(lambda e: e.tensor_scalar(ss, ss, 1.0 / d, eps, ALU.mult, ALU.add), *after)
            return G(lambda e: e.tensor_tensor(dst, ss, mh[0:p, 0:n], ALU.pow), t, t_c)

        def sumsq(dst, src, junk, *after):
            return S(lambda e: e.activation(junk, src, ACT.Square, accum_out=dst), *after)

        bankfree = [[] for _ in range(8)]

        def norm_T(src, scale, bias, banks, t_src, tmp):
            hold = [[], []]
            for k in range(8):
                b = banks[k % len(banks)]
                for t in range(NT):
                    tk = TR(PS[b][:, t * 128:(t + 1) * 128], src[:, t, k * 128:(k + 1) * 128], t_src[t], t_c,
                            *bankfree[b], mark=(t == NT - 1))
                h, l, q = xh3[:, k, 0:TX], xl3[:, k, 0:TX], tmp[:, (k % 2) * 512:(k % 2) * 512 + 512]
                if scale is None:
                    a = S(lambda e, h=h, b=b: e.activation(h, PS[b][:, :], ACT.Copy), tk)
                    v = V(lambda e, h=h, l=l, b=b: e.tensor_tensor(l, PS[b][:, :], h.bitcast(F32), ALU.subtract), a)
                    bankfree[b] = [v]
                    continue
                if bias is None:
                    v = V(lambda e, q=q, b=b, k=k: e.tensor_scalar(q, PS[b][:, :], scale[:, k:k + 1], None, ALU.mult), tk,
                          *hold[k % 2])
                else:
                    v = V(lambda e, q=q, b=b, k=k: e.tensor_scalar(q, PS[b][:, :], scale[:, k:k + 1], bias[:, k:k + 1],
                                                                   ALU.mult, ALU.add), tk, *hold[k % 2])
                bankfree[b] = [v]
                a = S(lambda e, h=h, q=q: e.activation(h, q, ACT.Copy), v)
                V(lambda e, h=h, l=l, q=q: e.tensor_tensor(l, q, h.bitcast(F32), ALU.subtract), a)
                hold[k % 2] = [a]

        xh3 = xh_[:, 0:8 * TA].rearrange("p (k c) -> p k c", k=8)
        xl3 = xl_[:, 0:8 * TA].rearrange("p (k c) -> p k c", k=8)

        xs3 = big[:, 8192:12288].rearrange("p (t d) -> p t d", t=NT)
        junk = big[:, 12288:13312]
        ssa = sm[:, 0:4]
        ssm = sm[0:NM, 4:5]
        for t in range(NT):
            a = sumsq(sm[:, t:t + 1], h3[:, t, :], junk, t_x)
        am = sumsq(ssm, mrow, junk[0:NM, :])
        r = rstd(sm[:, 8:12], ssa, 1024.0, 1e-5, am)
        rm = rstd(sm[0:NM, 12:13], ssm, 1024.0, 1e-5, am)
        t_src = [V(lambda e, t=t: e.tensor_scalar(xs3[:, t, :], h3[:, t, :], sm[:, 8 + t:9 + t], None, ALU.mult), r)
                 for t in range(NT)]
        tm = V(lambda e: e.tensor_scalar(mrow, mrow, sm[0:NM, 12:13], None, ALU.mult), rm)
        prep()
        norm_T(xs3, col("mixw"), None, [0, 1, 2], t_src, big[:, 13312:14336])
        for k in range(8):
            tk = TR(PS[3][:, k * NM:(k + 1) * NM], mrow[:, k * 128:(k + 1) * 128], tm, t_c)
        mw = col("mixw").rearrange("p (k o) -> p k o", o=1).to_broadcast([128, 8, NM])
        qm = big[:, 14336:14464].rearrange("p (k c) -> p k c", k=8)
        v = V(lambda e: e.tensor_tensor(qm, PS[3][:, 0:128].rearrange("p (k c) -> p k c", k=8), mw, ALU.mult), tk)
        zpad = big[:, 14464:14576]
        v = V(lambda e: e.memset(zpad, 0.0))
        hp, lp, hm, lm = xh_[:, 8 * TA:NX], xl_[:, 8 * TA:NX], xh3[:, :, TX:TA], xl3[:, :, TX:TA]
        S(lambda e: e.activation(hp, zpad, ACT.Copy), v)
        S(lambda e: e.activation(lp, zpad, ACT.Copy), v)
        a = S(lambda e: e.activation(hm, qm, ACT.Copy), v)
        V(lambda e: e.tensor_tensor(lm, qm, hm.bitcast(F32), ALU.subtract), a)
        fence()

        off, lim = [0], [BIG1]

        def carve(n, p=128):
            o = off[0]
            off[0] += n
            assert off[0] <= lim[0], off[0]
            return big[0:p, o:o + n]

        mixT = carve(4096).rearrange("p (k c) -> p k c", k=8)
        gqT = carve(1024).rearrange("p (a c) -> p a c", a=2)
        gkT = carve(1024).rearrange("p (a c) -> p a c", a=2)
        gkm = carve(32).rearrange("p (a c) -> p a c", a=2)
        lrT = carve(TA, 16)
        sqT = carve(2048).rearrange("p (a c) -> p a c", a=4)
        skT1 = carve(TA)
        gv = carve(2048).rearrange("p (t c) -> p t c", t=NT)
        gvm = carve(512, NM)
        gr = carve(2048).rearrange("p (t c) -> p t c", t=NT)
        sv = carve(512).rearrange("p (t c) -> p t c", t=NT)
        svm = carve(128, NM)
        mark1 = off[0]
        rr = {"i": 0}

        def bank(banks=tuple(range(8))):
            b = banks[rr["i"] % len(banks)]
            rr["i"] += 1
            return b

        def projT(pv, c, m, tp, outs, scale=None, rows=None):
            for (a, z, dst) in outs:
                b = bank()
                tk = MM3(PS[b][0:m, 0:z - a], [(tuple(w[:, k, c:c + m] for w in pv), (xh3[:, k, a:z], xl3[:, k, a:z]))
                                               for k in range(8)], tp, *bankfree[b])
                src = PS[b][0:rows or m, 0:z - a]
                if scale is None:
                    v = V(lambda e, dst=dst, src=src: e.tensor_copy(dst, src), tk)
                else:
                    v = V(lambda e, dst=dst, src=src: e.tensor_scalar(dst, src, scale, None, ALU.mult), tk)
                bankfree[b] = [v]
            return tk, v

        def xcol(x, k, a):
            return x[:, k * TA + a:k * TA + a + 128]

        def projR(pv, c, m, tp, outs, fn=None):
            for (a, z, dst) in outs:
                b = bank()
                tk = MM3(PS[b][:, 0:m], [((xcol(xh_, k, a), xcol(xl_, k, a)), tuple(w[:, k, c:c + m] for w in pv))
                                         for k in range(8)], tp, *bankfree[b])
                v = S(lambda e, dst=dst, src=PS[b][0:z, 0:m]: e.activation(dst, src, fn or ACT.Copy), tk)
                bankfree[b] = [v]
            return tk, v

        def rowsT(dst, c, n=CW):
            return [(t * 128, 128, dst[:, t, c:c + n]) for t in range(NT)]

        for b in range(8):
            bankfree[b] = []
        pv, tp, n = panel("w1", 0)
        for a in range(2):
            tk, v = projT(pv, 128 * a, 128, tp, [(0, TX, gqT[:, a, :])], scale=0.125)
        release(n, tk)
        pv, tp, n = panel("w1", 1)
        for a in range(2):
            tk, v = projT(pv, 128 * a, 128, tp, [(0, TX, gkT[:, a, :]), (TX, TA, gkm[:, a, :])])
        release(n, tk)
        for i in range(2):
            pv, tp, n = panel("w1", 2 + i)
            for a in range(2):
                tk, v = projT(pv, 128 * a, 128, tp, [(0, TX, sqT[:, 2 * i + a, :])])
            release(n, tk)
        for i in range(2):
            pv, tp, n = panel("w1", 4 + i)
            tk, v = projR(pv, 0, CW, tp, rowsT(gv, CW * i) + [(TX, NM, gvm[:, CW * i:CW * i + CW])])
            release(n, tk)
        for i in range(2):
            pv, tp, n = panel("w1", 6 + i)
            tk, v = projR(pv, 0, CW, tp, rowsT(gr, CW * i), fn=ACT.Silu)
            release(n, tk)
        vg = v
        pv, tp, n = panel("w1", 8)
        projT(pv, 0, 128, tp, [(0, TX, skT1[:, 0:TX]), (TX, TA, skT1[:, TX:TA])])
        tk, v = projR(pv, 128, 128, tp, rowsT(sv, 0, 128) + [(TX, NM, svm)])
        release(n, tk)
        pv, tp, n = panel("w1", 9, last=True)
        tk, v = projT(pv, 0, 128, tp, [(0, TX, lrT[:, 0:TX]), (TX, TA, lrT[:, TX:TA])], rows=16)
        release(n, tk)
        gnw = row("gnw").rearrange("p (o c) -> p o c", o=1).to_broadcast([128, 16, 128])
        grv = gr.rearrange("p t (h c) -> p (t h) c", h=4)
        V(lambda e: e.tensor_tensor(grv, grv, gnw, ALU.mult), vg, t_r)
        fence()
        splits.close()
        smix = scope()
        over = sbs(smix, "over1", OVER, F32, "right")
        xT = over[:, 0:8 * TA]
        ooff = [8 * TA]

        def carve_o(n, p=128):
            o = ooff[0]
            ooff[0] += n
            assert ooff[0] <= OVER
            return over[0:p, o:o + n]

        for b in range(8):
            bankfree[b] = []

        def beside(*gens):
            gens = list(gens)
            while gens:
                for g in list(gens):
                    try:
                        next(g)
                    except StopIteration:
                        gens.remove(g)

        zb = xT[:, 0:2 * TA].rearrange("p (a c) -> p a c", a=2)
        za = xT[:, 2 * TA:4 * TA].rearrange("p (a c) -> p a c", a=2)
        bx = carve_o(1024).rearrange("p (a c) -> p a c", a=2)
        bm = carve_o(32).rearrange("p (a c) -> p a c", a=2)
        Qs = carve_o(1024).rearrange("p (a c) -> p a c", a=2)
        Ks = carve_o(1024).rearrange("p (a c) -> p a c", a=2)
        Qs2 = carve_o(1024).rearrange("p (a c) -> p a c", a=2)
        A = carve_o(2048)
        khm = carve_o(256, NM)
        St = carve_o(2048).rearrange("p (c a v) -> p c a v", c=4, a=2)
        rc = [xT[:, 4 * TA:4 * TA + 528], xT[:, 4 * TA + 528:4 * TA + 1056]]

        def rope(xap, a, z, i):
            b = 4 + i % 4
            tk = MM(PS[b][:, 0:z - a], col("rot"), xap, *bankfree[b])
            w = rc[i % 2][:, 0:z - a]
            v = V(lambda e: e.tensor_tensor(w, PS[b][:, 0:z - a], col("sin", a, z), ALU.mult), tk)
            bankfree[b] = [v]
            V(lambda e: e.tensor_tensor(xap, xap, col("cos", a, z), ALU.mult))
            return V(lambda e: e.tensor_tensor(xap, xap, w, ALU.add))

        def gla():
            for a in range(2):
                for i, (c0, c1) in enumerate(((0, TX), (TX, TA))):
                    b = 2 * a + i
                    tk = MM(PS[b][:, 0:c1 - c0], cols[0:16, COFF["wgu"][0] + 128 * a:COFF["wgu"][0] + 128 * a + 128],
                            lrT[:, c0:c1])
                    t = V(lambda e, a=a, b=b, c0=c0, c1=c1: e.tensor_scalar(zb[:, a, c0:c1], PS[b][:, 0:c1 - c0],
                                                                            col("bgate", a, a + 1), None, ALU.add), tk)
                    bankfree[b] = [t]
            t_lr[0] = tk
            S(lambda e: e.activation(za, zb, ACT.Abs), t)
            S(lambda e: e.activation(za, za, ACT.Exp, scale=-1.0))
            t = S(lambda e: e.activation(za, za, ACT.Ln, bias=1.0))
            yield
            yield
            V(lambda e: e.scalar_tensor_tensor(out=zb, in0=zb, scalar=0.0, in1=za, op0=ALU.min, op1=ALU.subtract), t)
            for a in range(2):
                V(lambda e, a=a: e.tensor_tensor_scan(bx[:, a, :], col("reset", 0, TX), zb[:, a, 0:TX], 0.0, ALU.mult, ALU.add))
                V(lambda e, a=a: e.tensor_tensor_scan(bm[:, a, :], col("reset", TX, TA), zb[:, a, TX:TA], 0.0, ALU.mult,
                                                      ALU.add))
            last = V(lambda e: e.memset(A, 0.0))
            V(lambda e: e.memset(St, 0.0))
            mm = last
            Df, Ef = xT[:, 0:1024], xT[:, 2 * TA:2 * TA + 1024]
            Efv = Ef.rearrange("p (a c) -> p a c", a=2)
            ex = last

            def decay(s, ex):
                bxf = bx.rearrange("p a c -> p (a c)").rearrange("p (n s) -> p n s", s=2 * s)
                ref = bxf[:, :, s - 1:s].to_broadcast([128, 512 // s, 2 * s])
                d = V(lambda e: e.tensor_tensor(Df.rearrange("p (n s) -> p n s", s=2 * s), bxf, ref, ALU.subtract), ex)
                S(lambda e: e.activation(Ef, Df, ACT.Abs), d)
                return S(lambda e: e.activation(Ef, Ef, ACT.Exp, scale=-1.0 / 16.0))

            for li, s in enumerate((0,) + LEVELS):
                if s == 0:
                    q_in, k_in, t_q = gqT, gkT, last
                else:
                    V(lambda e: e.tensor_tensor(Qs, gqT, Efv, ALU.mult), ex, mm)
                    t_q = V(lambda e: e.tensor_tensor(Ks, gkT, Efv, ALU.mult))
                    q_in, k_in = Qs, Ks
                if li < len(LEVELS):
                    ex = decay(LEVELS[li], t_q)
                mms = []
                for c in range(NT):
                    cc, par = c // 2, c % 2
                    p0 = 64 * par
                    for i in range(4):
                        ci, h = 2 * cc + i // 2, 2 * (i % 2) + par
                        mm = MM(PS[c][:, i * 128:(i + 1) * 128], k_in[p0:p0 + 64, h // 2, ci * 128:(ci + 1) * 128],
                                q_in[p0:p0 + 64, h // 2, ci * 128:(ci + 1) * 128], t_q, *bankfree[c])
                    mms.append(mm)
                yield
                for c in range(NT):
                    mk = cols[:, COFF["masks"][0] + 128 * li:COFF["masks"][0] + 128 * (li + 1)].bitcast(U32)\
                        .rearrange("p (o c) -> p o c", o=1).to_broadcast([128, 4, 128])
                    v = V(lambda e, c=c, mk=mk: e.copy_predicated(
                        A[:, c * 512:(c + 1) * 512].rearrange("p (h i) -> p h i", h=4), mk,
                        PS[c][:, :].rearrange("p (h i) -> p h i", h=4)), mms[c])
                    bankfree[c] = [v]
            dec3 = sm[:, 16:24].rearrange("p (a c) -> p a c", a=2)
            bc = bx.rearrange("p a c -> p (a c)").rearrange("p (n s) -> p n s", s=128)
            d = V(lambda e: e.tensor_tensor(Df.rearrange("p (n s) -> p n s", s=128),
                                            bc[:, :, 127:128].to_broadcast([128, 8, 128]), bc, ALU.subtract), ex)
            d2 = V(lambda e: e.tensor_tensor(Qs2[:, :, 0:NM], bm[:, :, NM - 1:NM].to_broadcast([128, 2, NM]), bm, ALU.subtract))
            ex = S(lambda e: e.activation(Ef, Df, ACT.Exp, scale=1.0 / 16.0), d)
            ex2 = S(lambda e: e.activation(Qs2[:, :, 0:NM], Qs2[:, :, 0:NM], ACT.Exp, scale=1.0 / 16.0), d2)
            t_dec = S(lambda e: e.activation(sm[:, 16:24], bc[:, :, 127], ACT.Exp, scale=1.0 / 16.0))
            V(lambda e: e.tensor_tensor(Ks.rearrange("p a c -> p (a c)"), gkT.rearrange("p a c -> p (a c)"), Ef, ALU.mult), ex, mm)
            t_km = V(lambda e: e.tensor_tensor(gkm, gkm, Qs2[:, :, 0:NM], ALU.mult), ex2)
            ex = S(lambda e: e.activation(Qs2.rearrange("p a c -> p (a c)"), bx.rearrange("p a c -> p (a c)"), ACT.Exp,
                                          scale=1.0 / 16.0), t_km)
            yield
            t_qb = V(lambda e: e.tensor_tensor(Qs2, Qs2, gqT, ALU.mult), ex)
            khv = Qs.rearrange("p a c -> p (a c)").rearrange("p (c d) -> p c d", c=4)
            t_kh = []
            for c in range(4):
                dst = khm if c == 0 else khv[:, c - 1, :]
                w = NM if c == 0 else 128
                for a in range(2):
                    src = gkm[:, a, :] if c == 0 else Ks[:, a, (c - 1) * 128:c * 128]
                    tk = TR(PS[c][0:w, a * 128:(a + 1) * 128], src, t_km, *bankfree[c])
                v = V(lambda e, dst=dst, c=c, w=w: e.tensor_copy(dst, PS[c][0:w, 0:256]), tk)
                bankfree[c] = [v]
                t_kh.append(v)
                yield
            for c in range(NT):
                kk = khm if c == 0 else khv[:, c - 1, :]
                vv = gvm if c == 0 else gv[:, c - 1, :]
                for a in range(2):
                    tk = MM(PS[c][:, a * 256:(a + 1) * 256], kk[:, a * 128:(a + 1) * 128], vv[:, a * 256:(a + 1) * 256],
                            t_kh[c], *bankfree[c])
                for a in range(2):
                    for u in range(2):
                        p0 = 64 * u
                        blk = PS[c][p0:p0 + 64, a * 256 + u * 128:a * 256 + (u + 1) * 128]
                        dst = St[p0:p0 + 64, c, a, u * 128:(u + 1) * 128]
                        if c == 0:
                            t_S = V(lambda e, dst=dst, blk=blk: e.tensor_copy(dst, blk), tk)
                        else:
                            t_S = V(lambda e, dst=dst, blk=blk, a=a, u=u, p0=p0, c=c: e.scalar_tensor_tensor(
                                out=dst, in0=St[p0:p0 + 64, c - 1, a, u * 128:(u + 1) * 128],
                                scalar=dec3[p0:p0 + 64, a, c - 1:c], in1=blk, op0=ALU.mult, op1=ALU.add), tk, t_dec)
                bankfree[c] = [t_S]
                yield
            ss4, r4 = sm[:, 32:48], sm[:, 48:64]
            xfree = [qv.tok()]
            for c in range(NT):
                b = c % 2
                o = xT[:, b * 512:(b + 1) * 512]
                sq = xT[:, 1056 + b * 512:1056 + (b + 1) * 512]
                for a in range(2):
                    MM(PS[b][:, a * 256:(a + 1) * 256], Qs2[:, a, c * 128:(c + 1) * 128], St[:, c, a, :], t_qb, t_S,
                       *bankfree[b], stop=False)
                    for u in range(2):
                        h = 2 * a + u
                        blk = ((c // 2) * 2 + u) * 4 + (c % 2) * 2 + a
                        tk = MM(PS[b][:, h * 128:(h + 1) * 128], A[:, blk * 128:(blk + 1) * 128],
                                gv[:, c, h * 128:(h + 1) * 128], start=False, stop=(u == 1), mark=True)
                a = S(lambda e, b=b, sq=sq: e.activation(sq, PS[b][:, :], ACT.Square), tk, *xfree)
                v = V(lambda e, c=c, b=b, o=o: e.tensor_tensor(o, PS[b][:, :], gr[:, c, :], ALU.mult), a,
                      *(ofree[b] if c >= 2 else []))
                V(lambda e, c=c, sq=sq: e.tensor_reduce(ss4[:, 4 * c:4 * c + 4], sq.rearrange("p (h v) -> p h v", h=4), AX,
                                                        ALU.add), a)
                bankfree[b] = [qv.tok()]
                r = rstd(r4[:, 4 * c:4 * c + 4], ss4[:, 4 * c:4 * c + 4], 128.0, 1e-5)
                yield
                v = V(lambda e, c=c, o=o: e.tensor_tensor(
                    o.rearrange("p (h v) -> p h v", h=4), o.rearrange("p (h v) -> p h v", h=4),
                    r4[:, 4 * c:4 * c + 4].rearrange("p (h o) -> p h o", o=1).to_broadcast([128, 4, 128]), ALU.mult), r)
                xfree = [v]
                b2 = 2 + b
                for h in range(4):
                    tk = TR(PS[b2][:, h * 128:(h + 1) * 128], o[:, h * 128:(h + 1) * 128], v, *bankfree[b2], mark=(h == 3))
                ofree[b] = [tk]
                cp = S(lambda e, b2=b2, c=c: e.activation(mixT[:, 0:4, c * 128:(c + 1) * 128],
                                                          PS[b2][:, :].rearrange("p (h v) -> p h v", h=4), ACT.Copy), tk)
                bankfree[b2] = [cp]
                yield

        def swa():
            for a in range(4):
                rope(sqT[:, a, :], 0, TX, a)
            rope(skT1[:, 0:TX], 0, TX, 0)
            t_rope = rope(skT1[:, TX:TA], TX, TA, 1)
            yield
            Sa = xT[:, 4 * TA:4 * TA + 1088].rearrange("p (h k) -> p h k", h=4)
            PT = [xT[:, 3200:3712], xT[:, 3712:4224], lrT]
            snk = row("sink")
            ptf = [t_lr[0]]
            saf = t_rope
            for n in range(NT):
                w0 = 0 if n else 128
                for g in range(2):
                    p0, b = 64 * g, 4 + g
                    for j in range(4):
                        q = sqT[p0:p0 + 64, j, n * 128:(n + 1) * 128]
                        MM(PS[b][:, 256:272], q, skT1[p0:p0 + 64, TX:TA], t_rope, *bankfree[b], mark=False)
                        tk = MM(PS[b][:, w0:256], q, skT1[p0:p0 + 64, (n - 1) * 128 + w0:(n + 1) * 128])
                        v = V(lambda e, b=b, j=j, w0=w0: e.scalar_tensor_tensor(
                            out=Sa[:, j, w0:272], in0=PS[b][:, w0:272], scalar=0.125, in1=col("wmask", w0, 272),
                            op0=ALU.mult, op1=ALU.add), tk, saf)
                        bankfree[b] = [v]
                        if j == 1:
                            yield
                    mx, ng, Z, es = (sm[:, 64 + 4 * i:68 + 4 * i] for i in range(4))
                    sk4 = snk[:, 4 * g:4 * g + 4]
                    V(lambda e, w0=w0: e.tensor_reduce(mx, Sa[:, :, w0:272], AX, ALU.max))
                    V(lambda e, sk4=sk4: e.tensor_tensor(mx, mx, sk4, ALU.max))
                    V(lambda e: e.tensor_scalar(ng, mx, -1.0, None, ALU.mult))
                    v = V(lambda e, sk4=sk4: e.tensor_tensor(es, sk4, mx, ALU.subtract))
                    for j in range(4):
                        S(lambda e, j=j, w0=w0: e.activation(Sa[:, j, w0:272], Sa[:, j, w0:272], ACT.Exp, bias=ng[:, j:j + 1],
                                                             accum_out=Z[:, j:j + 1]), v)
                    a = S(lambda e: e.activation(es, es, ACT.Exp))
                    yield
                    V(lambda e: e.tensor_tensor(Z, Z, es, ALU.add), a)
                    V(lambda e: e.reciprocal(Z, Z))
                    v = V(lambda e, w0=w0: e.tensor_tensor(
                        Sa[:, :, w0:272], Sa[:, :, w0:272],
                        Z.rearrange("p (h o) -> p h o", o=1).to_broadcast([128, 4, 272 - w0]), ALU.mult))
                    blocks = [(0, 0, 128)] * (n > 0) + [(1, 128, 128), (2, 256, NM)]
                    tv = {}
                    for (bi, c0, w) in blocks:
                        b = 6 if bi != 1 else 4 + g
                        for j in range(4):
                            tk = TR(PS[b][0:w, j * 128:(j + 1) * 128], Sa[:, j, c0:c0 + w], v, *bankfree[b], mark=(j == 3))
                        dst = PT[bi][0:w, 0:512]
                        cp = S(lambda e, dst=dst, b=b, w=w: e.activation(dst, PS[b][0:w, :], ACT.Copy), tk, *ptf)
                        bankfree[b] = [cp]
                        tv[bi] = cp
                        saf = tk
                    yield
                    for i, (bi, c0, w) in enumerate(blocks):
                        vs = svm if bi == 2 else sv[:, n - 1 + bi, :]
                        tk = MM(PS[7][64 * g:64 * g + 64, :], vs[:, 64 * g:64 * g + 64], PT[bi][0:w, 0:512],
                                tv[bi], *bankfree[7], start=(i == 0), stop=(i == len(blocks) - 1))
                    ptf = [tk]
                cp = S(lambda e, n=n: e.activation(mixT[:, 4:8, n * 128:(n + 1) * 128],
                                                   PS[7][:, :].rearrange("p (j c) -> p j c", j=4), ACT.Copy), tk)
                bankfree[7] = [cp]
                yield

        t_lr = [None]
        ofree = [[], []]
        beside(gla(), swa())
        fence()

        smix.close()
        splits, xh_, xl_ = open_split("b")
        xh3 = xh_[:, 0:8 * TA].rearrange("p (k c) -> p k c", k=8)
        xl3 = xl_[:, 0:8 * TA].rearrange("p (k c) -> p k c", k=8)
        for b in range(8):
            bankfree[b] = []
        prep()
        t_m = []
        for k in range(8):
            h, l, m = xh3[:, k, 0:TX], xl3[:, k, 0:TX], mixT[:, k, :]
            a = S(lambda e, h=h, m=m: e.activation(h, m, ACT.Copy))
            t_m.append(V(lambda e, h=h, l=l, m=m: e.tensor_tensor(l, m, h.bitcast(F32), ALU.subtract), a))

        def out_proj(name, gate, tmp, *after):
            for qc in range(4):
                pv, tp, n = panel(name, qc, last=(qc == 3 and gate is None))
                for t in range(NT):
                    b = bank()
                    tk = MM3(PS[b][:, 0:CW], [((xh3[:, k, t * 128:(t + 1) * 128], xl3[:, k, t * 128:(t + 1) * 128]),
                                               tuple(w[:, k, :] for w in pv)) for k in range(8)], tp, *bankfree[b], *after)
                    hs = h3[:, t, qc * CW:(qc + 1) * CW]
                    if gate is None:
                        v = V(lambda e, hs=hs, b=b: e.tensor_tensor(hs, hs, PS[b][:, 0:CW], ALU.add), tk)
                    else:
                        v = V(lambda e, b=b, qc=qc: e.tensor_tensor(tmp, PS[b][:, 0:CW], gate[:, qc * CW:(qc + 1) * CW],
                                                                    ALU.mult), tk)
                        V(lambda e, hs=hs: e.tensor_tensor(hs, hs, tmp, ALU.add))
                    bankfree[b] = [v]
                release(n, tk)

        out_proj("wo1", None, None, t_m[-1])
        fence()
        sb1.close()
        g2b = sb("g2b", 1024)
        B2b = sb("B2b", 1024)
        sff = scope()
        AH = sbs(sff, "ah", 4096, R32)[:, :].rearrange("p (f c) -> p f c", f=8)
        AL = sbs(sff, "al", 4096, R32)[:, :].rearrange("p (f c) -> p f c", f=8)
        fbig = sbs(sff, "fbig", 8768)

        csil = sm[:, 96:104]
        t_cs = S(lambda e: e.activation(csil, col("ccol"), ACT.Silu), t_c)
        acc = [fbig[:, 0:256], fbig[:, 256:512]]
        ones = fbig[:, 512:640]
        n2row = fbig[:, 640:1664]
        sqt = [fbig[:, 1664:2176], fbig[:, 2176:2688]]
        sqq = [fbig[:, 2688:3200], fbig[:, 3200:3712]]
        xs3b = fbig[:, 3712:3712 + 4096].rearrange("p (t d) -> p t d", t=NT)
        jk = fbig[:, 1664:2688]
        accfree = [[], []]
        pending = []
        V(lambda e: e.memset(ones, 1.0))
        s_b = sem("s_b")
        for i, dst in enumerate((g1b, B2b[:, :], A2b, g2b[:, :], n2row)):
            t_b = LOAD(qs, dst, brows[:, i * 1024:(i + 1) * 1024].to_broadcast([128, 1024]), s_b, qs.tok())

        def ada_acc(i, pv, tp):
            a = acc[i % 2]
            V(lambda e: e.tensor_scalar(a, pv[:, 0, :], csil[:, 0:1], None, ALU.mult), tp, t_cs, *accfree[i % 2])
            for k in range(1, 8):
                v = V(lambda e, k=k: e.scalar_tensor_tensor(out=a, in0=pv[:, k, :], scalar=csil[:, k:k + 1], in1=a,
                                                            op0=ALU.mult, op1=ALU.add))
            pending.append((i, v))
            return v

        def ada_sums():
            while pending:
                i, v = pending.pop(0)
                a = acc[i % 2]
                if i < 8:
                    for j in range(2):
                        tk = MM(PS[7][:, j:j + 1], a[:, j * 128:(j + 1) * 128], ones[:, 0:1], v, *bankfree[7])
                    v = V(lambda e, i=i: e.tensor_tensor(mod[:, 2 * i:2 * i + 2], PS[7][:, 0:2],
                                                         col("adab", 2 * i, 2 * i + 2), ALU.add), tk)
                else:
                    tk = MM(PS[7][:, 0:CW], ones, a, v, *bankfree[7])
                    c = (i % 4) * CW
                    d = (g1b, B2b, A2b, g2b)[i // 4 - 2][:, c:c + CW]
                    v = V(lambda e, d=d: e.tensor_tensor(d, d, PS[7][:, 0:CW], ALU.add), tk, t_b)
                    if i // 4 == 4:
                        nr = n2row[:, c:c + CW]
                        V(lambda e, d=d, nr=nr: e.scalar_tensor_tensor(out=d, in0=d, scalar=1.0, in1=nr, op0=ALU.add,
                                                                       op1=ALU.mult))
                bankfree[7] = [v]
                accfree[i % 2] = [tk]

        def row_norm(eps, junk):
            for t in range(NT):
                a = sumsq(sm[:, t:t + 1], h3[:, t, :], junk)
            return rstd(sm[:, 8:12], sm[:, 0:4], 1024.0, eps, a)

        r = row_norm(1e-5, jk)
        prep()
        t_src = [V(lambda e, t=t: e.tensor_scalar(xs3b[:, t, :], h3[:, t, :], sm[:, 8 + t:9 + t], None, ALU.mult), r)
                 for t in range(NT)]
        for b in range(8):
            bankfree[b] = []
        norm_T(xs3b, col("ffw"), None, [0, 1, 2, 3], t_src, jk)
        fence()

        for b in range(8):
            bankfree[b] = []
        fb = (0, 1, 2, 3, 4, 5, 6)
        for q in range(4):
            t_a = []
            for i in range(4):
                pv, tp, n = panel("ff1", 4 * q + i)
                for j in range(2):
                    f = 2 * i + j
                    b = bank(fb)
                    tk = MM3(PS[b][:, :], [(tuple(w[:, k, j * 128:(j + 1) * 128] for w in pv), (xh3[:, k, 0:TX], xl3[:, k, 0:TX]))
                                           for k in range(8)], tp, *bankfree[b])
                    u, w2 = sqt[f % 2], sqq[f % 2]
                    a = S(lambda e, u=u, b=b: e.activation(u, PS[b][:, :], ACT.Relu), tk, qv.tok())
                    bankfree[b] = [a]
                    v = V(lambda e, u=u, w2=w2: e.tensor_tensor(w2, u, u, ALU.mult), a)
                    a = S(lambda e, f=f, w2=w2: e.activation(AH[:, f, :], w2, ACT.Copy), v)
                    v = V(lambda e, f=f, w2=w2: e.tensor_tensor(AL[:, f, :], w2, AH[:, f, :].bitcast(F32), ALU.subtract), a)
                    t_a.append([a, v])
                release(n, tk)
                ada_sums()
            for i in range(4):
                pv, tp, n = panel("ff2", 4 * q + i)
                for t in range(NT):
                    b = bank(fb)
                    for k in range(8):
                        c = slice(t * 128, (t + 1) * 128)
                        first = [*tp, *bankfree[b]] if k == 0 else []
                        MM(PS[b][:, 0:CW], AH[:, k, c], pv[0][:, k, :], *first, *t_a[k], start=(k == 0), stop=False)
                        MM(PS[b][:, 0:CW], AL[:, k, c], pv[0][:, k, :], start=False, stop=False)
                        tk = MM(PS[b][:, 0:CW], AH[:, k, c], pv[1][:, k, :], start=False, stop=(k == 7))
                    hs = h3[:, t, i * CW:(i + 1) * CW]
                    v = V(lambda e, hs=hs, b=b: e.tensor_tensor(hs, hs, PS[b][:, 0:CW], ALU.add), tk)
                    bankfree[b] = [v]
                release(n, tk)
                ada_sums()
        fence()

        for t in range(NT):
            a = sumsq(sm[:, t:t + 1], h3[:, t, :], jk)
        r = rstd(sm[:, 8:12], sm[:, 0:4], 1024.0, 1e-5, a)
        for t in range(NT):
            v = V(lambda e, t=t: e.scalar_tensor_tensor(out=h3[:, t, :], in0=h3[:, t, :], scalar=sm[:, 8 + t:9 + t],
                                                        in1=row("fw"), op0=ALU.mult, op1=ALU.mult), r)
            a = sumsq(sm[:, t:t + 1], h3[:, t, :], jk, v)
        r = rstd(sm[:, 12:16], sm[:, 0:4], 1024.0, 1e-6, a)
        sc1 = sm[:, 104:112]
        v = V(lambda e: e.scalar_tensor_tensor(out=sc1, in0=mod[:, 8:16], scalar=1.0, in1=col("n1g"), op0=ALU.add, op1=ALU.mult))
        t_src = [V(lambda e, t=t: e.tensor_scalar(xs3b[:, t, :], h3[:, t, :], sm[:, 12 + t:13 + t], None, ALU.mult), r)
                 for t in range(NT)]
        for b in range(8):
            bankfree[b] = []
        norm_T(xs3b, sc1, mod[:, 0:8], [0, 1, 2, 3], t_src, jk)
        fence()

        sff.close()
        sb2 = scope()
        big = sbs(sb2, "big2", BIG2)
        for b in range(8):
            bankfree[b] = []
        off[0], lim[0] = 0, BIG2
        qk = carve(4096).rearrange("p (a c) -> p a c", a=8)
        mv = carve(4 * 4 * 129).rearrange("p (t h c) -> p t h c", t=4, h=4)
        mo = carve(2048).rearrange("p (t c) -> p t c", t=NT)
        dq = carve(2048).rearrange("p (a c) -> p a c", a=4)
        dk = carve(2048).rearrange("p (a c) -> p a c", a=4)
        dv = carve(2048).rearrange("p (t c) -> p t c", t=NT)
        hoM = carve(2048)
        ub = hoM[:, 0:1030].rearrange("p (a c) -> p a c", a=2)
        cy = hoM[:, 1030:1542]
        hoM = hoM.rearrange("p (t c) -> p t c", t=NT)
        V(lambda e: e.memset(ub[:, :, 0:3], 0.0))
        V(lambda e: e.memset(mv[:, :, :, 128:129], 1.0))
        cyfree = None
        ubfree = [None, None]
        for i in range(4):
            pv, tp, n = panel("w2", i)
            for j in range(2):
                ch = 2 * i + j
                b = bank()
                tk = MM3(PS[b][:, :], [(tuple(w[:, k, j * 128:(j + 1) * 128] for w in pv), (xh3[:, k, 0:TX], xl3[:, k, 0:TX]))
                                       for k in range(8)], tp, *bankfree[b])
                u = ub[:, ch % 2, :]
                cw = [col("convw", 4 * ch + w, 4 * ch + w + 1) for w in range(4)]
                cp = S(lambda e, u=u, b=b: e.activation(u[:, 3:515], PS[b][:, :], ACT.Copy), tk, ubfree[ch % 2] or qv.tok())
                bankfree[b] = [cp]
                V(lambda e, u=u, cw=cw: e.tensor_scalar(cy, u[:, 0:512], cw[0], None, ALU.mult), cp, cyfree or cp)
                for w in (1, 2, 3):
                    v = V(lambda e, u=u, cw=cw, w=w: e.scalar_tensor_tensor(out=cy, in0=u[:, w:w + 512], scalar=cw[w], in1=cy,
                                                                        op0=ALU.mult, op1=ALU.add))
                a = S(lambda e, ch=ch: e.activation(qk[:, ch, :], cy, ACT.Silu, bias=col("convb", ch, ch + 1)), v)
                cyfree = a
                ubfree[ch % 2] = v
            release(n, tk)
        for i, dst in ((4, dq), (6, dk)):
            for g in range(2):
                pv, tp, n = panel("w2", i + g)
                for a in range(2):
                    tk, v = projT(pv, 128 * a, 128, tp, [(0, TX, dst[:, 2 * g + a, :])])
                release(n, tk)
        for g in range(2):
            pv, tp, n = panel("w2", 8 + g)
            for t in range(NT):
                b = bank()
                tk = MM3(PS[b][:, 0:CW], [((xcol(xh_, k, t * 128), xcol(xl_, k, t * 128)), tuple(w[:, k, :] for w in pv))
                                          for k in range(8)], tp, *bankfree[b])
                v = V(lambda e, t=t, b=b, g=g: e.tensor_copy(mv[:, t, 2 * g:2 * g + 2, 0:128],
                                                             PS[b][:, 0:CW].rearrange("p (h c) -> p h c", h=2)), tk)
                bankfree[b] = [v]
            release(n, tk)
        for i, dst, fn in ((10, dv, ACT.Copy), (12, mo, ACT.Sigmoid)):
            for g in range(2):
                pv, tp, n = panel("w2", i + g)
                tk, v = projR(pv, 0, CW, tp, rowsT(dst, CW * g), fn=fn)
                release(n, tk)
        mng = row("mng").rearrange("p (o c) -> p o c", o=1).to_broadcast([128, 4, 512])
        V(lambda e: e.tensor_tensor(mo, mo, mng, ALU.mult), v)
        pv, tp, n = panel("w2", 14, last=True)
        gb = []
        for i in range(2):
            b = bank()
            tk = MM3(PS[b][:, :], [(tuple(w[:, k, i * 128:(i + 1) * 128] for w in pv), (xh3[:, k, 0:TX], xl3[:, k, 0:TX]))
                                   for k in range(8)], tp, *bankfree[b])
            gb.append(b)
        release(n, tk)
        fence()
        splits.close()
        smix = scope()
        over = sbs(smix, "over2", OVER, F32, "right")
        xT = over[:, 0:8 * TA]
        ooff[0] = 8 * TA
        off[0], lim[0] = 8 * TA, OVER
        big = over

        ig, lf, bb, MM_, tmp = (xT[0:4, i * 512:(i + 1) * 512] for i in range(5))
        V(lambda e: e.tensor_scalar(ig, PS[gb[0]][0:4, :], cols[0:4, COFF["gbi"][0]:COFF["gbi"][0] + 1], None, ALU.add), tk)
        v = V(lambda e: e.tensor_scalar(lf, PS[gb[1]][0:4, :], cols[0:4, COFF["gbf"][0]:COFF["gbf"][0] + 1], None, ALU.add))
        S(lambda e: e.activation(tmp, lf, ACT.Abs), v)
        S(lambda e: e.activation(tmp, tmp, ACT.Exp, scale=-1.0))
        a = S(lambda e: e.activation(tmp, tmp, ACT.Ln, bias=1.0))
        V(lambda e: e.scalar_tensor_tensor(out=lf, in0=lf, scalar=0.0, in1=tmp, op0=ALU.min, op1=ALU.subtract), a)
        onesrow = xT[0:4, 5 * 512:6 * 512]
        V(lambda e: e.memset(onesrow, 1.0))
        V(lambda e: e.tensor_tensor_scan(bb, onesrow, lf, 0.0, ALU.mult, ALU.add))
        V(lambda e: e.tensor_tensor(ig, ig, bb, ALU.subtract))
        V(lambda e: e.tensor_tensor_scan(MM_, ig, ig, 0.0, ALU.max, ALU.max))
        V(lambda e: e.tensor_tensor(bb, bb, MM_, ALU.add))
        V(lambda e: e.tensor_scalar(bb, bb, -1.0, None, ALU.mult))
        v = V(lambda e: e.tensor_scalar(MM_, MM_, -1.0, None, ALU.mult))
        ac, emc = sm[:, 128:144], sm[:, 144:160]
        for t in range(NT):
            TR(PS[0][:, 4 * t:4 * t + 4], ig[:, t * 128:(t + 1) * 128], v, mark=False)
            tk = TR(PS[0][:, 16 + 4 * t:20 + 4 * t], bb[:, t * 128:(t + 1) * 128])
        v = V(lambda e: e.tensor_copy(ac, PS[0][:, 0:16]), tk)
        a = S(lambda e: e.activation(emc, PS[0][:, 16:32], ACT.Exp), v)
        Wt = big[:, 4224:6272].rearrange("p (j c) -> p j c", j=4)
        Dt = big[:, 6272:6784]
        dn = sm[:, 160:164]
        sel = cols[0:4, COFF["sel"][0]:COFF["sel"][0] + 512]
        for b in range(8):
            bankfree[b] = [v, a]
        num_t = None
        for h in range(4):
            tmb = MM(PS[1][:, :], sel[:, h * 128:(h + 1) * 128], MM_, *bankfree[1])
            for j in range(NT):
                w = TX - j * 128
                b = 2 + j % 2
                tk = MM(PS[b][:, 0:w], qk[:, 4 + h, j * 128:(j + 1) * 128], qk[:, h, j * 128:TX], *bankfree[b])
                V(lambda e, j=j, w=w, h=h: e.tensor_scalar(Dt[:, 0:w], PS[1][:, j * 128:TX], ac[:, 4 * j + h:4 * j + h + 1], 0.0,
                                                           ALU.add, ALU.min), tmb, qs.tok())
                a = S(lambda e, w=w: e.activation(Dt[:, 0:w], Dt[:, 0:w], ACT.Exp), qv.tok())
                V(lambda e: e.tensor_tensor(Dt[:, 0:128], Dt[:, 0:128], col("caus"), ALU.mult), a)
                v = V(lambda e, j=j, w=w, b=b: e.scalar_tensor_tensor(
                    out=Wt[:, j, j * 128:TX], in0=PS[b][:, 0:w], scalar=128.0 ** -0.5, in1=Dt[:, 0:w], op0=ALU.mult,
                    op1=ALU.mult), tk, num_t or tk)
                bankfree[b] = [v]
            bankfree[1] = [v]
            for t in range(NT):
                b = 4 + t
                for j in range(t + 1):
                    tk = MM(PS[b][:, 0:129], Wt[:, j, t * 128:(t + 1) * 128], mv[:, j, h, :], v, *bankfree[b],
                            start=(j == 0), stop=(j == t))
                V(lambda e, b=b, t=t, h=h: e.tensor_tensor(dn[:, t:t + 1], PS[b][:, 128:129], emc[:, 4 * t + h:4 * t + h + 1],
                                                           ALU.max), tk)
                V(lambda e, b=b, t=t: e.scalar_tensor_tensor(out=dn[:, t:t + 1], in0=PS[b][:, 128:129], scalar=-1.0,
                                                             in1=dn[:, t:t + 1], op0=ALU.mult, op1=ALU.max))
                V(lambda e, t=t: e.reciprocal(dn[:, t:t + 1], dn[:, t:t + 1]))
                vv = V(lambda e, b=b, t=t, h=h: e.tensor_scalar(hoM[:, t, h * 128:(h + 1) * 128], PS[b][:, 0:128],
                                                                dn[:, t:t + 1], None, ALU.mult))
                bankfree[b] = [vv]
            num_t = tk
        fence()

        def head_norm(o3, gate, eps):
            s4, r4 = sm[:, 176:192], sm[:, 192:208]
            sqb = over[:, 4224:6272]
            a = S(lambda e: e.activation(sqb, o3.rearrange("p t c -> p (t c)"), ACT.Square), qv.tok())
            V(lambda e: e.tensor_reduce(s4, sqb.rearrange("p (n c) -> p n c", c=128), AX, ALU.add), a)
            for i in range(4):
                r = rstd(r4[:, 4 * i:4 * i + 4], s4[:, 4 * i:4 * i + 4], 128.0, eps)
            ov = o3.rearrange("p t (h c) -> p (t h) c", h=4)
            V(lambda e: e.tensor_tensor(ov, ov, r4.rearrange("p (n o) -> p n o", o=1).to_broadcast([128, 16, 128]), ALU.mult), r)
            V(lambda e: e.tensor_tensor(ov, ov, gate, ALU.mult))

        head_norm(hoM, mo.rearrange("p t (h c) -> p (t h) c", h=4), 1e-6)
        fence()

        lt = sm[:, 208:272]
        ls = sm[:, 272:276]
        V(lambda e: e.tensor_tensor_reduce(out=lt, in0=row("lq1"), in1=row("lk1"), scale=1.0, scalar=0.0, op0=ALU.mult,
                                           op1=ALU.add, accum_out=ls[:, 0:1]))
        v = V(lambda e: e.tensor_tensor_reduce(out=lt, in0=row("lq2"), in1=row("lk2"), scale=1.0, scalar=0.0, op0=ALU.mult,
                                               op1=ALU.add, accum_out=ls[:, 1:2]))
        a = S(lambda e: e.activation(ls[:, 0:2], ls[:, 0:2], ACT.Exp), v)
        V(lambda e: e.tensor_tensor(ls[:, 2:3], ls[:, 1:2], ls[:, 0:1], ALU.subtract), a)
        V(lambda e: e.tensor_scalar(ls[:, 2:3], ls[:, 2:3], -0.2, None, ALU.add))
        for b in range(8):
            bankfree[b] = []
        hoD = qk[:, 0:4, :].rearrange("p a (t c) -> p (a t c)", t=1).rearrange("p (t c) -> p t c", t=NT)
        P = [xT[:, i * 512:(i + 1) * 512] for i in range(4)]
        aTt = [xT[:, 2048 + i * 512:2560 + i * 512].rearrange("p (j c) -> p j c", j=4) for i in range(2)]
        sc = sm[:, 276:300]
        cnt = 0
        pf = [[], []]
        atf = [[], []]
        for t in range(NT):
            n = (t + 1) * 128
            for h in range(4):
                i2 = cnt % 2
                cnt += 1
                so = sc[:, 12 * i2:12 * i2 + 12]
                P0, P1 = P[2 * i2], P[2 * i2 + 1]
                for p in range(2):
                    b = 2 * i2 + p
                    tk = MM(PS[b][:, 0:n], dq[64 * p:64 * p + 64, h, t * 128:(t + 1) * 128], dk[64 * p:64 * p + 64, h, 0:n],
                            *bankfree[b])
                    V(lambda e, b=b, n=n: e.tensor_tensor(PS[b][:, n - 128:n], PS[b][:, n - 128:n], col("negm"), ALU.add), tk)
                    V(lambda e, b=b, n=n, p=p, so=so: e.tensor_reduce(so[:, p:p + 1], PS[b][:, 0:n], AX, ALU.max))
                    v = V(lambda e, p=p, so=so: e.tensor_scalar(so[:, 2 + p:3 + p], so[:, p:p + 1], -0.125, None, ALU.mult))
                    a = S(lambda e, b=b, n=n, p=p, so=so, Pp=P[2 * i2 + p]: e.activation(
                        Pp[:, 0:n], PS[b][:, 0:n], ACT.Exp, bias=so[:, 2 + p:3 + p], scale=0.125,
                        accum_out=so[:, 4 + p:5 + p]), v, *pf[i2])
                    bankfree[b] = [a]
                V(lambda e, so=so: e.reciprocal(so[:, 6:8], so[:, 4:6]), a)
                V(lambda e, so=so: e.tensor_tensor(so[:, 7:8], so[:, 7:8], ls[:, 2:3], ALU.mult))
                V(lambda e, so=so, P1=P1, n=n: e.tensor_scalar(P1[:, 0:n], P1[:, 0:n], so[:, 7:8], None, ALU.mult))
                v = V(lambda e, so=so, P0=P0, P1=P1, n=n: e.scalar_tensor_tensor(
                    out=P0[:, 0:n], in0=P0[:, 0:n], scalar=so[:, 6:7], in1=P1[:, 0:n], op0=ALU.mult, op1=ALU.add))
                b = 4 + i2
                for j in range(t + 1):
                    tk = TR(PS[b][:, j * 128:(j + 1) * 128], P0[:, j * 128:(j + 1) * 128], v, *bankfree[b], mark=(j == t))
                pf[i2] = [tk]
                at = aTt[i2]
                cp = S(lambda e, b=b, at=at, n=n: e.activation(at.rearrange("p j c -> p (j c)")[:, 0:n], PS[b][:, 0:n], ACT.Copy),
                       tk, *atf[i2])
                bankfree[b] = [cp]
                ob = 6 + t % 2
                for j in range(t + 1):
                    tk = MM(PS[ob][:, h * 128:(h + 1) * 128], at[:, j, :], dv[:, j, h * 128:(h + 1) * 128], cp, *bankfree[ob],
                            start=(j == 0), stop=(j == t))
                atf[i2] = [tk]
            v = V(lambda e, ob=ob, t=t: e.tensor_copy(hoD[:, t, :], PS[ob][:, :]), tk)
            bankfree[ob] = [v]
        fence()
        dg8 = sm[:, 300:428]
        V(lambda e: e.tensor_scalar(dg8, row("dng"), 0.8, None, ALU.mult))
        head_norm(hoD, dg8.rearrange("p (o c) -> p o c", o=1).to_broadcast([128, 16, 128]), 1e-6)
        fence()

        smix.close()
        splits, xh_, xl_ = open_split("c")
        xh3 = xh_[:, 0:8 * TA].rearrange("p (k c) -> p k c", k=8)
        xl3 = xl_[:, 0:8 * TA].rearrange("p (k c) -> p k c", k=8)
        prep()
        for k in range(8):
            o3 = hoM if k < 4 else hoD
            b, h4 = k % 4, k % 4
            for t in range(NT):
                tk = TR(PS[b][:, t * 128:(t + 1) * 128], o3[:, t, h4 * 128:(h4 + 1) * 128], *(bankfree[b] if k > 3 else []),
                        mark=(t == NT - 1))
            h, l = xh3[:, k, 0:TX], xl3[:, k, 0:TX]
            a = S(lambda e, h=h, b=b: e.activation(h, PS[b][:, :], ACT.Copy), tk)
            v = V(lambda e, h=h, l=l, b=b: e.tensor_tensor(l, PS[b][:, :], h.bitcast(F32), ALU.subtract), a)
            bankfree[b] = [v]
        fence()
        for b in range(8):
            bankfree[b] = []
        out_proj("wo2", g1b, dq[:, 0, 0:CW])
        fence()
        sb2.close()
        sb3 = scope()
        big = sbs(sb3, "big3", 12288)
        h2 = big[:, 0:4096].rearrange("p (t d) -> p t d", t=NT)
        r = row_norm(1e-6, big[:, 8192:9216])
        t_src = []
        for t in range(NT):
            V(lambda e, t=t: e.scalar_tensor_tensor(out=h2[:, t, :], in0=h3[:, t, :], scalar=sm[:, 8 + t:9 + t], in1=A2b,
                                                    op0=ALU.mult, op1=ALU.mult), r)
            t_src.append(V(lambda e, t=t: e.tensor_tensor(h2[:, t, :], h2[:, t, :], B2b[:, :], ALU.add)))
        for b in range(8):
            bankfree[b] = []
        norm_T(h2, None, None, [0, 1, 2, 3], t_src, raw)
        fence()
        qT = big[:, 4096:12288].rearrange("p (a c) -> p a c", a=16)
        for b in range(8):
            bankfree[b] = []
        for i in range(8):
            pv, tp, n = panel("wq", i)
            for a in range(2):
                tk, v = projT(pv, 128 * a, 128, tp, [(0, TX, qT[:, 2 * i + a, :])])
            release(n, tk)
        tf = fence()
        splits.close()
        big = sbs(ctx, "big4", BIG4)
        off[0], lim[0] = 0, BIG4
        sk = carve(2048).rearrange("p (a c) -> p a c", a=16)
        t_sk = LOAD(qd, sk, skT, s_sk, *tf)
        for b in range(8):
            bankfree[b] = []
        sS = carve(2048).rearrange("p (a c) -> p a c", a=16)
        cand = carve(2048)
        oh = carve(2048)
        svv = carve(256).rearrange("p (a k) -> p a k", a=16)
        siv = carve(256).bitcast(U32).rearrange("p (a k) -> p a k", a=16)
        sif = carve(256).rearrange("p (a k) -> p a k", a=16)
        fv = carve(128).rearrange("p (h k) -> p h k", h=8)
        fpo = carve(128).bitcast(U32).rearrange("p (h k) -> p h k", h=8)
        fhi = carve(128).bitcast(U32)
        fhf = carve(128)
        es0 = carve(128)
        es1 = carve(128)
        gw = carve(256).rearrange("p (i k) -> p i k", i=2)
        eid = carve(256).bitcast(U32).rearrange("p (i k) -> p i k", i=2)
        act = carve(256).rearrange("p (i k) -> p i k", i=2)
        w_ = carve(256).rearrange("p (i k) -> p i k", i=2)
        eidf = carve(128)
        w32 = carve(4128)
        eidT = carve(128).bitcast(U32)
        yT = cand[:, 0:1024]
        jk2 = carve(1024)
        gs_ = carve((NG - 4) * 1024)
        gs = [raw[:, i * 1024:(i + 1) * 1024] if i < 4 else gs_[:, (i - 4) * 1024:(i - 3) * 1024] for i in range(NG)]
        s_g = [sem(f"s_g{i}") for i in range(NG)]
        iota = col("iota")
        gi = {"n": 0}
        gfree = [list(tf) for _ in range(NG)]

        def gather(tab, idx, tok):
            i = gi["n"] % NG
            gi["n"] += 1
            qg.add(lambda e, i=i, idx=idx: e.indirect_dma_start(
                gs[i], None, tab, bass.IndirectOffsetOnAxis(ap=idx, axis=0)), [tok, *gfree[i]], sem=s_g[i], inc=16)
            dma_n[s_g[i].name] = dma_n.get(s_g[i].name, 0) + 16
            return i, (s_g[i], dma_n[s_g[i].name])

        def topk(t):
            e2 = t % 2
            for q in range(4):
                b = q % 2 + 4
                for a in range(4):
                    tk = MM(PS[b][:, a * 128:(a + 1) * 128], qT[:, 4 * q + a, t * 128:(t + 1) * 128], sk[:, 4 * q + a, :], t_sk,
                            *bankfree[b])
                v = S(lambda e, q=q, b=b: e.activation(sS[:, 4 * q:4 * q + 4, :], PS[b][:, :].rearrange("p (a c) -> p a c", a=4),
                                                       ACT.Copy), tk, qv.tok())
                bankfree[b] = [v]

            def top16(vals, src, idx, *after):
                V(lambda e: e.max(vals[:, 0:8], src), *after)
                V(lambda e: e.max_index(idx[:, 0:8], vals[:, 0:8], src))
                V(lambda e: e.match_replace(src, vals[:, 0:8], src, -3.0e38))
                V(lambda e: e.max(vals[:, 8:16], src))
                V(lambda e: e.max_index(idx[:, 8:16], vals[:, 8:16], src))

            for a in range(16):
                top16(svv[:, a, :], sS[:, a, :], siv[:, a, :], v)
            V(lambda e: e.tensor_copy(sif, siv))
            s4 = svv.rearrange("p (h t) k -> p h t k", t=2)
            c4 = cand.rearrange("p (h i j) -> p h i j", h=8, i=16)
            V(lambda e: e.tensor_tensor(
                c4, s4[:, :, 0, :].rearrange("p h (k o) -> p h k o", o=1).to_broadcast([128, 8, 16, 16]),
                s4[:, :, 1, :].rearrange("p h (o k) -> p h o k", o=1).to_broadcast([128, 8, 16, 16]), ALU.add))
            for h in range(8):
                top16(fv[:, h, :], cand[:, h * 256:(h + 1) * 256], fpo[:, h, :])
            fpf = fpo.rearrange("p h k -> p (h k)")
            i4 = sif.rearrange("p (h t) k -> p h t k", t=2)
            for part, es in ((0, es0), (1, es1)):
                V(lambda e, part=part: e.tensor_scalar(fhi, fpf, 4 if part == 0 else 15, None,
                                                       ALU.logical_shift_right if part == 0 else ALU.bitwise_and))
                V(lambda e: e.tensor_copy(fhf, fhi))
                o3_ = oh.rearrange("p (n i) -> p n i", i=16)
                V(lambda e, o3_=o3_: e.tensor_tensor(
                    o3_, fhf.rearrange("p (n o) -> p n o", o=1).to_broadcast([128, 128, 16]),
                    iota.rearrange("p (o i) -> p o i", o=1).to_broadcast([128, 128, 16]), ALU.is_equal))
                o4_ = oh.rearrange("p (h k i) -> p h k i", h=8, k=16)
                V(lambda e, o4_=o4_, part=part: e.tensor_tensor(
                    o4_, o4_, i4[:, :, part, :].rearrange("p h (o k) -> p h o k", o=1).to_broadcast([128, 8, 16, 16]), ALU.mult))
                V(lambda e, o3_=o3_, es=es: e.tensor_reduce(es, o3_, AX, ALU.add))
            V(lambda e: e.scalar_tensor_tensor(out=eidf, in0=es0, scalar=128.0, in1=es1, op0=ALU.mult, op1=ALU.add))
            ve = V(lambda e, e2=e2: e.tensor_copy(eid[:, e2, :], eidf), ufree[e2])
            V(lambda e: e.tensor_copy(sm[:, 128:136], fv[:, :, 0]))
            gv_ = gw[:, e2, :].rearrange("p (h k) -> p h k", h=8)
            v = V(lambda e, gv_=gv_: e.tensor_tensor(
                gv_, fv, sm[:, 128:136].rearrange("p (h o) -> p h o", o=1).to_broadcast([128, 8, 16]), ALU.subtract))
            a = S(lambda e, e2=e2: e.activation(gw[:, e2, :], gw[:, e2, :], ACT.Exp), v)
            V(lambda e, gv_=gv_: e.tensor_reduce(sm[:, 136:144], gv_, AX, ALU.add), a)
            V(lambda e: e.reciprocal(sm[:, 136:144], sm[:, 136:144]))
            V(lambda e, gv_=gv_: e.tensor_tensor(
                gv_, gv_, sm[:, 136:144].rearrange("p (h o) -> p h o", o=1).to_broadcast([128, 8, 16]), ALU.mult))
            return ve

        def turn_ids(ve, *after):
            tk = TR(PS[6][:, 0:128], eidf, ve, *bankfree[6])
            v = V(lambda e: e.tensor_copy(eidT, PS[6][:, 0:128]), tk, *after)
            bankfree[6] = [v]
            return v

        V(lambda e: e.memset(w32[:, :], 0.0))
        ufree = [tf[0], tf[0]]
        ve = topk(0)
        vt = turn_ids(ve)
        yfree, vgl = [], None
        for t in range(NT):
            e2 = t % 2
            for k in range(128):
                i, tok = gather(utab, eid[:, e2, k:k + 1], ve)
                v = V(lambda e, i=i, k=k, t=t, e2=e2: e.tensor_tensor_reduce(
                    out=jk2, in0=gs[i], in1=h2[:, t, :], scale=1.0, scalar=0.0, op0=ALU.mult, op1=ALU.add,
                    accum_out=act[:, e2, k:k + 1]), tok)
                gfree[i] = [v]
            ufree[e2] = v
            a = S(lambda e, e2=e2: e.activation(w_[:, e2, :], act[:, e2, :], ACT.Gelu), v)
            v = V(lambda e, e2=e2: e.tensor_tensor(w_[:, e2, :], w_[:, e2, :], gw[:, e2, :], ALU.mult), a)
            tk = TR(PS[7][:, 0:128], w_[:, e2, :], v, *bankfree[7])
            vw = V(lambda e: e.tensor_copy(w32[:, 32:].rearrange("p (t c) -> p t c", c=32)[:, :, 0], PS[7][:, 0:128]), tk)
            bankfree[7] = [vw]
            if t + 1 < NT:
                ve = topk(t + 1)
            for m in range(32):
                gg = [gather(vtab, eidT[:, 32 * j + m:32 * j + m + 1], vt) for j in range(4)]
                for hf in range(2):
                    for j in range(4):
                        i, tok = gg[j]
                        c0 = 32 + 32 * (32 * j + m) - m
                        tk = MM(PS[hf][32 * j:32 * j + 32, :], w32[:, c0:c0 + 32], gs[i][:, hf * 512:(hf + 1) * 512],
                                vw, tok, *yfree, start=(m == 0), stop=(m == 31), mark=True)
                        gfree[i] = [tk]
            if t + 1 < NT:
                vt = turn_ids(ve)
            for hf in range(2):
                v = V(lambda e, hf=hf: e.tensor_tensor(yT[:, hf * 512:(hf + 1) * 512], PS[hf][:, :],
                                                       g2b[:, hf * 512:(hf + 1) * 512], ALU.mult), tk)
            yfree = [v]
            V(lambda e, t=t: e.tensor_tensor(h3[:, t, :], h3[:, t, :], yT, ALU.add))
            a = sumsq(sm[:, 0:1], h3[:, t, :], oh[:, 0:1024], qv.tok())
            r = rstd(sm[:, 8:9], sm[:, 0:1], 1024.0, 1e-6, a)
            v = V(lambda e, t=t: e.scalar_tensor_tensor(out=h3[:, t, :], in0=h3[:, t, :], scalar=sm[:, 8:9], in1=row("fg"),
                                                        op0=ALU.mult, op1=ALU.mult), r)
            t_o = LOAD(qd, out[t * 128:(t + 1) * 128, :], h3[:, t, :], s_out, v)
        qd.items.append((qd.need([t_o]), None, None, 0))

        block = ctx.enter_context(nc.Block())

        @block.sync
        def _(e):
            qd.run(e)

        @block.scalar
        def _(e):
            qs.run(e)

        @block.gpsimd
        def _(e):
            qg.run(e)

        @block.vector
        def _(e):
            qv.run(e)

        @block.tensor
        def _(e):
            qp.run(e)


def shape_constants():
    c = {}
    c["ident"] = np.eye(128)
    inv = np.float32(1.0) / np.float32(500000.0) ** (np.arange(0, 16, 2, dtype=np.float32) / np.float32(16))
    pos = np.concatenate([np.arange(NM, NM + TX), np.arange(NM)]).astype(np.float32)
    ang = (pos[None, :] * inv.astype(np.float32)[:, None]).astype(np.float32)
    cos = np.ones((64, TA), np.float32)
    sin = np.zeros((64, TA), np.float32)
    cos[0:8] = cos[8:16] = np.cos(ang)
    sin[0:8] = sin[8:16] = np.sin(ang)
    c["cos"], c["sin"] = np.tile(cos, (2, 1)), np.tile(sin, (2, 1))
    rot = np.zeros((128, 128), np.float32)
    for b in (0, 64):
        for m in range(8):
            rot[b + m + 8, b + m] = -1.0
            rot[b + m, b + m + 8] = 1.0
    c["rot"] = rot
    j, i = np.arange(128)[:, None], np.arange(128)[None, :]
    ms = [(j == i)]
    for s in LEVELS:
        ms.append((j // (2 * s) == i // (2 * s)) & (j % (2 * s) < s) & (i % (2 * s) >= s))
    c["masks"] = np.concatenate(ms, axis=1).astype(np.float32)
    r, k = np.arange(128)[:, None], np.arange(256)[None, :]
    dist = 128 + r - k
    w = np.zeros((128, 272), np.float32)
    w[:, 0:256] = np.where((dist >= 0) & (dist < 128), 0.0, BIGNEG)
    c["wmask"] = w
    c["negm"] = np.where(i <= j, 0.0, BIGNEG)
    c["caus"] = (j <= i).astype(np.float32)
    rs = np.ones((128, TA), np.float32)
    rs[:, [0, 128, 256, 384, 512]] = 0.0
    c["reset"] = rs
    c["iota"] = np.tile(np.arange(16, dtype=np.float32), (128, 1))
    sel = np.zeros((128, 4, 128), np.float32)
    for h in range(4):
        sel[h, h, :] = 1.0
    c["sel"] = sel.reshape(128, 512)
    c["mhalf"] = np.full((128, 4), -0.5)
    return c


def colv(v):
    return np.asarray(v).reshape(-1, 128).T


def panelize(w):
    k, n = w.shape
    return np.ascontiguousarray(w.reshape(8, 128, n).transpose(1, 0, 2).reshape(128, 8 * n))


def kernel(x, meta_tokens, norm_mix_w, w_in, w_gate_up, b_gate, gla_norm_w, sinks, w_out, norm_ff_w, w_ff1, w_ff2,
           final_norm_w, c_2, ada_w_2, ada_b_2, norm1_g_2, w_in_2, conv_w_2, conv_b_2, mlstm_gate_b_2, mlstm_norm_g_2,
           lambda_q1_2, lambda_k1_2, lambda_q2_2, lambda_k2_2, diff_norm_g_2, w_out_2, norm2_g_2, peer_w_query_2,
           peer_sub_keys_2, peer_u_2, peer_v_2, final_g_2):
    import concourse.bacc as bacc
    from concourse.bass_utils import run_bass_kernel_spmd

    A = np.asarray
    f = np.float32
    c = shape_constants()
    c.update(mixw=colv(A(norm_mix_w)[0]), ffw=colv(A(norm_ff_w)[0]), n1g=colv(A(norm1_g_2)[0]),
             bgate=colv(A(b_gate)[0]), adab=colv(A(ada_b_2)[0]), ccol=colv(A(c_2)[0]))
    cw = A(conv_w_2)[0]
    c["convw"] = cw.reshape(4, 8, 128).transpose(2, 1, 0).reshape(128, 32)
    c["convb"] = colv(A(conv_b_2)[0])
    w2 = A(w_in_2)[0]
    pack = np.zeros((128, NCOL), f)
    for name, w in COLS:
        o = COFF[name][0]
        if name in c:
            pack[:, o:o + w] = c[name]
    gbv = A(mlstm_gate_b_2)[0]
    pack[0:4, COFF["gbi"][0]] = gbv[0:4]
    pack[0:4, COFF["gbf"][0]] = gbv[4:8]
    pack[0:16, COFF["wgu"][0]:COFF["wgu"][0] + 256] = A(w_gate_up)[0]
    rows = np.concatenate([A(final_norm_w), A(final_g_2), A(gla_norm_w)[0], A(mlstm_norm_g_2)[0], A(diff_norm_g_2)[0],
                           A(sinks)[0], A(lambda_q1_2)[0], A(lambda_k1_2)[0], A(lambda_q2_2)[0],
                           A(lambda_k2_2)[0]]).reshape(1, NROW)
    w1 = A(w_in)[0]
    gq, gk, gv_, gr_, glr, sq, sk_, sv_ = np.split(w1, np.cumsum([256, 256, 512, 512, 16, 512, 128]), axis=1)
    sqh = sq.reshape(1024, 8, 64)
    sqp = np.concatenate([sqh[:, [j, j + 4]].reshape(1024, 128) for j in range(4)], axis=1)
    wo = A(w_out)[0]
    woh = wo[512:].reshape(8, 64, 1024)
    wop = np.concatenate([wo[0:512]] + [woh[[j, j + 4]].reshape(128, 1024) for j in range(4)], axis=0)
    ff1, ff2, ada, wo2, wq = A(w_ff1)[0], A(w_ff2)[0], A(ada_w_2)[0], A(w_out_2)[0], A(peer_w_query_2)[0]
    cut = lambda w: [w[:, i:i + CW] for i in range(0, w.shape[1], CW)]
    pad = lambda w: np.concatenate([w, np.zeros((1024, 128 - w.shape[1]), f)], axis=1)
    P = {
        "w1": cut(gq) + cut(gk) + cut(sqp) + cut(gv_) + cut(gr_) + [np.concatenate([sk_, sv_], 1), pad(glr)],
        "wo1": cut(wop),
        "ff1": cut(ff1),
        "ff2": [ff2[q * 1024:(q + 1) * 1024, h * CW:(h + 1) * CW] for q in range(4) for h in range(4)],
        "ada": cut(ada),
        "w2": cut(w2[:, 0:1024]) + cut(w2[:, 2056:3080]) + cut(w2[:, 1024:1536]) + cut(w2[:, 3080:3592])
        + cut(w2[:, 1536:2048]) + [np.concatenate([pad(w2[:, 2048:2052]), pad(w2[:, 2052:2056])], 1)],
        "wo2": cut(wo2),
        "wq": cut(wq),
    }
    skt = A(peer_sub_keys_2)[0].reshape(16, 128, 128).transpose(2, 0, 1).reshape(128, 2048)
    ab = A(ada_b_2)[0]
    brows = np.concatenate([ab[2048:6144], A(norm2_g_2)[0]]).reshape(1, 5120)
    arrays = {"brows": brows, "packs": pack, "rows": rows, "x": A(x)[0], "meta": A(meta_tokens), "skt": skt, "utab": A(peer_u_2)[0],
              "vtab": A(peer_v_2)[0]}
    for name, ws in P.items():
        for i, w in enumerate(ws):
            arrays[f"{name}_{i}"] = panelize(w)
    arrays = {k: np.ascontiguousarray(v) for k, v in arrays.items()}

    nc = bacc.Bacc("TRN2", target_bir_lowering=False, num_devices=1)
    ap = {k: nc.dram_tensor(k, v.shape, F32, kind="ExternalInput").ap() for k, v in arrays.items()}
    o = nc.dram_tensor("out0", (TX, 1024), F32, kind="ExternalOutput").ap()
    W = {name: [ap[f"{name}_{i}"] for i in range(len(ws))] for name, ws in P.items()}
    build(nc, ap["packs"], ap["rows"], ap["brows"], ap["x"], ap["meta"], W, ap["skt"], ap["utab"], ap["vtab"], o)
    r = run_bass_kernel_spmd(nc, [arrays], core_ids=[0])
    return r.results[0]["out0"].reshape(1, TX, 1024)
```

```python
from contextlib import ExitStack

import numpy as np

import concourse.bass as bass
from concourse import mybir

F32 = mybir.dt.float32
U32 = mybir.dt.uint32
R32 = mybir.dt.float32r
ALU = mybir.AluOpType
ACT = mybir.ActivationFunctionType
AX = mybir.AxisListType.X

NT = 4
NM = 16
TX = 512
TA = TX + NM
LEVELS = (64, 32, 16, 8, 4, 2, 1)
BIGNEG = -1e30

COLS = [("ident", 128), ("mhalf", 4), ("mixw", 8), ("ffw", 8), ("n1g", 8), ("bgate", 2), ("adab", 48), ("ccol", 8),
        ("convw", 32), ("convb", 8), ("gbi", 1), ("gbf", 1), ("wgu", 256), ("cos", TA), ("sin", TA),
        ("rot", 128), ("masks", 8 * 128), ("wmask", 272), ("negm", 128), ("caus", 128), ("reset", TA),
        ("iota", 16), ("sel", 512)]
COFF = {}
_o = 0
for _n, _w in COLS:
    COFF[_n] = (_o, _w)
    _o += _w
NCOL = _o
ROWS = [("fw", 1024), ("fg", 1024), ("gnw", 128), ("mng", 512), ("dng", 128), ("sink", 8),
        ("lq1", 64), ("lk1", 64), ("lq2", 64), ("lk2", 64)]
ROFF = {}
_o = 0
for _n, _w in ROWS:
    ROFF[_n] = (_o, _w)
    _o += _w
NROW = _o

BIG1 = 19016
BIG4 = 16464
OVER = 2 * 4096 + 2 * (8 * TA + 112)
BIG2 = 16968
NP_RING = 2
CW = 256
NG = 15


class Queue:

    def __init__(self, sem):
        self.sem, self.n, self.items, self.seen = sem, 0, [], {}

    def need(self, toks):
        waits = []
        for sem, val in toks:
            if self.seen.get(sem.name, 0) < val:
                self.seen[sem.name] = val
                waits.append((sem, val))
        return waits

    def tok(self):
        return (self.sem, self.n)

    def add(self, fn, after, mark=True, sem=None, inc=1):
        waits = self.need(after)
        if sem is None and mark:
            self.n += 1
            sem = self.sem
        self.items.append((waits, fn, sem, inc))
        return (sem, self.n) if inc == 1 else None

    def run(self, eng):
        for waits, fn, sem, inc in self.items:
            for s, v in waits:
                eng.wait_ge(s, v)
            if fn is None:
                continue
            ins = fn(eng)
            if sem is not None:
                ins.then_inc(sem, inc)


def build(nc, packs, rows, brows, x, meta, W, skT, utab, vtab, out):
    ctx = ExitStack()
    with ctx:
        def sb(name, n, dt=F32, p=128):
            return ctx.enter_context(nc.sbuf_tensor(name, [p, n], dt))

        def scope():
            return ctx.enter_context(ExitStack())

        def sbs(sc, name, n, dt=F32, side="left"):
            return sc.enter_context(nc.sbuf_tensor(name, [128, n], dt, side=side))

        raw = sb("raw", NP_RING * 8 * CW)
        hres = sb("hres", 4096)
        cols = sb("cols", NCOL)
        rowb = sb("rowb", NROW)
        mod = sb("mod", 16)
        small = sb("small", 640)
        NX = 8 * TA + 112

        def open_split(tag):
            sc = scope()
            wh, wl = sbs(sc, "wh" + tag, 4096, R32, "right"), sbs(sc, "wl" + tag, 4096, R32, "right")
            xh, xl = sbs(sc, "xh" + tag, NX, R32, "right"), sbs(sc, "xl" + tag, NX, R32, "right")
            state.update(wh=wh, wl=wl, wfree=[[], []])
            return sc, xh, xl

        state = {"wi": 0, "prep": 0, "ready": None}
        g1b = cols[:, COFF["cos"][0]:COFF["cos"][0] + 1024]
        A2b = cols[:, COFF["masks"][0]:COFF["masks"][0] + 1024]
        PS = [ctx.enter_context(nc.psum_tensor(f"ps{i}", [128, 512], F32)) for i in range(8)]

        def sem(name):
            return ctx.enter_context(nc.semaphore(name))

        qv, qs, qg, qp, qd = (Queue(sem("s_" + n)) for n in ("vec", "act", "pool", "pe", "sp"))

        def V(f, *after):
            return qv.add(f, [*after, qv.tok()])

        def V2(f, *after):
            return qv.add(f, [*after, (qv.sem, qv.n - 1)])

        def S(f, *after):
            return qs.add(f, [*after, qs.tok()])

        def G(f, *after):
            return qg.add(f, [*after, qg.tok()])

        def MM(o, l, r, *after, start=True, stop=True, mark=None, share=False):
            return qp.add(lambda e: e.matmul(o, lhsT=l, rhs=r, start=start, stop=stop, skip_group_check=share),
                          after, mark=stop if mark is None else mark)

        def TR(o, i, *after, mark=True):
            k = i.shape[0]
            return qp.add(lambda e: e.transpose(o, i, ident[0:k, 0:k]), after, mark=mark)

        def fence():
            toks = [q.tok() for q in (qv, qs, qg, qp) if q.n]
            for q in (qv, qs, qg, qp):
                q.items.append((q.need([t for t in toks if t[0] is not q.sem]), None, None, 0))
            return toks

        def col(name, a=0, b=None):
            o, w = COFF[name]
            return cols[:, o + a:o + (w if b is None else b)]

        def row(name, a=0, b=None):
            o, w = ROFF[name]
            return rowb[:, o + a:o + (w if b is None else b)]

        ident = col("ident")
        dma_n = {}

        def LOAD(q, dst, src, s, *after):
            q.add(lambda e: e.dma_start(dst, src), after, sem=s, inc=16)
            dma_n[s.name] = dma_n.get(s.name, 0) + 16
            return (s, dma_n[s.name])

        s_c, s_r, s_sk, s_out = sem("s_c"), sem("s_r"), sem("s_sk"), sem("s_out")
        s_pan = [sem(f"s_pan{i}") for i in range(NP_RING)]
        h3 = hres[:, :].rearrange("p (t d) -> p t d", t=NT)
        splits, xh_, xl_ = open_split("a")
        sb1 = scope()
        big = sbs(sb1, "big1", BIG1)
        mrow = big[0:NM, 16384:16384 + 1024]
        cut0 = COFF["convw"][0]
        t_c = LOAD(qs, cols[:, 0:cut0], packs[:, 0:cut0], s_c)
        s_m, s_c2 = sem("s_m"), sem("s_c2")
        t_m = LOAD(qs, mrow, meta, s_m)
        t_x = [LOAD(qd, h3[:, t, :], x[t * 128:(t + 1) * 128, :], sem(f"s_x{t}")) for t in range(NT)]

        order = [("w1", i) for i in range(10)] + [("wo1", i) for i in range(4)]
        ffs = []
        for q in range(4):
            ffs += [("ff1", 4 * q + i) for i in range(4)] + [("ff2", 4 * q + i) for i in range(4)]
        for i, f in enumerate(ffs):
            order += ([("ada", i)] if i < 24 else []) + [f]
        order += [("w2", i) for i in range(15)] + [("wo2", i) for i in range(4)] + [("wq", i) for i in range(8)]
        loaded = {}

        def issue(n, *after):
            name, i = order[n]
            slot = n % NP_RING
            w = W[name][i].shape[1]
            loaded[n] = LOAD(qd, raw[:, slot * 2048:slot * 2048 + w], W[name][i], s_pan[slot], *after)

        for n in range(NP_RING):
            issue(n)

        def prep():
            while state["ready"] is None and state["prep"] < len(order):
                n = state["prep"]
                state["prep"] += 1
                name, i = order[n]
                w = W[name][i].shape[1]
                r = raw[:, (n % NP_RING) * 2048:(n % NP_RING) * 2048 + w]
                if name == "ada":
                    toks = [ada_acc(i, r.rearrange("p (k c) -> p k c", k=8), loaded[n])]
                else:
                    u = state["wi"] % 2
                    state["wi"] += 1
                    hi, lo = (state[x][:, u * 2048:u * 2048 + w] for x in ("wh", "wl"))
                    a = S(lambda e, hi=hi, r=r: e.activation(hi, r, ACT.Copy), loaded[n], *state["wfree"][u])
                    v = V(lambda e, hi=hi, lo=lo, r=r: e.tensor_tensor(lo, r, hi.bitcast(F32), ALU.subtract), a,
                          *state["wfree"][u])
                    toks = [a, v]
                    state["ready"] = (name, i, u, toks, hi.rearrange("p (k c) -> p k c", k=8),
                                      lo.rearrange("p (k c) -> p k c", k=8))
                if n + NP_RING < len(order):
                    issue(n + NP_RING, *toks)

        def panel(name, i, last=False):
            prep()
            nm, j, u, toks, hi, lo = state["ready"]
            assert (nm, j) == (name, i), (nm, j, name, i)
            state["ready"] = None
            if not last:
                prep()
            return (hi, lo), toks, u

        def release(u, tok):
            state["wfree"][u] = [tok]

        def MM3(o, parts, tp, *after, each=None):
            for k, ((lh, ll), (rh, rl)) in enumerate(parts):
                f = ([*after] if k == 0 else []) + ([each[k]] if each else [])
                MM(o, lh, rh, *tp, *f, start=(k == 0), stop=False)
                MM(o, ll, rh, start=False, stop=False)
                tk = MM(o, lh, rl, start=False, stop=(k == len(parts) - 1))
            return tk

        sm = small
        mh = col("mhalf")

        def rstd(dst, ss, d, eps, *after):
            p, n = ss.shape[0], ss.shape[1]
            t = V(lambda e: e.tensor_scalar(ss, ss, 1.0 / d, eps, ALU.mult, ALU.add), *after)
            return G(lambda e: e.tensor_tensor(dst, ss, mh[0:p, 0:n], ALU.pow), t, t_c)

        def sumsq(dst, src, junk, *after):
            return S(lambda e: e.activation(junk, src, ACT.Square, accum_out=dst), *after)

        bankfree = [[] for _ in range(8)]

        xh3 = xh_[:, 0:8 * TA].rearrange("p (k c) -> p k c", k=8)
        xl3 = xl_[:, 0:8 * TA].rearrange("p (k c) -> p k c", k=8)

        def st_sum(junk):
            def f(t):
                sumsq(sm[:, t:t + 1], h3[:, t, :], junk, qv.tok())
            return f

        def rstd_of(t, eps):
            ss, d = sm[:, t:t + 1], sm[:, 8 + t:9 + t]
            t_ = V(lambda e: e.tensor_scalar(ss, ss, 1.0 / 1024.0, eps, ALU.mult, ALU.add), qs.tok())
            return G(lambda e: e.tensor_tensor(d, ss, mh[:, 0:1], ALU.pow), t_)

        def st_scale(rows3, eps):
            def f(t):
                r = rstd_of(t, eps)
                v_rows[t] = V(lambda e: e.tensor_scalar(rows3[:, t, :], h3[:, t, :], sm[:, 8 + t:9 + t], None, ALU.mult), r)
            return f

        def st_turn(src3, scale, bias, q2):
            def f(t):
                for g in range(2):
                    b = 6 + g
                    for k in range(4):
                        tk = TR(PS[b][:, k * 128:(k + 1) * 128], src3[:, t, (4 * g + k) * 128:(4 * g + k + 1) * 128],
                                v_rows[t], *bankfree[b], mark=(k == 3))
                    p = PS[b][:, :].rearrange("p (k c) -> p k c", k=4)
                    if scale is not None:
                        q = q2[:, g * 512:(g + 1) * 512].rearrange("p (k c) -> p k c", k=4)
                        sb_ = scale[:, 4 * g:4 * g + 4].rearrange("p (k o) -> p k o", o=1).to_broadcast([128, 4, 128])
                        tk = V(lambda e, q=q, p=p, sb_=sb_: e.tensor_tensor(q, p, sb_, ALU.mult), tk, qs.tok())
                        bankfree[b] = [tk]
                        p = q
                        if bias is not None:
                            bb_ = bias[:, 4 * g:4 * g + 4].rearrange("p (k o) -> p k o", o=1).to_broadcast([128, 4, 128])
                            tk = V(lambda e, q=q, bb_=bb_: e.tensor_tensor(q, q, bb_, ALU.add))
                    turned[g] = (p, tk)
            return f

        def st_parts(in_psum):
            def f(t):
                aa = []
                hl = [[x[:, 4 * g:4 * g + 4, t * 128:(t + 1) * 128] for x in (xh3, xl3)] for g in range(2)]
                for g in range(2):
                    p, tk = turned[g]
                    aa.append(S(lambda e, h=hl[g][0], p=p: e.activation(h, p, ACT.Copy), tk))
                for g in range(2):
                    v = (V2 if g else V)(lambda e, h=hl[g][0], l=hl[g][1], p=turned[g][0]: e.tensor_tensor(l, p, h.bitcast(F32),
                                                                                           ALU.subtract), aa[g])
                    if in_psum:
                        bankfree[6 + g] = [v]
            return f

        v_rows, turned = {}, {}

        def step(stages, t):
            for i in reversed(range(len(stages))):
                if 0 <= t - i < NT:
                    stages[i](t - i)

        xs3 = big[:, 8192:12288].rearrange("p (t d) -> p t d", t=NT)
        junk = big[:, 12288:13312]
        zpad = big[:, 14464:14576]
        zv = V(lambda e: e.memset(zpad, 0.0))
        hp, lp = xh_[:, 8 * TA:NX], xl_[:, 8 * TA:NX]
        S(lambda e: e.activation(hp, zpad, ACT.Copy), zv)
        S(lambda e: e.activation(lp, zpad, ACT.Copy))
        for q in (qv, qs, qg, qp):
            q.items.append((q.need([t_c]), None, None, 0))

        def st_first(t):
            sumsq(sm[:, t:t + 1], h3[:, t, :], junk, t_x[t])

        stages_A = [st_first, st_scale(xs3, 1e-5), st_turn(xs3, col("mixw"), None, big[:, 13312:14336]), st_parts(False)]
        for t in range(NT + 3):
            step(stages_A, t)
            if t == 0:
                t_c2 = LOAD(qs, cols[:, cut0:NCOL], packs[:, cut0:NCOL], s_c2)
                t_r = LOAD(qs, rowb[:, :], rows.to_broadcast([128, NROW]), s_r)
            if t == 3:
                prep()
        ssm = sm[0:NM, 4:5]
        am = sumsq(ssm, mrow, junk[0:NM, :], t_m)
        rm = rstd(sm[0:NM, 12:13], ssm, 1024.0, 1e-5, am)
        tm = V(lambda e: e.tensor_scalar(mrow, mrow, sm[0:NM, 12:13], None, ALU.mult), rm)
        for k in range(8):
            tk = TR(PS[3][:, k * NM:(k + 1) * NM], mrow[:, k * 128:(k + 1) * 128], tm, t_c)
        mw = col("mixw").rearrange("p (k o) -> p k o", o=1).to_broadcast([128, 8, NM])
        qm = big[:, 14336:14464].rearrange("p (k c) -> p k c", k=8)
        v = V(lambda e: e.tensor_tensor(qm, PS[3][:, 0:128].rearrange("p (k c) -> p k c", k=8), mw, ALU.mult), tk)
        hm, lm = xh3[:, :, TX:TA], xl3[:, :, TX:TA]
        a = S(lambda e: e.activation(hm, qm, ACT.Copy), v)
        V(lambda e: e.tensor_tensor(lm, qm, hm.bitcast(F32), ALU.subtract), a)
        fence()

        off, lim = [0], [BIG1]

        def carve(n, p=128):
            o = off[0]
            off[0] += n
            assert off[0] <= lim[0], off[0]
            return big[0:p, o:o + n]

        mixT = carve(4096).rearrange("p (k c) -> p k c", k=8)
        gqT = carve(1024).rearrange("p (a c) -> p a c", a=2)
        gkT = carve(1024).rearrange("p (a c) -> p a c", a=2)
        gkm = carve(32).rearrange("p (a c) -> p a c", a=2)
        lrT = carve(TA, 16)
        sqT = carve(2048).rearrange("p (a c) -> p a c", a=4)
        skT1 = carve(TA)
        gv = carve(2048).rearrange("p (t c) -> p t c", t=NT)
        gvm = carve(512, NM)
        gr = carve(2048).rearrange("p (t c) -> p t c", t=NT)
        sv = carve(512).rearrange("p (t c) -> p t c", t=NT)
        svm = carve(128, NM)
        mark1 = off[0]
        rr = {"i": 0}

        state["banks"] = tuple(range(8))

        def bank(banks=None):
            banks = banks or state["banks"]
            b = banks[rr["i"] % len(banks)]
            rr["i"] += 1
            return b

        def projT(pv, c, m, tp, outs, scale=None, rows=None):
            for (a, z, dst) in outs:
                b = bank()
                tk = MM3(PS[b][0:m, 0:z - a], [(tuple(w[:, k, c:c + m] for w in pv), (xh3[:, k, a:z], xl3[:, k, a:z]))
                                               for k in range(8)], tp, *bankfree[b])
                src = PS[b][0:rows or m, 0:z - a]
                if scale is None:
                    v = V(lambda e, dst=dst, src=src: e.tensor_copy(dst, src), tk)
                else:
                    v = V(lambda e, dst=dst, src=src: e.tensor_scalar(dst, src, scale, None, ALU.mult), tk)
                bankfree[b] = [v]
            return tk, v

        def xcol(x, k, a):
            return x[:, k * TA + a:k * TA + a + 128]

        def projR(pv, c, m, tp, outs, fn=None, take=0):
            for (a, z, dst) in outs:
                b = bank()
                tk = MM3(PS[b][:, 0:m], [((xcol(xh_, k, a), xcol(xl_, k, a)), tuple(w[:, k, c:c + m] for w in pv))
                                         for k in range(8)], tp, *bankfree[b])
                v = S(lambda e, dst=dst, src=PS[b][0:z, take:m]: e.activation(dst, src, fn or ACT.Copy), tk)
                bankfree[b] = [v]
            return tk, v

        def rowsT(dst, c, n=CW):
            return [(t * 128, 128, dst[:, t, c:c + n]) for t in range(NT)]

        for b in range(8):
            bankfree[b] = []
        for q in (qv, qs, qg, qp):
            q.items.append((q.need([t_c2, t_r]), None, None, 0))
        pv, tp, n = panel("w1", 0)
        tk, v = projT(pv, 0, 128, tp, [(0, TX, lrT[:, 0:TX]), (TX, TA, lrT[:, TX:TA])], rows=16)
        release(n, tk)
        v_lr = v
        pv, tp, n = panel("w1", 1)
        for a in range(2):
            tk, v = projT(pv, 128 * a, 128, tp, [(0, TX, gqT[:, a, :])], scale=0.125)
        release(n, tk)
        scr = big[:, 0:4096]
        zb = scr[:, 0:2 * TA].rearrange("p (a c) -> p a c", a=2)
        za = scr[:, 2 * TA:4 * TA].rearrange("p (a c) -> p a c", a=2)
        rc = [scr[:, 4 * TA:4 * TA + 528], scr[:, 4 * TA + 528:4 * TA + 1056]]
        bx = carve(1024).rearrange("p (a c) -> p a c", a=2)
        bm = carve(32).rearrange("p (a c) -> p a c", a=2)
        for a in range(2):
            for c0, c1 in ((0, TX), (TX, TA)):
                b = bank()
                tk = MM(PS[b][:, 0:c1 - c0], cols[0:16, COFF["wgu"][0] + 128 * a:COFF["wgu"][0] + 128 * a + 128],
                        lrT[:, c0:c1], v_lr, *bankfree[b])
                t = V(lambda e, a=a, b=b, c0=c0, c1=c1: e.tensor_scalar(zb[:, a, c0:c1], PS[b][:, 0:c1 - c0],
                                                                        col("bgate", a, a + 1), None, ALU.add), tk)
                bankfree[b] = [t]
        t_lr = [tk]
        S(lambda e: e.activation(za, zb, ACT.Abs), t)
        S(lambda e: e.activation(za, za, ACT.Exp, scale=-1.0))
        t_z0 = S(lambda e: e.activation(za, za, ACT.Ln, bias=1.0))
        pv, tp, n = panel("w1", 2)
        for a in range(2):
            tk, v = projT(pv, 128 * a, 128, tp, [(0, TX, gkT[:, a, :]), (TX, TA, gkm[:, a, :])])
        release(n, tk)
        V(lambda e: e.scalar_tensor_tensor(out=zb, in0=zb, scalar=0.0, in1=za, op0=ALU.min, op1=ALU.subtract), t_z0)
        for a in range(2):
            V(lambda e, a=a: e.tensor_tensor_scan(bx[:, a, :], col("reset", 0, TX), zb[:, a, 0:TX], 0.0, ALU.mult, ALU.add))
            V(lambda e, a=a: e.tensor_tensor_scan(bm[:, a, :], col("reset", TX, TA), zb[:, a, TX:TA], 0.0, ALU.mult,
                                                  ALU.add))

        def rope(xap, a, z, i, *after):
            b = bank()
            tk = MM(PS[b][:, 0:z - a], col("rot"), xap, *after, *bankfree[b])
            w = rc[i % 2][:, 0:z - a]
            v = V(lambda e: e.tensor_tensor(w, PS[b][:, 0:z - a], col("sin", a, z), ALU.mult), tk)
            bankfree[b] = [v]
            V2(lambda e: e.tensor_tensor(xap, xap, col("cos", a, z), ALU.mult), tk)
            V(lambda e: e.tensor_tensor(xap, xap, w, ALU.add))

        todo = []
        for i in range(2):
            pv, tp, n = panel("w1", 3 + i)
            for a in range(2):
                tk, v = projT(pv, 128 * a, 128, tp, [(0, TX, sqT[:, 2 * i + a, :])])
                todo.append((sqT[:, 2 * i + a, :], 0, TX, v))
            release(n, tk)
        pv, tp, n = panel("w1", 5)
        tk, v = projT(pv, 0, 128, tp, [(0, TX, skT1[:, 0:TX]), (TX, TA, skT1[:, TX:TA])])
        todo += [(skT1[:, 0:TX], 0, TX, v), (skT1[:, TX:TA], TX, TA, v)]
        tk, v = projR(pv, 0, CW, tp, rowsT(sv, 0, 128) + [(TX, NM, svm)], take=128)
        release(n, tk)
        for i in range(2):
            pv, tp, n = panel("w1", 6 + i)
            tk, v = projR(pv, 0, CW, tp, rowsT(gv, CW * i) + [(TX, NM, gvm[:, CW * i:CW * i + CW])])
            release(n, tk)
            for _ in range(2):
                x_, a, z, v = todo.pop(0)
                rope(x_, a, z, len(todo), v)
        for i in range(2):
            pv, tp, n = panel("w1", 8 + i, last=(i == 1))
            if i == 0:
                for _ in range(2):
                    x_, a, z, v = todo.pop(0)
                    rope(x_, a, z, len(todo), v)
            tk, vg = projR(pv, 0, CW, tp, rowsT(gr, CW * i), fn=ACT.Silu)
            release(n, tk)
        gnw = row("gnw").rearrange("p (o c) -> p o c", o=1).to_broadcast([128, 16, 128])
        grv = gr.rearrange("p t (h c) -> p (t h) c", h=4)
        V(lambda e: e.tensor_tensor(grv, grv, gnw, ALU.mult), vg, t_r)
        fence()
        splits.close()
        smix = scope()
        over = sbs(smix, "over1", OVER, F32, "right")
        xT = over[:, 0:8 * TA]
        ooff = [8 * TA]

        def carve_o(n, p=128):
            o = ooff[0]
            ooff[0] += n
            assert ooff[0] <= OVER
            return over[0:p, o:o + n]

        for b in range(8):
            bankfree[b] = []

        def beside(*gens):
            gens = list(gens)
            while gens:
                for g in list(gens):
                    try:
                        next(g)
                    except StopIteration:
                        gens.remove(g)

        Qs = carve_o(1024).rearrange("p (a c) -> p a c", a=2)
        Ks = carve_o(1024).rearrange("p (a c) -> p a c", a=2)
        Qd, Kd = (carve_o(1024).rearrange("p (a c) -> p a c", a=2) for _ in range(2))
        Qs2 = carve_o(1024).rearrange("p (a c) -> p a c", a=2)
        A = carve_o(2048)
        khm = carve_o(256, NM)
        St = carve_o(2048).rearrange("p (c a v) -> p c a v", c=4, a=2)
        def gla():
            G(lambda e: e.memset(A, 0.0))
            t_z = G(lambda e: e.memset(St, 0.0))
            last = qv.tok()
            mm = last
            Df, Ef = xT[:, 0:1024], xT[:, 2 * TA:2 * TA + 1024]
            Efv = Ef.rearrange("p (a c) -> p a c", a=2)
            ex = last
            mmp = [last, last]

            def decay(s, ex, *after):
                bxf = bx.rearrange("p a c -> p (a c)").rearrange("p (n s) -> p n s", s=2 * s)
                ref = bxf[:, :, s - 1:s].to_broadcast([128, 512 // s, 2 * s])
                d3, e3 = (x.rearrange("p (n s) -> p n s", s=2 * s) for x in (Df, Ef))
                d = G(lambda e: e.tensor_tensor(d3, bxf, ref, ALU.subtract), ex)
                S(lambda e: e.activation(e3[:, :, 0:s], d3[:, :, 0:s], ACT.Exp, scale=-1.0 / 16.0), d, *after)
                return S(lambda e: e.activation(e3[:, :, s:2 * s], d3[:, :, s:2 * s], ACT.Exp, scale=1.0 / 16.0))

            def level_in(li, ex):
                if li == 0:
                    q_in, k_in, t_q = gqT, gkT, [last, t_z]
                else:
                    q_in, k_in = (Qs, Ks) if li % 2 else (Qd, Kd)
                    t_q = [V(lambda e, q_in=q_in: e.tensor_tensor(q_in, gqT, Efv, ALU.mult), ex, mmp[li % 2]),
                           G(lambda e, k_in=k_in: e.tensor_tensor(k_in, gkT, Efv, ALU.mult), ex, mmp[li % 2])]
                if li < len(LEVELS):
                    ex = decay(LEVELS[li], ex, *t_q)
                return q_in, k_in, t_q, ex

            q_in, k_in, t_q, ex = level_in(0, ex)
            for li in range(len(LEVELS) + 1):
                mms = []
                for c in range(NT):
                    cc, par = c // 2, c % 2
                    p0 = 64 * par
                    for i in range(4):
                        ci, h = 2 * cc + i // 2, 2 * (i % 2) + par
                        mm = MM(PS[c][:, i * 128:(i + 1) * 128], k_in[p0:p0 + 64, h // 2, ci * 128:(ci + 1) * 128],
                                q_in[p0:p0 + 64, h // 2, ci * 128:(ci + 1) * 128], *t_q, *bankfree[c])
                    mms.append(mm)
                mmp[li % 2] = mm
                if li < len(LEVELS):
                    q_in, k_in, t_q, ex = level_in(li + 1, ex)
                yield
                for c in range(NT):
                    mk = cols[:, COFF["masks"][0] + 128 * li:COFF["masks"][0] + 128 * (li + 1)].bitcast(U32)\
                        .rearrange("p (o c) -> p o c", o=1).to_broadcast([128, 4, 128])
                    v = (V2 if c else V)(lambda e, c=c, mk=mk: e.copy_predicated(
                        A[:, c * 512:(c + 1) * 512].rearrange("p (h i) -> p h i", h=4), mk,
                        PS[c][:, :].rearrange("p (h i) -> p h i", h=4)), mms[c], t_z)
                    bankfree[c] = [v]
            dec3 = sm[:, 16:24].rearrange("p (a c) -> p a c", a=2)
            bc = bx.rearrange("p a c -> p (a c)").rearrange("p (n s) -> p n s", s=128)
            d = V(lambda e: e.tensor_tensor(Df.rearrange("p (n s) -> p n s", s=128),
                                            bc[:, :, 127:128].to_broadcast([128, 8, 128]), bc, ALU.subtract), ex, qg.tok())
            d2 = V(lambda e: e.tensor_tensor(Qs2[:, :, 0:NM], bm[:, :, NM - 1:NM].to_broadcast([128, 2, NM]), bm, ALU.subtract))
            ex = S(lambda e: e.activation(Ef, Df, ACT.Exp, scale=1.0 / 16.0), d, qg.tok())
            ex2 = S(lambda e: e.activation(Qs2[:, :, 0:NM], Qs2[:, :, 0:NM], ACT.Exp, scale=1.0 / 16.0), d2)
            t_dec = S(lambda e: e.activation(sm[:, 16:24], bc[:, :, 127], ACT.Exp, scale=1.0 / 16.0))
            V(lambda e: e.tensor_tensor(Ks.rearrange("p a c -> p (a c)"), gkT.rearrange("p a c -> p (a c)"), Ef, ALU.mult), ex, mm)
            t_km = V(lambda e: e.tensor_tensor(gkm, gkm, Qs2[:, :, 0:NM], ALU.mult), ex2)
            ex = S(lambda e: e.activation(Qs2.rearrange("p a c -> p (a c)"), bx.rearrange("p a c -> p (a c)"), ACT.Exp,
                                          scale=1.0 / 16.0), t_km)
            yield
            t_qb = V(lambda e: e.tensor_tensor(Qs2, Qs2, gqT, ALU.mult), ex)
            khv = Qs.rearrange("p a c -> p (a c)").rearrange("p (c d) -> p c d", c=4)
            t_kh = []
            for c in range(4):
                dst = khm if c == 0 else khv[:, c - 1, :]
                w = NM if c == 0 else 128
                for a in range(2):
                    src = gkm[:, a, :] if c == 0 else Ks[:, a, (c - 1) * 128:c * 128]
                    tk = TR(PS[c][0:w, a * 128:(a + 1) * 128], src, t_km, *bankfree[c])
                v = V(lambda e, dst=dst, c=c, w=w: e.tensor_copy(dst, PS[c][0:w, 0:256]), tk)
                bankfree[c] = [v]
                t_kh.append(v)
                yield
            for c in range(NT):
                kk = khm if c == 0 else khv[:, c - 1, :]
                vv = gvm if c == 0 else gv[:, c - 1, :]
                for a in range(2):
                    tk = MM(PS[c][:, a * 256:(a + 1) * 256], kk[:, a * 128:(a + 1) * 128], vv[:, a * 256:(a + 1) * 256],
                            t_kh[c], *bankfree[c])
                for a in range(2):
                    for u in range(2):
                        p0 = 64 * u
                        blk = PS[c][p0:p0 + 64, a * 256 + u * 128:a * 256 + (u + 1) * 128]
                        dst = St[p0:p0 + 64, c, a, u * 128:(u + 1) * 128]
                        if c == 0:
                            t_S = V(lambda e, dst=dst, blk=blk: e.tensor_copy(dst, blk), tk)
                        else:
                            t_S = V(lambda e, dst=dst, blk=blk, a=a, u=u, p0=p0, c=c: e.scalar_tensor_tensor(
                                out=dst, in0=St[p0:p0 + 64, c - 1, a, u * 128:(u + 1) * 128],
                                scalar=dec3[p0:p0 + 64, a, c - 1:c], in1=blk, op0=ALU.mult, op1=ALU.add), tk, t_dec)
                bankfree[c] = [t_S]
                yield
            ss4, r4 = sm[:, 32:48], sm[:, 48:64]
            xfree = [qv.tok()]
            for c in range(NT):
                b = c % 2
                o = xT[:, b * 512:(b + 1) * 512]
                sq = xT[:, 1056 + b * 512:1056 + (b + 1) * 512]
                for a in range(2):
                    MM(PS[b][:, a * 256:(a + 1) * 256], Qs2[:, a, c * 128:(c + 1) * 128], St[:, c, a, :], t_qb, t_S,
                       *bankfree[b], stop=False)
                    for u in range(2):
                        h = 2 * a + u
                        blk = ((c // 2) * 2 + u) * 4 + (c % 2) * 2 + a
                        tk = MM(PS[b][:, h * 128:(h + 1) * 128], A[:, blk * 128:(blk + 1) * 128],
                                gv[:, c, h * 128:(h + 1) * 128], start=False, stop=(u == 1), mark=True)
                a = S(lambda e, b=b, sq=sq: e.activation(sq, PS[b][:, :], ACT.Square), tk, *xfree)
                v = V(lambda e, c=c, b=b, o=o: e.tensor_tensor(o, PS[b][:, :], gr[:, c, :], ALU.mult), a,
                      *(ofree[b] if c >= 2 else []))
                V(lambda e, c=c, sq=sq: e.tensor_reduce(ss4[:, 4 * c:4 * c + 4], sq.rearrange("p (h v) -> p h v", h=4), AX,
                                                        ALU.add), a)
                bankfree[b] = [qv.tok()]
                r = rstd(r4[:, 4 * c:4 * c + 4], ss4[:, 4 * c:4 * c + 4], 128.0, 1e-5)
                yield
                v = V(lambda e, c=c, o=o: e.tensor_tensor(
                    o.rearrange("p (h v) -> p h v", h=4), o.rearrange("p (h v) -> p h v", h=4),
                    r4[:, 4 * c:4 * c + 4].rearrange("p (h o) -> p h o", o=1).to_broadcast([128, 4, 128]), ALU.mult), r)
                xfree = [v]
                b2 = 2 + b
                for h in range(4):
                    tk = TR(PS[b2][:, h * 128:(h + 1) * 128], o[:, h * 128:(h + 1) * 128], v, *bankfree[b2], mark=(h == 3))
                ofree[b] = [tk]
                cp = S(lambda e, b2=b2, c=c: e.activation(mixT[:, 0:4, c * 128:(c + 1) * 128],
                                                          PS[b2][:, :].rearrange("p (h v) -> p h v", h=4), ACT.Copy), tk)
                bankfree[b2] = [cp]
                yield

        Sg = [xT[:, 4 * TA:4 * TA + 1088].rearrange("p (h k) -> p h k", h=4),
              carve(1088).rearrange("p (h k) -> p h k", h=4)]
        PTg = [[xT[:, 3200:3712], xT[:, 3712:4224], lrT], [carve(512), carve(512), carve(512, 16)]]

        def swa():
            t_rope = qv.tok()
            gens = [swa_half(0, t_rope), swa_half(1, t_rope)]
            while gens:
                for q in list(gens):
                    if next(q, "end") == "end":
                        gens.remove(q)
                yield

        def swa_half(g, t_rope):
            Sa, PT = Sg[g], PTg[g]
            B = (4 + 2 * g, 5 + 2 * g)
            p0 = 64 * g
            sk4 = row("sink")[:, 4 * g:4 * g + 4]
            mx, ng, Z, es = (sm[:, 64 + 16 * g + 4 * i:68 + 16 * g + 4 * i] for i in range(4))
            ptf = [t_lr[0]]
            saf = t_rope
            for n in range(NT):
                w0 = 0 if n else 128
                for j in range(4):
                    b = B[j % 2]
                    q = sqT[p0:p0 + 64, j, n * 128:(n + 1) * 128]
                    MM(PS[b][:, 256:272], q, skT1[p0:p0 + 64, TX:TA], t_rope, *bankfree[b], mark=False)
                    tk = MM(PS[b][:, w0:256], q, skT1[p0:p0 + 64, (n - 1) * 128 + w0:(n + 1) * 128])
                    v = V(lambda e, b=b, j=j, w0=w0: e.scalar_tensor_tensor(
                        out=Sa[:, j, w0:272], in0=PS[b][:, w0:272], scalar=0.125, in1=col("wmask", w0, 272),
                        op0=ALU.mult, op1=ALU.add), tk, saf)
                    bankfree[b] = [v]
                    if j == 1:
                        yield
                V(lambda e, w0=w0: e.tensor_reduce(mx, Sa[:, :, w0:272], AX, ALU.max))
                V(lambda e: e.tensor_tensor(mx, mx, sk4, ALU.max))
                V(lambda e: e.tensor_scalar(ng, mx, -1.0, None, ALU.mult))
                v = V(lambda e: e.tensor_tensor(es, sk4, mx, ALU.subtract))
                for j in range(4):
                    S(lambda e, j=j, w0=w0: e.activation(Sa[:, j, w0:272], Sa[:, j, w0:272], ACT.Exp, bias=ng[:, j:j + 1],
                                                         accum_out=Z[:, j:j + 1]), v)
                a = S(lambda e: e.activation(es, es, ACT.Exp))
                yield
                V(lambda e: e.tensor_tensor(Z, Z, es, ALU.add), a)
                V(lambda e: e.reciprocal(Z, Z))
                v = V(lambda e, w0=w0: e.tensor_tensor(
                    Sa[:, :, w0:272], Sa[:, :, w0:272],
                    Z.rearrange("p (h o) -> p h o", o=1).to_broadcast([128, 4, 272 - w0]), ALU.mult))
                yield
                blocks = [(0, 0, 128)] * (n > 0) + [(1, 128, 128), (2, 256, NM)]
                tv = {}
                for (bi, c0, w) in blocks:
                    b = B[bi % 2]
                    for j in range(4):
                        tk = TR(PS[b][0:w, j * 128:(j + 1) * 128], Sa[:, j, c0:c0 + w], v, *bankfree[b], mark=(j == 3))
                    dst = PT[bi][0:w, 0:512]
                    cp = S(lambda e, dst=dst, b=b, w=w: e.activation(dst, PS[b][0:w, :], ACT.Copy), tk, *ptf)
                    bankfree[b] = [cp]
                    tv[bi] = cp
                    saf = tk
                yield
                b = B[1]
                for i, (bi, c0, w) in enumerate(blocks):
                    vs = svm if bi == 2 else sv[:, n - 1 + bi, :]
                    tk = MM(PS[b][p0:p0 + 64, :], vs[:, p0:p0 + 64], PT[bi][0:w, 0:512],
                            tv[bi], *bankfree[b], start=(i == 0), stop=(i == len(blocks) - 1))
                ptf = [tk]
                cp = S(lambda e, n=n, b=b: e.activation(mixT[p0:p0 + 64, 4:8, n * 128:(n + 1) * 128],
                                                        PS[b][p0:p0 + 64, :].rearrange("p (j c) -> p j c", j=4), ACT.Copy), tk)
                bankfree[b] = [cp]
                yield

        ofree = [[], []]
        beside(gla(), swa())
        fence()

        smix.close()
        splits, xh_, xl_ = open_split("b")
        xh3 = xh_[:, 0:8 * TA].rearrange("p (k c) -> p k c", k=8)
        xl3 = xl_[:, 0:8 * TA].rearrange("p (k c) -> p k c", k=8)
        for b in range(8):
            bankfree[b] = []
        prep()
        t_m = []
        for k in range(8):
            h, l, m = xh3[:, k, 0:TX], xl3[:, k, 0:TX], mixT[:, k, :]
            a = S(lambda e, h=h, m=m: e.activation(h, m, ACT.Copy))
            t_m.append(V(lambda e, h=h, l=l, m=m: e.tensor_tensor(l, m, h.bitcast(F32), ALU.subtract), a))

        def out_proj(name, gate, tmp, stages, each=None):
            for qc in range(4):
                if qc == 3:
                    state["banks"] = (0, 1, 2, 3, 4, 5)
                pv, tp, n = panel(name, qc)
                for t in range(NT):
                    b = bank()
                    tk = MM3(PS[b][:, 0:CW], [((xh3[:, k, t * 128:(t + 1) * 128], xl3[:, k, t * 128:(t + 1) * 128]),
                                               tuple(w[:, k, :] for w in pv)) for k in range(8)], tp, *bankfree[b], each=each)
                    hs = h3[:, t, qc * CW:(qc + 1) * CW]
                    if gate is None:
                        v = V(lambda e, hs=hs, b=b: e.tensor_tensor(hs, hs, PS[b][:, 0:CW], ALU.add), tk)
                    else:
                        v = V(lambda e, b=b, qc=qc: e.tensor_tensor(tmp, PS[b][:, 0:CW], gate[:, qc * CW:(qc + 1) * CW],
                                                                    ALU.mult), tk)
                        V(lambda e, hs=hs: e.tensor_tensor(hs, hs, tmp, ALU.add))
                    bankfree[b] = [v]
                    if qc == 3:
                        step(stages, t)
                release(n, tk)
            for t in range(NT, NT + len(stages) - 1):
                step(stages, t)
            state["banks"] = tuple(range(8))

        csil = sm[:, 96:104]
        t_cs = S(lambda e: e.activation(csil, col("ccol"), ACT.Silu), t_c)
        acc = [col("reset", 0, 256), col("reset", 256, 512)]
        ones = col("rot")
        accfree = [[], []]
        pending = []
        V(lambda e: e.memset(ones, 1.0))
        def ada_acc(i, pv, tp):
            a = acc[i % 2]
            V(lambda e: e.tensor_scalar(a, pv[:, 0, :], csil[:, 0:1], None, ALU.mult), tp, t_cs, *accfree[i % 2])
            for k in range(1, 8):
                v = V(lambda e, k=k: e.scalar_tensor_tensor(out=a, in0=pv[:, k, :], scalar=csil[:, k:k + 1], in1=a,
                                                            op0=ALU.mult, op1=ALU.add))
            pending.append((i, v))
            return v

        xs1 = big[:, 0:4096].rearrange("p (t d) -> p t d", t=NT)
        q1, j1 = big[:, 4096:5120], big[:, 5120:6144]
        out_proj("wo1", None, None, [st_sum(j1), st_scale(xs1, 1e-5), st_turn(xs1, col("ffw"), None, q1), st_parts(False)],
                 each=t_m)
        fence()
        sb1.close()
        g2b = sb("g2b", 1024)
        B2b = sb("B2b", 1024)
        sff = scope()
        AH = sbs(sff, "ah", 4096, R32)[:, :].rearrange("p (f c) -> p f c", f=8)
        AL = sbs(sff, "al", 4096, R32)[:, :].rearrange("p (f c) -> p f c", f=8)
        fbig = sbs(sff, "fbig", 8768)

        n2row = fbig[:, 640:1664]
        sqt = [fbig[:, 1664:2176], fbig[:, 2176:2688]]
        sqq = [fbig[:, 2688:3200], fbig[:, 3200:3712]]
        xs3b = fbig[:, 3712:3712 + 4096].rearrange("p (t d) -> p t d", t=NT)
        jk = fbig[:, 1664:2688]
        s_b = sem("s_b")
        for i, dst in enumerate((g1b, B2b[:, :], A2b, g2b[:, :], n2row)):
            t_b = LOAD(qs, dst, brows[:, i * 1024:(i + 1) * 1024].to_broadcast([128, 1024]), s_b, qs.tok())

        def ada_sums():
            while pending:
                i, v = pending.pop(0)
                a = acc[i % 2]
                if i < 8:
                    for j in range(2):
                        tk = MM(PS[7][:, j:j + 1], a[:, j * 128:(j + 1) * 128], ones[:, 0:1], v, *bankfree[7])
                    v = V(lambda e, i=i: e.tensor_tensor(mod[:, 2 * i:2 * i + 2], PS[7][:, 0:2],
                                                         col("adab", 2 * i, 2 * i + 2), ALU.add), tk)
                else:
                    tk = MM(PS[7][:, 0:CW], ones, a, v, *bankfree[7])
                    c = (i % 4) * CW
                    d = (g1b, B2b, A2b, g2b)[i // 4 - 2][:, c:c + CW]
                    v = V(lambda e, d=d: e.tensor_tensor(d, d, PS[7][:, 0:CW], ALU.add), tk, t_b)
                    if i // 4 == 4:
                        nr = n2row[:, c:c + CW]
                        V(lambda e, d=d, nr=nr: e.scalar_tensor_tensor(out=d, in0=d, scalar=1.0, in1=nr, op0=ALU.add,
                                                                       op1=ALU.mult))
                bankfree[7] = [v]
                accfree[i % 2] = [tk]

        for b in range(8):
            bankfree[b] = []
        fb = (0, 1, 2, 3, 4, 5, 6)
        sc1 = sm[:, 104:112]
        def st_final(t):
            r = rstd_of(t, 1e-5)
            v = V(lambda e: e.scalar_tensor_tensor(out=h3[:, t, :], in0=h3[:, t, :], scalar=sm[:, 8 + t:9 + t],
                                                   in1=row("fw"), op0=ALU.mult, op1=ALU.mult), r)
            sumsq(sm[:, t:t + 1], h3[:, t, :], jk, v)

        stages_H = [st_sum(jk), st_final, st_scale(xs3b, 1e-6), st_turn(xs3b, sc1, mod[:, 0:8], fbig[:, 2688:3712]),
                    st_parts(False)]
        for q in range(4):
            t_a = []
            for i in range(4):
                pv, tp, n = panel("ff1", 4 * q + i)
                for j in range(2):
                    f = 2 * i + j
                    b = bank(fb)
                    tk = MM3(PS[b][:, :], [(tuple(w[:, k, j * 128:(j + 1) * 128] for w in pv), (xh3[:, k, 0:TX], xl3[:, k, 0:TX]))
                                           for k in range(8)], tp, *bankfree[b])
                    u, w2 = sqt[f % 2], sqq[f % 2]
                    a = S(lambda e, u=u, b=b: e.activation(u, PS[b][:, :], ACT.Relu), tk, qv.tok())
                    bankfree[b] = [a]
                    v = V(lambda e, u=u, w2=w2: e.tensor_tensor(w2, u, u, ALU.mult), a)
                    a = S(lambda e, f=f, w2=w2: e.activation(AH[:, f, :], w2, ACT.Copy), v)
                    v = V(lambda e, f=f, w2=w2: e.tensor_tensor(AL[:, f, :], w2, AH[:, f, :].bitcast(F32), ALU.subtract), a)
                    t_a.append([a, v])
                release(n, tk)
                ada_sums()
            for i in range(4):
                pv, tp, n = panel("ff2", 4 * q + i)
                last_ = (q, i) == (3, 3)
                for t in range(NT):
                    b = bank(fb[:5] if last_ else fb)
                    for k in range(8):
                        c = slice(t * 128, (t + 1) * 128)
                        first = [*tp, *bankfree[b]] if k == 0 else []
                        MM(PS[b][:, 0:CW], AH[:, k, c], pv[0][:, k, :], *first, *t_a[k], start=(k == 0), stop=False)
                        MM(PS[b][:, 0:CW], AL[:, k, c], pv[0][:, k, :], start=False, stop=False)
                        tk = MM(PS[b][:, 0:CW], AH[:, k, c], pv[1][:, k, :], start=False, stop=(k == 7))
                    hs = h3[:, t, i * CW:(i + 1) * CW]
                    v = V(lambda e, hs=hs, b=b: e.tensor_tensor(hs, hs, PS[b][:, 0:CW], ALU.add), tk)
                    bankfree[b] = [v]
                    if last_:
                        if t == 0:
                            V(lambda e: e.scalar_tensor_tensor(out=sc1, in0=mod[:, 8:16], scalar=1.0, in1=col("n1g"),
                                                               op0=ALU.add, op1=ALU.mult))
                        step(stages_H, t)
                release(n, tk)
                ada_sums()
        for t in range(NT, NT + len(stages_H) - 1):
            step(stages_H, t)
        fence()

        sff.close()
        sb2 = scope()
        big = big2 = sbs(sb2, "big2", BIG2)
        for b in range(8):
            bankfree[b] = []
        off[0], lim[0] = 0, BIG2
        qk = carve(4096).rearrange("p (a c) -> p a c", a=8)
        mv = carve(4 * 4 * 129).rearrange("p (t h c) -> p t h c", t=4, h=4)
        mo = carve(2048).rearrange("p (t c) -> p t c", t=NT)
        dq = carve(2048).rearrange("p (a c) -> p a c", a=4)
        dk = carve(2048).rearrange("p (a c) -> p a c", a=4)
        dv = carve(2048).rearrange("p (t c) -> p t c", t=NT)
        hoM = carve(2048)
        ub = hoM[:, 0:1030].rearrange("p (a c) -> p a c", a=2)
        cy = hoM[:, 1030:1542]
        hoM = hoM.rearrange("p (t c) -> p t c", t=NT)
        V(lambda e: e.memset(ub[:, :, 0:3], 0.0))
        V(lambda e: e.memset(mv[:, :, :, 128:129], 1.0))
        cyfree = None
        ubfree = [None, None]
        for i in range(4):
            pv, tp, n = panel("w2", i)
            for j in range(2):
                ch = 2 * i + j
                b = bank()
                tk = MM3(PS[b][:, :], [(tuple(w[:, k, j * 128:(j + 1) * 128] for w in pv), (xh3[:, k, 0:TX], xl3[:, k, 0:TX]))
                                       for k in range(8)], tp, *bankfree[b])
                u = ub[:, ch % 2, :]
                cw = [col("convw", 4 * ch + w, 4 * ch + w + 1) for w in range(4)]
                cp = S(lambda e, u=u, b=b: e.activation(u[:, 3:515], PS[b][:, :], ACT.Copy), tk, ubfree[ch % 2] or qv.tok())
                bankfree[b] = [cp]
                V(lambda e, u=u, cw=cw: e.tensor_scalar(cy, u[:, 0:512], cw[0], None, ALU.mult), cp, cyfree or cp)
                for w in (1, 2, 3):
                    v = V(lambda e, u=u, cw=cw, w=w: e.scalar_tensor_tensor(out=cy, in0=u[:, w:w + 512], scalar=cw[w], in1=cy,
                                                                        op0=ALU.mult, op1=ALU.add))
                a = S(lambda e, ch=ch: e.activation(qk[:, ch, :], cy, ACT.Silu, bias=col("convb", ch, ch + 1)), v)
                cyfree = a
                ubfree[ch % 2] = v
            release(n, tk)
        for i, dst in ((4, dq), (6, dk)):
            for g in range(2):
                pv, tp, n = panel("w2", i + g)
                for a in range(2):
                    tk, v = projT(pv, 128 * a, 128, tp, [(0, TX, dst[:, 2 * g + a, :])])
                release(n, tk)
        for g in range(2):
            pv, tp, n = panel("w2", 8 + g)
            for t in range(NT):
                b = bank()
                tk = MM3(PS[b][:, 0:CW], [((xcol(xh_, k, t * 128), xcol(xl_, k, t * 128)), tuple(w[:, k, :] for w in pv))
                                          for k in range(8)], tp, *bankfree[b])
                v = V(lambda e, t=t, b=b, g=g: e.tensor_copy(mv[:, t, 2 * g:2 * g + 2, 0:128],
                                                             PS[b][:, 0:CW].rearrange("p (h c) -> p h c", h=2)), tk)
                bankfree[b] = [v]
            release(n, tk)
        for i, dst, fn in ((10, dv, ACT.Copy), (12, mo, ACT.Sigmoid)):
            for g in range(2):
                pv, tp, n = panel("w2", i + g)
                tk, v = projR(pv, 0, CW, tp, rowsT(dst, CW * g), fn=fn)
                release(n, tk)
        mng = row("mng").rearrange("p (o c) -> p o c", o=1).to_broadcast([128, 4, 512])
        V(lambda e: e.tensor_tensor(mo, mo, mng, ALU.mult), v)
        pv, tp, n = panel("w2", 14, last=True)
        gb = []
        for i in range(2):
            b = bank()
            tk = MM3(PS[b][:, :], [(tuple(w[:, k, i * 128:(i + 1) * 128] for w in pv), (xh3[:, k, 0:TX], xl3[:, k, 0:TX]))
                                   for k in range(8)], tp, *bankfree[b])
            gb.append(b)
        release(n, tk)
        fence()
        splits.close()
        smix = scope()
        over = sbs(smix, "over2", OVER, F32, "right")
        xT = over[:, 0:8 * TA]
        ooff[0] = 8 * TA
        off[0], lim[0] = 8 * TA, OVER
        big = over

        ig, lf, bb, MM_, tmp = (xT[0:4, i * 512:(i + 1) * 512] for i in range(5))
        V(lambda e: e.tensor_scalar(ig, PS[gb[0]][0:4, :], cols[0:4, COFF["gbi"][0]:COFF["gbi"][0] + 1], None, ALU.add), tk)
        v = V(lambda e: e.tensor_scalar(lf, PS[gb[1]][0:4, :], cols[0:4, COFF["gbf"][0]:COFF["gbf"][0] + 1], None, ALU.add))
        S(lambda e: e.activation(tmp, lf, ACT.Abs), v)
        S(lambda e: e.activation(tmp, tmp, ACT.Exp, scale=-1.0))
        a = S(lambda e: e.activation(tmp, tmp, ACT.Ln, bias=1.0))
        V(lambda e: e.scalar_tensor_tensor(out=lf, in0=lf, scalar=0.0, in1=tmp, op0=ALU.min, op1=ALU.subtract), a)
        onesrow = xT[0:4, 5 * 512:6 * 512]
        V(lambda e: e.memset(onesrow, 1.0))
        V(lambda e: e.tensor_tensor_scan(bb, onesrow, lf, 0.0, ALU.mult, ALU.add))
        V(lambda e: e.tensor_tensor(ig, ig, bb, ALU.subtract))
        V(lambda e: e.tensor_tensor_scan(MM_, ig, ig, 0.0, ALU.max, ALU.max))
        V(lambda e: e.tensor_tensor(bb, bb, MM_, ALU.add))
        V(lambda e: e.tensor_scalar(bb, bb, -1.0, None, ALU.mult))
        v = V(lambda e: e.tensor_scalar(MM_, MM_, -1.0, None, ALU.mult))
        ac, emc = sm[:, 128:144], sm[:, 144:160]
        for t in range(NT):
            TR(PS[0][:, 4 * t:4 * t + 4], ig[:, t * 128:(t + 1) * 128], v, mark=False)
            tk = TR(PS[0][:, 16 + 4 * t:20 + 4 * t], bb[:, t * 128:(t + 1) * 128])
        v = V(lambda e: e.tensor_copy(ac, PS[0][:, 0:16]), tk)
        a = S(lambda e: e.activation(emc, PS[0][:, 16:32], ACT.Exp), v)
        oo = [3072]

        def oc(n):
            o = oo[0]
            oo[0] += n
            assert oo[0] <= OVER
            return over[:, o:o + n]

        Wt = oc(2048).rearrange("p (j c) -> p j c", j=4)
        Dts = [oc(512), oc(512)]
        P = [oc(512) for _ in range(4)]
        aTt = [oc(512).rearrange("p (j c) -> p j c", j=4) for _ in range(2)]
        ho4, sqb = oc(2048).rearrange("p (t c) -> p t c", t=NT), oc(2048)
        dn = sm[:, 160:164]
        sel = cols[0:4, COFF["sel"][0]:COFF["sel"][0] + 512]
        dg8 = sm[:, 300:428]
        for b in range(8):
            bankfree[b] = [v, a]
        lt = sm[:, 208:272]
        ls = sm[:, 272:276]
        V(lambda e: e.tensor_tensor_reduce(out=lt, in0=row("lq1"), in1=row("lk1"), scale=1.0, scalar=0.0, op0=ALU.mult,
                                           op1=ALU.add, accum_out=ls[:, 0:1]))
        v = V(lambda e: e.tensor_tensor_reduce(out=lt, in0=row("lq2"), in1=row("lk2"), scale=1.0, scalar=0.0, op0=ALU.mult,
                                               op1=ALU.add, accum_out=ls[:, 1:2]))
        a = S(lambda e: e.activation(ls[:, 0:2], ls[:, 0:2], ACT.Exp), v)
        V(lambda e: e.tensor_tensor(ls[:, 2:3], ls[:, 1:2], ls[:, 0:1], ALU.subtract), a)
        V(lambda e: e.tensor_scalar(ls[:, 2:3], ls[:, 2:3], -0.2, None, ALU.add))
        V(lambda e: e.tensor_scalar(dg8, row("dng"), 0.8, None, ALU.mult))

        def head_norm(o3, dst, gate, eps, s4, r4):
            a = S(lambda e: e.activation(sqb, o3.rearrange("p t c -> p (t c)"), ACT.Square), qv.tok())
            yield
            V(lambda e: e.tensor_reduce(s4, sqb.rearrange("p (n c) -> p n c", c=128), AX, ALU.add), a)
            for i in range(4):
                r = rstd(r4[:, 4 * i:4 * i + 4], s4[:, 4 * i:4 * i + 4], 128.0, eps)
            yield
            ov = o3.rearrange("p t (h c) -> p (t h) c", h=4)
            V(lambda e: e.tensor_tensor(ov, ov, r4.rearrange("p (n o) -> p n o", o=1).to_broadcast([128, 16, 128]), ALU.mult), r)
            V(lambda e: e.tensor_tensor(dst.rearrange("p t (h c) -> p (t h) c", h=4), ov, gate, ALU.mult))

        def mlstm():
            wfree = []
            for h in range(4):
                tmb = MM(PS[0][:, :], sel[:, h * 128:(h + 1) * 128], MM_, *bankfree[0])
                for j in range(NT):
                    w = TX - j * 128
                    Dt = Dts[j % 2]
                    tk = MM(PS[1][:, 0:w], qk[:, 4 + h, j * 128:(j + 1) * 128], qk[:, h, j * 128:TX], *bankfree[1])
                    v = V(lambda e, j=j, w=w, h=h, Dt=Dt: e.tensor_scalar(
                        Dt[:, 0:w], PS[0][:, j * 128:TX], ac[:, 4 * j + h:4 * j + h + 1], 0.0, ALU.add, ALU.min), tmb)
                    bankfree[0] = [v]
                    a = S(lambda e, w=w, Dt=Dt: e.activation(Dt[:, 0:w], Dt[:, 0:w], ACT.Exp), v)
                    yield
                    V(lambda e, Dt=Dt: e.tensor_tensor(Dt[:, 0:128], Dt[:, 0:128], col("caus"), ALU.mult), a)
                    v = V(lambda e, j=j, w=w, Dt=Dt: e.scalar_tensor_tensor(
                        out=Wt[:, j, j * 128:TX], in0=PS[1][:, 0:w], scalar=128.0 ** -0.5, in1=Dt[:, 0:w], op0=ALU.mult,
                        op1=ALU.mult), tk, *wfree)
                    bankfree[1] = [v]
                yield
                for pr in range(2):
                    b = (2, 7)[pr]
                    for t in (2 * pr, 2 * pr + 1):
                        c = 256 * (t % 2)
                        for j in range(t + 1):
                            tk = MM(PS[b][:, c:c + 129], Wt[:, j, t * 128:(t + 1) * 128], mv[:, j, h, :], v, *bankfree[b],
                                    start=(j == 0), stop=(j == t))
                    p2 = PS[b][:, :].rearrange("p (t c) -> p t c", t=2)
                    d2 = dn[:, 2 * pr:2 * pr + 2]
                    e2_ = emc.rearrange("p (t h) -> p t h", h=4)[:, 2 * pr:2 * pr + 2, h]
                    V(lambda e, p2=p2, d2=d2, e2_=e2_: e.tensor_tensor(d2, p2[:, :, 128], e2_, ALU.max), tk)
                    V(lambda e, p2=p2, d2=d2: e.scalar_tensor_tensor(out=d2, in0=p2[:, :, 128], scalar=-1.0, in1=d2,
                                                                     op0=ALU.mult, op1=ALU.max))
                    V(lambda e, d2=d2: e.reciprocal(d2, d2))
                    vv = V(lambda e, p2=p2, d2=d2, pr=pr, h=h: e.tensor_tensor(
                        hoM[:, 2 * pr:2 * pr + 2, h * 128:(h + 1) * 128], p2[:, :, 0:128],
                        d2.rearrange("p (t o) -> p t o", o=1).to_broadcast([128, 2, 128]), ALU.mult))
                    bankfree[b] = [vv]
                    yield
                wfree = [tk]
            yield from head_norm(hoM, hoM, mo.rearrange("p t (h c) -> p (t h) c", h=4), 1e-6, sm[:, 176:192], sm[:, 192:208])

        def diff(i2):
            so = sm[:, 276 + 12 * i2:288 + 12 * i2]
            P0, P1 = P[2 * i2], P[2 * i2 + 1]
            at = aTt[i2]
            b0, b1 = 3 + 2 * i2, 4 + 2 * i2
            pf, atf = [], []
            for t in range(NT):
                n = (t + 1) * 128
                for h in (i2, i2 + 2):
                    both = ((0, b0, P0), (1, b1, P1))
                    for p, b, Pp in both:
                        tk = MM(PS[b][:, 0:n], dq[64 * p:64 * p + 64, h, t * 128:(t + 1) * 128],
                                dk[64 * p:64 * p + 64, h, 0:n], *bankfree[b])
                        (V2 if p else V)(lambda e, b=b, n=n: e.tensor_tensor(PS[b][:, n - 128:n], PS[b][:, n - 128:n],
                                                                             col("negm"), ALU.add), tk)
                    for p, b, Pp in both:
                        V2(lambda e, b=b, n=n, p=p: e.tensor_reduce(so[:, p:p + 1], PS[b][:, 0:n], AX, ALU.max))
                    v = V(lambda e: e.tensor_scalar(so[:, 2:4], so[:, 0:2], -0.125, None, ALU.mult))
                    for p, b, Pp in both:
                        a = S(lambda e, b=b, n=n, p=p, Pp=Pp: e.activation(
                            Pp[:, 0:n], PS[b][:, 0:n], ACT.Exp, bias=so[:, 2 + p:3 + p], scale=0.125,
                            accum_out=so[:, 4 + p:5 + p]), v, *pf)
                        bankfree[b] = [a]
                    yield
                    V(lambda e: e.reciprocal(so[:, 6:8], so[:, 4:6]), a)
                    V(lambda e: e.tensor_tensor(so[:, 7:8], so[:, 7:8], ls[:, 2:3], ALU.mult))
                    V(lambda e, n=n: e.tensor_scalar(P1[:, 0:n], P1[:, 0:n], so[:, 7:8], None, ALU.mult))
                    v = V(lambda e, n=n: e.scalar_tensor_tensor(
                        out=P0[:, 0:n], in0=P0[:, 0:n], scalar=so[:, 6:7], in1=P1[:, 0:n], op0=ALU.mult, op1=ALU.add))
                    yield
                    for j in range(t + 1):
                        tk = TR(PS[b0][:, j * 128:(j + 1) * 128], P0[:, j * 128:(j + 1) * 128], v, *bankfree[b0], mark=(j == t))
                    pf = [tk]
                    cp = S(lambda e, n=n: e.activation(at.rearrange("p j c -> p (j c)")[:, 0:n], PS[b0][:, 0:n], ACT.Copy),
                           tk, *atf)
                    bankfree[b0] = [cp]
                    yield
                    for j in range(t + 1):
                        tk = MM(PS[b1][:, 0:128], at[:, j, :], dv[:, j, h * 128:(h + 1) * 128], cp, *bankfree[b1],
                                start=(j == 0), stop=(j == t))
                    atf = [tk]
                    v = V(lambda e, t=t, h=h: e.tensor_copy(ho4[:, t, h * 128:(h + 1) * 128], PS[b1][:, 0:128]), tk)
                    bankfree[b1] = [v]

        beside(mlstm(), diff(0), diff(1))
        fence()
        hoD = qk[:, 0:4, :]
        beside(head_norm(ho4, hoD, dg8.rearrange("p (o c) -> p o c", o=1).to_broadcast([128, 16, 128]), 1e-6,
                         sm[:, 428:444], sm[:, 444:460]))
        fence()

        smix.close()
        splits, xh_, xl_ = open_split("c")
        xh3 = xh_[:, 0:8 * TA].rearrange("p (k c) -> p k c", k=8)
        xl3 = xl_[:, 0:8 * TA].rearrange("p (k c) -> p k c", k=8)
        prep()
        for k in range(8):
            o3 = hoM if k < 4 else hoD
            b, h4 = k % 4, k % 4
            for t in range(NT):
                tk = TR(PS[b][:, t * 128:(t + 1) * 128], o3[:, t, h4 * 128:(h4 + 1) * 128], *(bankfree[b] if k > 3 else []),
                        mark=(t == NT - 1))
            h, l = xh3[:, k, 0:TX], xl3[:, k, 0:TX]
            a = S(lambda e, h=h, b=b: e.activation(h, PS[b][:, :], ACT.Copy), tk)
            v = V(lambda e, h=h, l=l, b=b: e.tensor_tensor(l, PS[b][:, :], h.bitcast(F32), ALU.subtract), a)
            bankfree[b] = [v]
        fence()
        for b in range(8):
            bankfree[b] = []
        h2 = big2[:, 0:4096].rearrange("p (t d) -> p t d", t=NT)
        qT = big2[:, 4096:12288].rearrange("p (a c) -> p a c", a=16)
        gtmp, j2 = big2[:, 16200:16456], big2[:, 14336:15360]

        def st_rows(t):
            r = rstd_of(t, 1e-6)
            V(lambda e: e.scalar_tensor_tensor(out=h2[:, t, :], in0=h3[:, t, :], scalar=sm[:, 8 + t:9 + t], in1=A2b,
                                               op0=ALU.mult, op1=ALU.mult), r)
            v_rows[t] = V(lambda e: e.tensor_tensor(h2[:, t, :], h2[:, t, :], B2b[:, :], ALU.add))

        out_proj("wo2", g1b, gtmp, [st_sum(j2), st_rows, st_turn(h2, None, None, None), st_parts(True)])
        fence()
        for b in range(8):
            bankfree[b] = []
        big = big2
        off[0], lim[0] = 12288, 16200
        sk = carve(2048).rearrange("p (a c) -> p a c", a=16)
        t_sk = LOAD(qd, sk, skT, s_sk)
        svv = carve(32).rearrange("p (a k) -> p a k", a=2)
        siv = carve(32).bitcast(U32).rearrange("p (a k) -> p a k", a=2)
        sif = carve(32).rearrange("p (a k) -> p a k", a=2)
        fv = carve(128).rearrange("p (h k) -> p h k", h=8)
        fpo = carve(128).bitcast(U32).rearrange("p (h k) -> p h k", h=8)
        fhi = carve(16).bitcast(U32)
        fhf = carve(16)
        es = [carve(16), carve(16)]
        gw = carve(256).rearrange("p (i k) -> p i k", i=2)
        eid = carve(256).bitcast(U32).rearrange("p (i k) -> p i k", i=2)
        act = carve(256).rearrange("p (i k) -> p i k", i=2)
        w_ = carve(256).rearrange("p (i k) -> p i k", i=2)
        eidf = carve(128)
        eidT = carve(128).bitcast(U32)
        sS = [A2b[:, 0:256], A2b[:, 256:512]]
        cand, oh = A2b[:, 512:768], A2b[:, 768:1024]
        iota = col("iota")
        sSfree = [[], []]

        def top16(vals, src, idx, *after):
            V(lambda e: e.max(vals[:, 0:8], src), *after)
            V(lambda e: e.max_index(idx[:, 0:8], vals[:, 0:8], src))
            V(lambda e: e.match_replace(src, vals[:, 0:8], src, -3.0e38))
            V(lambda e: e.max(vals[:, 8:16], src))
            return V(lambda e: e.max_index(idx[:, 8:16], vals[:, 8:16], src))

        def topk_head(t, h, *after):
            b = 4 + h % 2
            ss_ = sS[h % 2]
            for p in range(2):
                tk = MM(PS[b][:, p * 128:(p + 1) * 128], qT[:, 2 * h + p, t * 128:(t + 1) * 128], sk[:, 2 * h + p, :],
                        t_sk, *after, *bankfree[b])
            v = S(lambda e: e.activation(ss_, PS[b][:, 0:256], ACT.Copy), tk, *sSfree[h % 2])
            bankfree[b] = [v]
            for p in range(2):
                sSfree[h % 2] = [top16(svv[:, p, :], ss_[:, p * 128:(p + 1) * 128], siv[:, p, :], v)]
            V(lambda e: e.tensor_copy(sif, siv))
            V(lambda e: e.tensor_tensor(
                cand.rearrange("p (i j) -> p i j", i=16),
                svv[:, 0, :].rearrange("p (k o) -> p k o", o=1).to_broadcast([128, 16, 16]),
                svv[:, 1, :].rearrange("p (o k) -> p o k", o=1).to_broadcast([128, 16, 16]), ALU.add))
            top16(fv[:, h, :], cand, fpo[:, h, :])
            o3_ = oh.rearrange("p (n i) -> p n i", i=16)
            for part in range(2):
                V(lambda e, part=part: e.tensor_scalar(fhi, fpo[:, h, :], 4 if part == 0 else 15, None,
                                                       ALU.logical_shift_right if part == 0 else ALU.bitwise_and))
                V(lambda e: e.tensor_copy(fhf, fhi))
                V(lambda e: e.tensor_tensor(
                    o3_, fhf.rearrange("p (n o) -> p n o", o=1).to_broadcast([128, 16, 16]),
                    iota.rearrange("p (o i) -> p o i", o=1).to_broadcast([128, 16, 16]), ALU.is_equal))
                V(lambda e, part=part: e.tensor_tensor(
                    o3_, o3_, sif[:, part, :].rearrange("p (o k) -> p o k", o=1).to_broadcast([128, 16, 16]), ALU.mult))
                V(lambda e, part=part: e.tensor_reduce(es[part], o3_, AX, ALU.add))
            V(lambda e: e.scalar_tensor_tensor(out=eidf[:, 16 * h:16 * h + 16], in0=es[0], scalar=128.0, in1=es[1],
                                               op0=ALU.mult, op1=ALU.add))
            return V(lambda e: e.tensor_copy(eid[:, t % 2, 16 * h:16 * h + 16], eidf[:, 16 * h:16 * h + 16]), ufree[t % 2])

        def topk_end(t):
            e2 = t % 2
            V(lambda e: e.tensor_copy(sm[:, 128:136], fv[:, :, 0]))
            gv_ = gw[:, e2, :].rearrange("p (h k) -> p h k", h=8)
            v = V(lambda e: e.tensor_tensor(
                gv_, fv, sm[:, 128:136].rearrange("p (h o) -> p h o", o=1).to_broadcast([128, 8, 16]), ALU.subtract))
            a = S(lambda e: e.activation(gw[:, e2, :], gw[:, e2, :], ACT.Exp), v)
            V(lambda e: e.tensor_reduce(sm[:, 136:144], gv_, AX, ALU.add), a)
            V(lambda e: e.reciprocal(sm[:, 136:144], sm[:, 136:144]))
            V(lambda e: e.tensor_tensor(
                gv_, gv_, sm[:, 136:144].rearrange("p (h o) -> p h o", o=1).to_broadcast([128, 8, 16]), ALU.mult))

        state["banks"] = (0, 1, 2, 3)
        prev = None
        ve = [None] * 8
        ufree = [t_r, t_r]
        for i in range(8):
            pv, tp, n = panel("wq", i)
            for a in range(2):
                tk, v = projT(pv, 128 * a, 128, tp, [(0, TX, qT[:, 2 * i + a, :])])
            release(n, tk)
            if i:
                ve[i - 1] = topk_head(0, i - 1, prev)
            prev = v
        tf = fence()
        ve[7] = topk_head(0, 7)
        topk_end(0)
        splits.close()
        big = sbs(ctx, "big4", BIG4)
        off[0], lim[0] = 0, BIG4
        w32 = carve(4128)
        jk2 = carve(1024)
        yT = jk2
        gs_ = carve((NG - 4) * 1024)
        gs = [raw[:, i * 1024:(i + 1) * 1024] if i < 4 else gs_[:, (i - 4) * 1024:(i - 3) * 1024] for i in range(NG)]
        s_g = [sem(f"s_g{i}") for i in range(NG)]
        gi = {"n": 0}
        gfree = [list(tf) for _ in range(NG)]

        def gather(tab, idx, tok):
            i = gi["n"] % NG
            gi["n"] += 1
            qg.add(lambda e, i=i, idx=idx: e.indirect_dma_start(
                gs[i], None, tab, bass.IndirectOffsetOnAxis(ap=idx, axis=0)), [tok, *gfree[i]], sem=s_g[i], inc=16)
            dma_n[s_g[i].name] = dma_n.get(s_g[i].name, 0) + 16
            return i, (s_g[i], dma_n[s_g[i].name])

        def turn_ids(ve, *after):
            tk = TR(PS[6][:, 0:128], eidf, ve, *bankfree[6])
            v = V(lambda e: e.tensor_copy(eidT, PS[6][:, 0:128]), tk, *after)
            bankfree[6] = [v]
            return v

        V(lambda e: e.memset(w32[:, :], 0.0))
        vt = turn_ids(ve[7])
        yfree = []

        def finish(t, tk):
            for hf in range(2):
                v = V(lambda e, hf=hf: e.tensor_tensor(yT[:, hf * 512:(hf + 1) * 512], PS[hf][:, :],
                                                       g2b[:, hf * 512:(hf + 1) * 512], ALU.mult), tk)
            yfree[:] = [v]
            V(lambda e: e.tensor_tensor(h3[:, t, :], h3[:, t, :], yT, ALU.add))
            a = sumsq(sm[:, 0:1], h3[:, t, :], g1b, qv.tok())
            return V(lambda e: e.tensor_scalar(sm[:, 0:1], sm[:, 0:1], 1.0 / 1024.0, 1e-6, ALU.mult, ALU.add), a)

        def finish_out(t, v):
            r = G(lambda e: e.tensor_tensor(sm[:, 8:9], sm[:, 0:1], mh[:, 0:1], ALU.pow), v)
            v = V(lambda e: e.scalar_tensor_tensor(out=h3[:, t, :], in0=h3[:, t, :], scalar=sm[:, 8:9], in1=row("fg"),
                                                   op0=ALU.mult, op1=ALU.mult), r)
            return LOAD(qd, out[t * 128:(t + 1) * 128, :], h3[:, t, :], s_out, v)

        for t in range(NT):
            e2 = t % 2
            for k in range(128):
                if t and k == 0:
                    v_ms = finish(t - 1, t_y)
                if t and k == 9:
                    t_o = finish_out(t - 1, v_ms)
                i, tok = gather(utab, eid[:, e2, k:k + 1], ve[k // 16])
                v = V(lambda e, i=i, k=k, t=t, e2=e2: e.tensor_tensor_reduce(
                    out=jk2, in0=gs[i], in1=h2[:, t, :], scale=1.0, scalar=0.0, op0=ALU.mult, op1=ALU.add,
                    accum_out=act[:, e2, k:k + 1]), tok)
                gfree[i] = [v]
            ufree[e2] = v
            a = S(lambda e, e2=e2: e.activation(w_[:, e2, :], act[:, e2, :], ACT.Gelu), v)
            v = V(lambda e, e2=e2: e.tensor_tensor(w_[:, e2, :], w_[:, e2, :], gw[:, e2, :], ALU.mult), a)
            tk = TR(PS[7][:, 0:128], w_[:, e2, :], v, *bankfree[7])
            vw = V(lambda e: e.tensor_copy(w32[:, 32:].rearrange("p (t c) -> p t c", c=32)[:, :, 0], PS[7][:, 0:128]), tk)
            bankfree[7] = [vw]
            for m in range(32):
                gg = [gather(vtab, eidT[:, 32 * j + m:32 * j + m + 1], vt) for j in range(4)]
                for hf in range(2):
                    for j in range(4):
                        i, tok = gg[j]
                        c0 = 32 + 32 * (32 * j + m) - m
                        tk = MM(PS[hf][32 * j:32 * j + 32, :], w32[:, c0:c0 + 32], gs[i][:, hf * 512:(hf + 1) * 512],
                                vw, tok, *yfree, start=(m == 0), stop=(m == 31), mark=True)
                        gfree[i] = [tk]
                if t + 1 < NT and m % 3 == 0 and m < 24:
                    ve[m // 3] = topk_head(t + 1, m // 3)
                    if m == 21:
                        topk_end(t + 1)
            if t + 1 < NT:
                vt = turn_ids(ve[7])
            t_y = tk
        t_o = finish_out(NT - 1, finish(NT - 1, t_y))
        qd.items.append((qd.need([t_o]), None, None, 0))

        block = ctx.enter_context(nc.Block())

        @block.sync
        def _(e):
            qd.run(e)

        @block.scalar
        def _(e):
            qs.run(e)

        @block.gpsimd
        def _(e):
            qg.run(e)

        @block.vector
        def _(e):
            qv.run(e)

        @block.tensor
        def _(e):
            qp.run(e)


def shape_constants():
    c = {}
    c["ident"] = np.eye(128)
    inv = np.float32(1.0) / np.float32(500000.0) ** (np.arange(0, 16, 2, dtype=np.float32) / np.float32(16))
    pos = np.concatenate([np.arange(NM, NM + TX), np.arange(NM)]).astype(np.float32)
    ang = (pos[None, :] * inv.astype(np.float32)[:, None]).astype(np.float32)
    cos = np.ones((64, TA), np.float32)
    sin = np.zeros((64, TA), np.float32)
    cos[0:8] = cos[8:16] = np.cos(ang)
    sin[0:8] = sin[8:16] = np.sin(ang)
    c["cos"], c["sin"] = np.tile(cos, (2, 1)), np.tile(sin, (2, 1))
    rot = np.zeros((128, 128), np.float32)
    for b in (0, 64):
        for m in range(8):
            rot[b + m + 8, b + m] = -1.0
            rot[b + m, b + m + 8] = 1.0
    c["rot"] = rot
    j, i = np.arange(128)[:, None], np.arange(128)[None, :]
    ms = [(j == i)]
    for s in LEVELS:
        ms.append((j // (2 * s) == i // (2 * s)) & (j % (2 * s) < s) & (i % (2 * s) >= s))
    c["masks"] = np.concatenate(ms, axis=1).astype(np.float32)
    r, k = np.arange(128)[:, None], np.arange(256)[None, :]
    dist = 128 + r - k
    w = np.zeros((128, 272), np.float32)
    w[:, 0:256] = np.where((dist >= 0) & (dist < 128), 0.0, BIGNEG)
    c["wmask"] = w
    c["negm"] = np.where(i <= j, 0.0, BIGNEG)
    c["caus"] = (j <= i).astype(np.float32)
    rs = np.ones((128, TA), np.float32)
    rs[:, [0, 128, 256, 384, 512]] = 0.0
    c["reset"] = rs
    c["iota"] = np.tile(np.arange(16, dtype=np.float32), (128, 1))
    sel = np.zeros((128, 4, 128), np.float32)
    for h in range(4):
        sel[h, h, :] = 1.0
    c["sel"] = sel.reshape(128, 512)
    c["mhalf"] = np.full((128, 4), -0.5)
    return c


def colv(v):
    return np.asarray(v).reshape(-1, 128).T


def panelize(w):
    k, n = w.shape
    return np.ascontiguousarray(w.reshape(8, 128, n).transpose(1, 0, 2).reshape(128, 8 * n))


def kernel(x, meta_tokens, norm_mix_w, w_in, w_gate_up, b_gate, gla_norm_w, sinks, w_out, norm_ff_w, w_ff1, w_ff2,
           final_norm_w, c_2, ada_w_2, ada_b_2, norm1_g_2, w_in_2, conv_w_2, conv_b_2, mlstm_gate_b_2, mlstm_norm_g_2,
           lambda_q1_2, lambda_k1_2, lambda_q2_2, lambda_k2_2, diff_norm_g_2, w_out_2, norm2_g_2, peer_w_query_2,
           peer_sub_keys_2, peer_u_2, peer_v_2, final_g_2):
    import concourse.bacc as bacc
    from concourse.bass_utils import run_bass_kernel_spmd

    A = np.asarray
    f = np.float32
    c = shape_constants()
    c.update(mixw=colv(A(norm_mix_w)[0]), ffw=colv(A(norm_ff_w)[0]), n1g=colv(A(norm1_g_2)[0]),
             bgate=colv(A(b_gate)[0]), adab=colv(A(ada_b_2)[0]), ccol=colv(A(c_2)[0]))
    cw = A(conv_w_2)[0]
    c["convw"] = cw.reshape(4, 8, 128).transpose(2, 1, 0).reshape(128, 32)
    c["convb"] = colv(A(conv_b_2)[0])
    w2 = A(w_in_2)[0]
    pack = np.zeros((128, NCOL), f)
    for name, w in COLS:
        o = COFF[name][0]
        if name in c:
            pack[:, o:o + w] = c[name]
    gbv = A(mlstm_gate_b_2)[0]
    pack[0:4, COFF["gbi"][0]] = gbv[0:4]
    pack[0:4, COFF["gbf"][0]] = gbv[4:8]
    pack[0:16, COFF["wgu"][0]:COFF["wgu"][0] + 256] = A(w_gate_up)[0]
    rows = np.concatenate([A(final_norm_w), A(final_g_2), A(gla_norm_w)[0], A(mlstm_norm_g_2)[0], A(diff_norm_g_2)[0],
                           A(sinks)[0], A(lambda_q1_2)[0], A(lambda_k1_2)[0], A(lambda_q2_2)[0],
                           A(lambda_k2_2)[0]]).reshape(1, NROW)
    w1 = A(w_in)[0]
    gq, gk, gv_, gr_, glr, sq, sk_, sv_ = np.split(w1, np.cumsum([256, 256, 512, 512, 16, 512, 128]), axis=1)
    sqh = sq.reshape(1024, 8, 64)
    sqp = np.concatenate([sqh[:, [j, j + 4]].reshape(1024, 128) for j in range(4)], axis=1)
    wo = A(w_out)[0]
    woh = wo[512:].reshape(8, 64, 1024)
    wop = np.concatenate([wo[0:512]] + [woh[[j, j + 4]].reshape(128, 1024) for j in range(4)], axis=0)
    ff1, ff2, ada, wo2, wq = A(w_ff1)[0], A(w_ff2)[0], A(ada_w_2)[0], A(w_out_2)[0], A(peer_w_query_2)[0]
    cut = lambda w: [w[:, i:i + CW] for i in range(0, w.shape[1], CW)]
    pad = lambda w: np.concatenate([w, np.zeros((1024, 128 - w.shape[1]), f)], axis=1)
    P = {
        "w1": [pad(glr)] + cut(gq) + cut(gk) + cut(sqp) + [np.concatenate([sk_, sv_], 1)] + cut(gv_) + cut(gr_),
        "wo1": cut(wop),
        "ff1": cut(ff1),
        "ff2": [ff2[q * 1024:(q + 1) * 1024, h * CW:(h + 1) * CW] for q in range(4) for h in range(4)],
        "ada": cut(ada),
        "w2": cut(w2[:, 0:1024]) + cut(w2[:, 2056:3080]) + cut(w2[:, 1024:1536]) + cut(w2[:, 3080:3592])
        + cut(w2[:, 1536:2048]) + [np.concatenate([pad(w2[:, 2048:2052]), pad(w2[:, 2052:2056])], 1)],
        "wo2": cut(wo2),
        "wq": cut(wq),
    }
    skt = A(peer_sub_keys_2)[0].reshape(16, 128, 128).transpose(2, 0, 1).reshape(128, 2048)
    ab = A(ada_b_2)[0]
    brows = np.concatenate([ab[2048:6144], A(norm2_g_2)[0]]).reshape(1, 5120)
    arrays = {"brows": brows, "packs": pack, "rows": rows, "x": A(x)[0], "meta": A(meta_tokens), "skt": skt, "utab": A(peer_u_2)[0],
              "vtab": A(peer_v_2)[0]}
    for name, ws in P.items():
        for i, w in enumerate(ws):
            arrays[f"{name}_{i}"] = panelize(w)
    arrays = {k: np.ascontiguousarray(v) for k, v in arrays.items()}

    nc = bacc.Bacc("TRN2", target_bir_lowering=False, num_devices=1)
    ap = {k: nc.dram_tensor(k, v.shape, F32, kind="ExternalInput").ap() for k, v in arrays.items()}
    o = nc.dram_tensor("out0", (TX, 1024), F32, kind="ExternalOutput").ap()
    W = {name: [ap[f"{name}_{i}"] for i in range(len(ws))] for name, ws in P.items()}
    build(nc, ap["packs"], ap["rows"], ap["brows"], ap["x"], ap["meta"], W, ap["skt"], ap["utab"], ap["vtab"], o)
    r = run_bass_kernel_spmd(nc, [arrays], core_ids=[0])
    return r.results[0]["out0"].reshape(1, TX, 1024)
```
